# Optimizing a Trainium2 kernel written in Bass

```python
import math
import jax, jax.numpy as jnp
from jax import lax
import numpy as np

D_MODEL = 1024
BATCH = 1
SEQ = 512
DEPTH = 2

A_HEAD_DIM = 64
A_Q_HEADS = 8
A_KV_HEADS = 2
WINDOW = 128
ROPE_THETA = 10000.0
B_HEADS = 4
B_HEAD_DIM = 128
B_CONV = 4
B_CHUNK = 64
LRU_WIDTH = D_MODEL
LRU_BLOCKS = 4
LRU_CONV = 4
LRU_C = 8.0
D_FF = 4 * D_MODEL
A_Q_W = A_Q_HEADS * A_HEAD_DIM
A_KV_W = A_KV_HEADS * A_HEAD_DIM
B_W = B_HEADS * B_HEAD_DIM
HYB_SPLITS = (A_Q_W, A_KV_W, A_KV_W, 3 * B_W, B_W, B_HEADS, B_HEADS)
HYB_PROJ = A_Q_W + 2 * A_KV_W + 4 * B_W + 2 * B_HEADS
MIX_W = A_Q_W + B_W
N_HYB = (DEPTH + 1) // 2
N_REC = DEPTH // 2
DN_ALPHA = (2 * DEPTH) ** 0.25
DN_BETA = (8 * DEPTH) ** -0.25
LN_EPS = 1e-5
NORM_EPS = 1e-6


def split_cols(t, sizes):
    out, start = [], 0
    for s in sizes:
        out.append(t[..., start:start + s])
        start += s
    return out

def layer_norm(x, g, b):
    xf = x.astype(jnp.float32)
    mu = jnp.mean(xf, axis=-1, keepdims=True)
    var = jnp.mean(jnp.square(xf - mu), axis=-1, keepdims=True)
    y = (xf - mu) * lax.rsqrt(var + LN_EPS) * g.astype(jnp.float32) + b.astype(jnp.float32)
    return y.astype(x.dtype)

def l2_normalize(x):
    xf = x.astype(jnp.float32)
    return xf * lax.rsqrt(jnp.sum(xf * xf, axis=-1, keepdims=True) + NORM_EPS)

def apply_rope(x):
    T, dh = x.shape[1], x.shape[-1]
    half = dh // 2
    inv_freq = ROPE_THETA ** (-jnp.arange(half, dtype=jnp.float32) / half)
    ang = jnp.arange(T, dtype=jnp.float32)[:, None] * inv_freq[None, :]
    cos = jnp.cos(ang)[None, :, None, :]
    sin = jnp.sin(ang)[None, :, None, :]
    xf = x.astype(jnp.float32)
    x1, x2 = xf[..., :half], xf[..., half:]
    return jnp.concatenate([x1 * cos - x2 * sin, x2 * cos + x1 * sin], axis=-1).astype(x.dtype)

def causal_dwconv(x, w, b=None):
    K = w.shape[0]
    T = x.shape[1]
    xp = jnp.pad(x, ((0, 0), (K - 1, 0), (0, 0)))
    y = sum(xp[:, j:j + T] * w[j] for j in range(K))
    if b is not None:
        y = y + b
    return y

def sliding_window_attention(q, k, v, sinks):
    f32 = jnp.float32
    bsz, T, HQ, DH = q.shape
    HKV = k.shape[2]
    G = HQ // HKV
    W = WINDOW
    NB = T // W
    qb = q.reshape(bsz, NB, W, HKV, G, DH)

    def band(t):
        prev = jnp.pad(t, ((0, 0), (W, 0), (0, 0), (0, 0)))[:, :T]
        return jnp.concatenate([prev.reshape(bsz, NB, W, HKV, DH),
                                t.reshape(bsz, NB, W, HKV, DH)], axis=2)

    kb, vb = band(k), band(v)
    s = jnp.einsum('bnqhgd,bnkhd->bnhgqk', qb, kb).astype(f32) * (DH ** -0.5)
    dist = (jnp.arange(W)[:, None] + W) - jnp.arange(2 * W)[None, :]
    in_window = (dist >= 0) & (dist < W)
    key_pos = (jnp.arange(NB)[:, None] - 1) * W + jnp.arange(2 * W)[None, :]
    mask = in_window[None] & (key_pos >= 0)[:, None, :]
    s = jnp.where(mask[None, :, None, None], s, -jnp.inf)
    sink = jnp.broadcast_to(sinks.astype(f32).reshape(1, 1, HKV, G, 1, 1), s.shape[:-1] + (1,))
    p = jax.nn.softmax(jnp.concatenate([s, sink], axis=-1), axis=-1)[..., :-1]
    o = jnp.einsum('bnhgqk,bnkhd->bnqhgd', p.astype(v.dtype), vb)
    return o.reshape(bsz, T, HQ * DH)

def gated_delta_rule(q, k, v, g, beta):
    f32 = jnp.float32
    bsz, T, H, DK = q.shape
    DV = v.shape[-1]
    C = B_CHUNK
    N = T // C

    def chunk(t):
        t = t.astype(f32).reshape((bsz, N, C, H) + t.shape[3:])
        return jnp.moveaxis(t, 3, 1)

    q = chunk(q) * (DK ** -0.5)
    k = chunk(k)
    v = chunk(v)
    g = jnp.cumsum(chunk(g), axis=-1)
    beta = chunk(beta)
    k_beta = k * beta[..., None]
    v_beta = v * beta[..., None]
    idx = jnp.arange(C)
    incl = idx[:, None] >= idx[None, :]
    strict = idx[:, None] > idx[None, :]
    diff = g[..., :, None] - g[..., None, :]
    decay_incl = jnp.exp(jnp.where(incl, diff, -jnp.inf))
    decay_strict = jnp.where(strict, decay_incl, 0.0)
    a_mat = jnp.einsum('bhnik,bhnjk->bhnij', k_beta, k) * decay_strict
    eye = jnp.eye(C, dtype=f32)
    t_mat = lax.linalg.triangular_solve(a_mat + eye, jnp.broadcast_to(eye, a_mat.shape),
                                        left_side=True, lower=True, unit_diagonal=True)
    u = jnp.einsum('bhnij,bhnjv->bhniv', t_mat, v_beta)
    w = jnp.einsum('bhnij,bhnjk->bhnik', t_mat, k_beta * jnp.exp(g)[..., None])
    qk = jnp.einsum('bhnik,bhnjk->bhnij', q, k) * decay_incl
    q_g = q * jnp.exp(g)[..., None]
    g_last = g[..., -1]
    k_tail = k * jnp.exp(g_last[..., None] - g)[..., None]
    xs = tuple(jnp.moveaxis(t, 2, 0) for t in (q_g, k_tail, u, w, qk, g_last))

    def step(S, inp):
        q_c, kt_c, u_c, w_c, qk_c, gl_c = inp
        v_new = u_c - jnp.einsum('bhck,bhkv->bhcv', w_c, S)
        o_c = jnp.einsum('bhck,bhkv->bhcv', q_c, S) + jnp.einsum('bhij,bhjv->bhiv', qk_c, v_new)
        S = S * jnp.exp(gl_c)[..., None, None] + jnp.einsum('bhck,bhcv->bhkv', kt_c, v_new)
        return S, o_c

    S0 = jnp.zeros((bsz, H, DK, DV), f32)
    _, o = lax.scan(step, S0, xs)
    return jnp.transpose(o, (1, 0, 3, 2, 4)).reshape(bsz, T, H, DV)

def hybrid_mixer(x, w_in, sinks, conv_w, a_log, dt_bias, norm_w, w_out):
    f32 = jnp.float32
    bsz, T, _ = x.shape
    proj = x @ w_in
    qa, ka, va, qkv_b, z, beta_logit, a_logit = split_cols(proj, HYB_SPLITS)
    qa = apply_rope(qa.reshape(bsz, T, A_Q_HEADS, A_HEAD_DIM))
    ka = apply_rope(ka.reshape(bsz, T, A_KV_HEADS, A_HEAD_DIM))
    va = va.reshape(bsz, T, A_KV_HEADS, A_HEAD_DIM)
    o_a = sliding_window_attention(qa, ka, va, sinks)
    qkv_b = jax.nn.silu(causal_dwconv(qkv_b, conv_w))
    qb, kb, vb = split_cols(qkv_b, (B_W, B_W, B_W))
    qb = l2_normalize(qb.reshape(bsz, T, B_HEADS, B_HEAD_DIM))
    kb = l2_normalize(kb.reshape(bsz, T, B_HEADS, B_HEAD_DIM))
    vb = vb.reshape(bsz, T, B_HEADS, B_HEAD_DIM)
    beta = jax.nn.sigmoid(beta_logit.astype(f32))
    g = -jnp.exp(a_log.astype(f32)) * jax.nn.softplus(a_logit.astype(f32) + dt_bias.astype(f32))
    o_b = gated_delta_rule(qb, kb, vb, g, beta)
    o_b = o_b * lax.rsqrt(jnp.mean(o_b * o_b, axis=-1, keepdims=True) + NORM_EPS) * norm_w.astype(f32)
    o_b = o_b * jax.nn.silu(z.astype(f32).reshape(bsz, T, B_HEADS, B_HEAD_DIM))
    o_b = o_b.reshape(bsz, T, B_W).astype(x.dtype)
    return jnp.concatenate([o_a, o_b], axis=-1) @ w_out

def rg_lru(x, w_a, b_a, w_x, b_x, lam):
    f32 = jnp.float32
    bsz, T, W = x.shape
    xh = x.reshape(bsz, T, LRU_BLOCKS, W // LRU_BLOCKS)
    r = jax.nn.sigmoid((jnp.einsum('bthi,hij->bthj', xh, w_a).reshape(bsz, T, W) + b_a).astype(f32))
    i = jax.nn.sigmoid((jnp.einsum('bthi,hij->bthj', xh, w_x).reshape(bsz, T, W) + b_x).astype(f32))
    log_a = -LRU_C * r * jax.nn.softplus(-lam.astype(f32))
    a = jnp.exp(log_a)
    b = jnp.sqrt(-jnp.expm1(2.0 * log_a)) * (i * x.astype(f32))

    def combine(c1, c2):
        a1, b1 = c1
        a2, b2 = c2
        return a1 * a2, a2 * b1 + b2

    _, h = lax.associative_scan(combine, (a, b), axis=1)
    return h.astype(x.dtype)

def recurrent_mixer(x, w_in, conv_w, conv_b, w_a, b_a, w_x, b_x, lam, w_out):
    proj = x @ w_in
    xr, gate = split_cols(proj, (LRU_WIDTH, LRU_WIDTH))
    xr = causal_dwconv(xr, conv_w, conv_b)
    h = rg_lru(xr, w_a, b_a, w_x, b_x, lam)
    return (h * jax.nn.gelu(gate)) @ w_out

def sqrelu_mlp(x, w1, w2):
    h = jax.nn.relu(x @ w1)
    return (h * h) @ w2

def first_inputs(seed: int = 0) -> dict:
    key = jax.random.key(seed)
    ks = jax.random.split(key, 24)
    f32 = jnp.float32

    def nrm(k, shape, scale):
        return jax.random.normal(k, shape, f32) * scale

    bw = LRU_WIDTH // LRU_BLOCKS
    x = nrm(ks[0], (BATCH, SEQ, D_MODEL), 1.0)
    hyb_w_in = nrm(ks[1], (N_HYB, D_MODEL, HYB_PROJ), D_MODEL ** -0.5)
    hyb_sinks = nrm(ks[2], (N_HYB, A_Q_HEADS), 0.5)
    hyb_conv_w = nrm(ks[3], (N_HYB, B_CONV, 3 * B_W), B_CONV ** -0.5)
    hyb_a_log = jnp.log(jax.random.uniform(ks[4], (N_HYB, B_HEADS), f32, 1.0, 16.0))
    dt = jnp.exp(jax.random.uniform(ks[5], (N_HYB, B_HEADS), f32, math.log(1e-3), math.log(1e-1)))
    hyb_dt_bias = dt + jnp.log(-jnp.expm1(-dt))
    hyb_norm_w = 1.0 + nrm(ks[6], (N_HYB, B_HEAD_DIM), 0.02)
    hyb_w_out = nrm(ks[7], (N_HYB, MIX_W, D_MODEL), DN_BETA * MIX_W ** -0.5)
    rec_w_in = nrm(ks[8], (N_REC, D_MODEL, 2 * LRU_WIDTH), D_MODEL ** -0.5)
    rec_conv_w = nrm(ks[9], (N_REC, LRU_CONV, LRU_WIDTH), LRU_CONV ** -0.5)
    rec_conv_b = nrm(ks[10], (N_REC, LRU_WIDTH), 0.02)
    rec_w_a = nrm(ks[11], (N_REC, LRU_BLOCKS, bw, bw), bw ** -0.5)
    rec_b_a = nrm(ks[12], (N_REC, LRU_WIDTH), 0.02)
    rec_w_x = nrm(ks[13], (N_REC, LRU_BLOCKS, bw, bw), bw ** -0.5)
    rec_b_x = nrm(ks[14], (N_REC, LRU_WIDTH), 0.02)
    u = jax.random.uniform(ks[15], (N_REC, LRU_WIDTH), f32, 0.9, 0.999)
    a0 = u ** (1.0 / LRU_C)
    rec_lambda = jnp.log(a0) - jnp.log1p(-a0)
    rec_w_out = nrm(ks[16], (N_REC, LRU_WIDTH, D_MODEL), DN_BETA * LRU_WIDTH ** -0.5)
    ln1_g = 1.0 + nrm(ks[17], (DEPTH, D_MODEL), 0.02)
    ln1_b = nrm(ks[18], (DEPTH, D_MODEL), 0.02)
    mlp_w1 = nrm(ks[19], (DEPTH, D_MODEL, D_FF), D_MODEL ** -0.5)
    mlp_w2 = nrm(ks[20], (DEPTH, D_FF, D_MODEL), DN_BETA * D_FF ** -0.5)
    ln2_g = 1.0 + nrm(ks[21], (DEPTH, D_MODEL), 0.02)
    ln2_b = nrm(ks[22], (DEPTH, D_MODEL), 0.02)
    return {'x': x, 'hyb_w_in': hyb_w_in, 'hyb_sinks': hyb_sinks, 'hyb_conv_w': hyb_conv_w,
            'hyb_a_log': hyb_a_log, 'hyb_dt_bias': hyb_dt_bias, 'hyb_norm_w': hyb_norm_w,
            'hyb_w_out': hyb_w_out, 'rec_w_in': rec_w_in, 'rec_conv_w': rec_conv_w,
            'rec_conv_b': rec_conv_b, 'rec_w_a': rec_w_a, 'rec_b_a': rec_b_a, 'rec_w_x': rec_w_x,
            'rec_b_x': rec_b_x, 'rec_lambda': rec_lambda, 'rec_w_out': rec_w_out,
            'ln1_g': ln1_g, 'ln1_b': ln1_b, 'mlp_w1': mlp_w1, 'mlp_w2': mlp_w2,
            'ln2_g': ln2_g, 'ln2_b': ln2_b}

def first_block(x, hyb_w_in, hyb_sinks, hyb_conv_w, hyb_a_log, hyb_dt_bias, hyb_norm_w, hyb_w_out,
              rec_w_in, rec_conv_w, rec_conv_b, rec_w_a, rec_b_a, rec_w_x, rec_b_x, rec_lambda,
              rec_w_out, ln1_g, ln1_b, mlp_w1, mlp_w2, ln2_g, ln2_b):
    for layer in range(DEPTH):
        j = layer // 2
        if layer % 2 == 0:
            mix = hybrid_mixer(x, hyb_w_in[j], hyb_sinks[j], hyb_conv_w[j], hyb_a_log[j],
                               hyb_dt_bias[j], hyb_norm_w[j], hyb_w_out[j])
        else:
            mix = recurrent_mixer(x, rec_w_in[j], rec_conv_w[j], rec_conv_b[j], rec_w_a[j],
                                  rec_b_a[j], rec_w_x[j], rec_b_x[j], rec_lambda[j], rec_w_out[j])
        x = layer_norm(DN_ALPHA * x + mix, ln1_g[layer], ln1_b[layer])
        x = layer_norm(DN_ALPHA * x + sqrelu_mlp(x, mlp_w1[layer], mlp_w2[layer]), ln2_g[layer], ln2_b[layer])
    return x


HEAD_DIM = 64
A_GROUPS = ((128, 1), (512, 4), (2048, 16))
A_HEADS_PER_GROUP = 4
A_HEADS = A_HEADS_PER_GROUP * len(A_GROUPS)
A_WIDTH = A_HEADS * HEAD_DIM
B_HEADS_2 = D_MODEL // HEAD_DIM
B_WIDTH = B_HEADS_2 * HEAD_DIM
N_A = DEPTH // 2
N_B = DEPTH - N_A
D_FF_2 = 2816
CONV_W = 3
ROPE_DIM = HEAD_DIM // 4
ROPE_THETA_2 = 500000.0
BLK = 128
EPS = 1e-6
NEG = -1e30


def rms_norm(x, g):
    x32 = x.astype(jnp.float32)
    y = x32 * lax.rsqrt(jnp.mean(x32 * x32, axis=-1, keepdims=True) + EPS)
    return (y * g.astype(jnp.float32)).astype(x.dtype)

def rope_tables(T):
    pos = jnp.arange(T, dtype=jnp.float32)
    inv = ROPE_THETA_2 ** (-jnp.arange(0, ROPE_DIM, 2, dtype=jnp.float32) / ROPE_DIM)
    ang = pos[:, None] * inv[None, :]
    return jnp.cos(ang), jnp.sin(ang)

def apply_rope_2(t, cos, sin):
    half = ROPE_DIM // 2
    c = cos[None, :, None, :].astype(t.dtype)
    s = sin[None, :, None, :].astype(t.dtype)
    x1 = t[..., :half]
    x2 = t[..., half:ROPE_DIM]
    return jnp.concatenate([x1 * c - x2 * s, x2 * c + x1 * s, t[..., ROPE_DIM:]], axis=-1)

def banded_attention(q, k, v, n_back):
    N, L, H, D = q.shape
    nb = L // BLK
    qb = q.reshape(N, nb, BLK, H, D)
    kb = k.reshape(N, nb, BLK, H, D)
    vb = v.reshape(N, nb, BLK, H, D)

    def with_prev(t):
        prev = jnp.pad(t[:, :-1], ((0, 0), (1, 0), (0, 0), (0, 0), (0, 0)))
        return jnp.concatenate([prev, t], axis=2)

    kc, vc = with_prev(kb), with_prev(vb)
    s = jnp.einsum('nbqhd,nbkhd->nbhqk', qb, kc).astype(jnp.float32) * (D ** -0.5)
    rel = (jnp.arange(BLK)[:, None] + BLK) - jnp.arange(2 * BLK)[None, :]
    band = (rel >= 0) & (rel <= n_back)
    has_prev = (jnp.arange(nb)[:, None, None] > 0) | (jnp.arange(2 * BLK)[None, None, :] >= BLK)
    mask = band[None] & has_prev
    s = jnp.where(mask[None, :, None], s, NEG)
    m = jnp.max(s, axis=-1, keepdims=True)
    p = jnp.exp(s - m)
    l = jnp.sum(p, axis=-1, keepdims=True)
    o = jnp.einsum('nbhqk,nbkhd->nbqhd', (p / l).astype(v.dtype), vc)
    lse = (m + jnp.log(l))[..., 0]
    return o.reshape(N, L, H, D), lse.transpose(0, 1, 3, 2).reshape(N, L, H)

def dilated_mixer(xn, w_qkv, w_o, cos, sin):
    B, T, _ = xn.shape
    qkv = xn @ w_qkv
    q, k, v = jnp.split(qkv, 3, axis=-1)
    q = apply_rope_2(q.reshape(B, T, A_HEADS, HEAD_DIM), cos, sin)
    k = apply_rope_2(k.reshape(B, T, A_HEADS, HEAD_DIM), cos, sin)
    v = v.reshape(B, T, A_HEADS, HEAD_DIM)
    G = A_HEADS_PER_GROUP
    outs, lses = [], []
    for g, (window, r) in enumerate(A_GROUPS):
        L = T // r
        Lp = -(-L // BLK) * BLK

        def gather(t):
            t = t[:, :, g * G:(g + 1) * G].reshape(B, L, r, G, HEAD_DIM)
            t = t.transpose(0, 2, 1, 3, 4).reshape(B * r, L, G, HEAD_DIM)
            return jnp.pad(t, ((0, 0), (0, Lp - L), (0, 0), (0, 0)))

        o, lse = banded_attention(gather(q), gather(k), gather(v), window // r)
        o = o[:, :L].reshape(B, r, L, G, HEAD_DIM).transpose(0, 2, 1, 3, 4).reshape(B, T, G, HEAD_DIM)
        lse = lse[:, :L].reshape(B, r, L, G).transpose(0, 2, 1, 3).reshape(B, T, G)
        outs.append(o)
        lses.append(lse)
    alpha = jax.nn.softmax(jnp.stack(lses, axis=0), axis=0)
    o = jnp.concatenate([outs[g] * alpha[g][..., None].astype(outs[g].dtype)
                         for g in range(len(A_GROUPS))], axis=2)
    return o.reshape(B, T, A_WIDTH) @ w_o

def fox_mixer(xn, w_q, w_o, k, v, c):
    B, T, _ = xn.shape
    q = (xn @ w_q).reshape(B, T, B_HEADS_2, HEAD_DIM)
    c_t = c.transpose(0, 2, 1)
    scale = HEAD_DIM ** -0.5
    outs = []
    for i in range(T // BLK):
        q0, q1 = i * BLK, (i + 1) * BLK
        s = jnp.einsum('bqhd,bkhd->bhqk', q[:, q0:q1], k[:, :q1]).astype(jnp.float32) * scale
        s = s + (c_t[:, :, q0:q1, None] - c_t[:, :, None, :q1])
        causal = jnp.arange(q0, q1)[:, None] >= jnp.arange(q1)[None, :]
        s = jnp.where(causal, s, NEG)
        p = jax.nn.softmax(s, axis=-1).astype(v.dtype)
        outs.append(jnp.einsum('bhqk,bkhd->bqhd', p, v[:, :q1]))
    o = jnp.concatenate(outs, axis=1)
    return o.reshape(B, T, B_WIDTH) @ w_o

def conv_ffn(xn, w_up, cw, cb, w_down):
    a = xn @ w_up
    T = a.shape[1]
    ap = jnp.pad(a, ((0, 0), (CONV_W - 1, 0), (0, 0)))
    a = sum(ap[:, j:j + T] * cw[j] for j in range(CONV_W)) + cb
    gate, val = jnp.split(a, 2, axis=-1)
    return (jax.nn.gelu(gate, approximate=True) * val) @ w_down

def second_inputs(seed: int = 0) -> dict:
    key = jax.random.key(seed)
    ks = jax.random.split(key, 14)

    def nrm(k, shape, fan_in):
        return jax.random.normal(k, shape, jnp.float32) * fan_in ** -0.5

    return {
        "x": jax.random.normal(ks[0], (BATCH, SEQ, D_MODEL), jnp.float32),
        "norm_gains": 1.0 + 0.05 * jax.random.normal(ks[1], (DEPTH, 4, D_MODEL), jnp.float32),
        "w_qkv_a": nrm(ks[2], (N_A, D_MODEL, 3 * A_WIDTH), D_MODEL),
        "w_o_a": nrm(ks[3], (N_A, A_WIDTH, D_MODEL), A_WIDTH),
        "w_q_b": nrm(ks[4], (N_B, D_MODEL, B_WIDTH), D_MODEL),
        "w_o_b": nrm(ks[5], (N_B, B_WIDTH, D_MODEL), B_WIDTH),
        "kv_norm": 1.0 + 0.05 * jax.random.normal(ks[6], (D_MODEL,), jnp.float32),
        "w_kvf": nrm(ks[7], (D_MODEL, 2 * B_WIDTH + B_HEADS_2), D_MODEL),
        "b_f": 3.0 + 0.5 * jax.random.normal(ks[8], (B_HEADS_2,), jnp.float32),
        "w_up": nrm(ks[9], (DEPTH, D_MODEL, 2 * D_FF_2), D_MODEL),
        "conv_w": nrm(ks[10], (DEPTH, CONV_W, 2 * D_FF_2), CONV_W),
        "conv_b": 0.01 * jax.random.normal(ks[11], (DEPTH, 2 * D_FF_2), jnp.float32),
        "w_down": nrm(ks[12], (DEPTH, D_FF_2, D_MODEL), D_FF_2),
    }

def second_block(x, norm_gains, w_qkv_a, w_o_a, w_q_b, w_o_b, kv_norm, w_kvf, b_f,
              w_up, conv_w, conv_b, w_down):
    B, T, _ = x.shape
    cos, sin = rope_tables(T)
    h = x
    k_sh = v_sh = c_sh = None
    for l in range(DEPTH):
        g = norm_gains[l]
        if l < N_A:
            mix = dilated_mixer(rms_norm(h, g[0]), w_qkv_a[l], w_o_a[l], cos, sin)
        else:
            if l == N_A:
                kvf = rms_norm(h, kv_norm) @ w_kvf
                k_sh = kvf[..., :B_WIDTH].reshape(B, T, B_HEADS_2, HEAD_DIM)
                v_sh = kvf[..., B_WIDTH:2 * B_WIDTH].reshape(B, T, B_HEADS_2, HEAD_DIM)
                log_f = jax.nn.log_sigmoid((kvf[..., 2 * B_WIDTH:] + b_f).astype(jnp.float32))
                c_sh = jnp.cumsum(log_f, axis=1)
            j = l - N_A
            mix = fox_mixer(rms_norm(h, g[0]), w_q_b[j], w_o_b[j], k_sh, v_sh, c_sh)
        h = h + rms_norm(mix, g[1])
        f = conv_ffn(rms_norm(h, g[2]), w_up[l], conv_w[l], conv_b[l], w_down[l])
        h = h + rms_norm(f, g[3])
    return h


def setup_inputs(seed=0):
    out = dict(first_inputs(seed))
    for name, value in second_inputs(seed + 1).items():
        if name != "x":
            out[name + "_2"] = value
    return out


def reference(
    x, hyb_w_in, hyb_sinks, hyb_conv_w, hyb_a_log, hyb_dt_bias, hyb_norm_w, hyb_w_out, rec_w_in,
    rec_conv_w, rec_conv_b, rec_w_a, rec_b_a, rec_w_x, rec_b_x, rec_lambda, rec_w_out, ln1_g,
    ln1_b, mlp_w1, mlp_w2, ln2_g, ln2_b, norm_gains_2, w_qkv_a_2, w_o_a_2, w_q_b_2, w_o_b_2,
    kv_norm_2, w_kvf_2, b_f_2, w_up_2, conv_w_2, conv_b_2, w_down_2,
):
    x = first_block(
        x, hyb_w_in, hyb_sinks, hyb_conv_w, hyb_a_log, hyb_dt_bias, hyb_norm_w, hyb_w_out,
        rec_w_in, rec_conv_w, rec_conv_b, rec_w_a, rec_b_a, rec_w_x, rec_b_x, rec_lambda,
        rec_w_out, ln1_g, ln1_b, mlp_w1, mlp_w2, ln2_g, ln2_b,
    )
    return second_block(
        x, norm_gains_2, w_qkv_a_2, w_o_a_2, w_q_b_2, w_o_b_2, kv_norm_2, w_kvf_2, b_f_2,
        w_up_2, conv_w_2, conv_b_2, w_down_2,
    )


_drawn_inputs = setup_inputs


def setup_inputs(seed=0):
    import zlib

    import numpy as np

    out = dict(_drawn_inputs(seed))
    spreads = {}
    factors = {'hyb_sinks': 26.336,
     'hyb_a_log': 3.104,
     'hyb_norm_w': 23.337,
     'rec_b_a': 51.386,
     'rec_b_x': 8.0,
     'conv_b_2': 4.932}
    for name, (base, spread) in spreads.items():
        noise = np.random.default_rng([zlib.crc32(name.encode()), seed]).standard_normal(out[name].shape)
        drawn = base * np.exp(spread * noise) if base else spread * noise
        out[name] = __import__('jax').numpy.asarray(drawn.astype(out[name].dtype))
    for name, factor in factors.items():
        out[name] = (out[name] * factor).astype(out[name].dtype)
    return out
```

```python
import numpy as np
import concourse.bass as bass
from concourse import mybir
from contextlib import ExitStack

F = mybir.dt.float32
R = mybir.dt.float32r
ACT = mybir.ActivationFunctionType
ALU = mybir.AluOpType
AXX = mybir.AxisListType.X

T = 512
ALPHA = 4 ** 0.25

VEC_SIZES = [
    ("ln1g", 16), ("ln1b", 16), ("ln2g", 16), ("ln2b", 16), ("ng", 64), ("kvn", 8),
    ("hcw", 48), ("hnw", 1), ("sink", 8), ("alog", 1), ("dtb", 1),
    ("rcw", 32), ("rcb", 8), ("rba", 8), ("rbx", 8), ("lam", 8),
    ("bf", 1), ("fcw", 264), ("fcb", 88),
]
VEC_AT = {}
_n = 0
for _name, _k in VEC_SIZES:
    VEC_AT[_name] = _n
    _n += _k
NVEC = _n

SMALL = ["ident", "onesd", "ones", "rot1", "rot2"]
C0 = [("cos", 512), ("sin", 512), ("mi", 128), ("ms", 128), ("lv", 896), ("sel", 512), ("slide", 256)]
C2 = [("cos", 512), ("sin", 512), ("dil1", 256), ("causal", 512), ("dil3", 128), ("sel2", 256)]
C3 = [("causal", 512), ("seln", 2048)]


def places(parts):
    at, out = 0, {}
    for name, k in parts:
        out[name] = (at, k)
        at += k
    return out, at


def plan_units():
    plan = [("hyb", i, 8) for i in range(23)] + [("hwo", i, 8) for i in range(8)]

    def mlp(l):
        out = []
        for q in range(4):
            out += [(f"w1_{l}", q * 8 + m, 8) for m in range(8)]
            out += [(f"w2_{l}", q * 8 + m, 8) for m in range(8)]
        return out

    def ffn(l):
        out = []
        for q, n in enumerate((8, 8, 6)):
            out += [(f"up_{l}", 2 * (q * 8 + i) + s, 8) for i in range(n) for s in range(2)]
            out += [(f"dn{n}_{l}", (q * 8 if n == 8 else 0) + m, n) for m in range(8)]
        return out

    plan += mlp(0)
    plan += [("rin", i, 8) for i in range(16)] + [("rwg", i, 8) for i in range(4)]
    plan += [("rwo", i, 8) for i in range(8)]
    plan += mlp(1)
    plan += [("qkv", i, 8) for i in range(18)] + [("woa", i, 6) for i in range(8)]
    plan += ffn(0)
    plan += [("kvf", i, 8) for i in range(17)] + [("wqb", i, 8) for i in range(8)]
    plan += [("wob", i, 8) for i in range(8)]
    plan += ffn(1)
    return plan


class Program:

    def __init__(self, sems, dsems):
        self.sems = sems
        self.dsems = dsems
        self.q = {e: [] for e in ("pe", "act", "dve", "pool", "sp")}
        self.count = {e: 0 for e in self.q}
        self.seen = {e: {} for e in self.q}
        self.ndma = {"sp": 0, "pool": 0}
        self.dlast = {}

    def waits(self, e, after):
        out = []
        for t in flat(after):
            if self.seen[e].get(t[0], 0) < t[1]:
                self.seen[e][t[0]] = t[1]
                out.append(t)
        return out

    def op(self, e, fn, *after, inc=True):
        w = self.waits(e, after)
        if inc:
            self.count[e] += 1
        self.q[e].append((w, fn, (e, 1) if inc else None))
        return (e, self.count[e]) if inc else None

    def dma(self, e, out, in_, *after):
        ring = self.dsems[e]
        s = ring[self.ndma[e] % len(ring)]
        self.ndma[e] += 1
        before = self.dlast.get(s)
        w = self.waits(e, [after, before or []])
        self.dlast[s] = (s, (before[1] if before else 0) + 16)
        self.q[e].append((w, lambda g: g.dma_start(out, in_), (s, 16)))
        return self.dlast[s]

    def now(self, *engines):
        return [(e, self.count[e]) for e in engines if self.count[e]]

    def fence(self, *also, engines=("pe", "act", "dve", "pool")):
        j = self.now("pe", "act", "dve", "pool") + list(flat(also))
        for e in engines:
            w = self.waits(e, j)
            if w:
                self.q[e].append((w, None, None))
        return j

    def play(self, e, eng):
        for w, fn, inc in self.q[e]:
            for s, v in w:
                eng.wait_ge(self.sems[s], v)
            if fn is None:
                continue
            ins = fn(eng)
            if inc is not None:
                ins.then_inc(self.sems[inc[0]], inc[1])


def flat(x):
    if x is None:
        return
    if isinstance(x, tuple) and len(x) == 2 and isinstance(x[0], str):
        yield x
        return
    for y in x:
        yield from flat(y)


def build_program(nc, D):
    with ExitStack() as ctx:
        def sb(name, shape, dt=F):
            return ctx.enter_context(nc.sbuf_tensor(name, shape, dt))

        names = ["pe", "act", "dve", "pool"] + [f"ds{i}" for i in range(6)] + [f"dp{i}" for i in range(6)]
        sems = {n: ctx.enter_context(nc.semaphore("s_" + n)) for n in names}
        p = Program(sems, {"sp": [f"ds{i}" for i in range(6)], "pool": [f"dp{i}" for i in range(6)]})

        NRAW, NW = 3, 4
        RAW = sb("RAW", [128, NRAW, 2, 1024])
        WH = sb("WH", [128, NW, 1024], R)
        WL = sb("WL", [128, NW, 1024], R)
        X = sb("X", [128, 8, T])
        XH = sb("XH", [128, 8, T], R)
        XL = sb("XL", [128, 8, T], R)
        Y = sb("Y", [128, 8, T])
        TM = sb("TM", [128, 8, T])
        VEC = sb("VEC", [128, NVEC])
        CST = sb("CST", [128, len(SMALL) * 128])
        COL = sb("COL", [128, 256])
        with nc.sbuf_tensor("H", [128, 32, T], R) as H:
            pass
        AR = sb("AR", [128, 32, T])
        PS = [ctx.enter_context(nc.psum_tensor(f"ps{i}", [128, T], F)) for i in range(8)]

        cst = {n: CST[:, 128 * i:128 * i + 128] for i, n in enumerate(SMALL)}
        ident, ones, onesd = cst["ident"], cst["ones"], cst["onesd"]

        def vec(name, i=0, n=1, lo=0, hi=128):
            a = VEC_AT[name] + i
            return VEC[lo:hi, a:a + n]

        def act(out, in_, func, *after, scale=1.0, bias=0.0, accum=None):
            def go(g):
                kw = {} if accum is None else {"accum_out": accum}
                return g.activation(out, in_, func, bias=bias, scale=scale, **kw)
            return p.op("act", go, *after)

        def tt(out, a, b, op, *after, e="dve"):
            return p.op(e, lambda g: g.tensor_tensor(out, a, b, op), *after)

        def ts(out, a, s1, op0, *after, s2=None, op1=ALU.bypass, e="dve"):
            return p.op(e, lambda g: g.tensor_scalar(out, a, s1, s2, op0, op1), *after)

        def stt(out, a, s, b, op0, op1, *after):
            return p.op("dve", lambda g: g.scalar_tensor_tensor(out, a, s, b, op0, op1), *after)

        def copy(out, a, *after, e="dve"):
            return p.op(e, lambda g: g.tensor_copy(out, a), *after)

        def mm(out, lhsT, rhs, start, stop, *after, inc=False):
            return p.op("pe", lambda g: g.matmul(out, lhsT, rhs, start=start, stop=stop), *after, inc=inc)

        def tr(out, in_, idn, *after, inc=False):
            return p.op("pe", lambda g: g.transpose(out, in_, idn), *after, inc=inc)

        def scan(out, a, b, *after):
            return p.op("dve", lambda g: g.tensor_tensor_scan(out, a, b, 0.0, ALU.mult, ALU.add), *after)

        def recip(out, a, *after):
            return p.op("dve", lambda g: g.reciprocal(out, a), *after)

        def rmax(out, a, *after, negate=False):
            return p.op("dve", lambda g: g.reduce_max(out, a, AXX, negate=negate), *after)

        def fill(out, value, *after):
            return p.op("dve", lambda g: g.memset(out, value), *after)

        def f32(ap):
            return ap.bitcast(F)

        def split(h, l, src, *after):
            a = act(h, src, ACT.Copy, *after)
            return [a, tt(l, src, f32(h), ALU.subtract, a, *after)]

        PLAN = plan_units()
        groups, i = [], 0
        while i < len(PLAN):
            name, at, kb = PLAN[i]
            two = i + 1 < len(PLAN) and PLAN[i + 1] == (name, at + 1, kb)
            groups.append((name, at, kb, i, 2 if two else 1))
            i += 2 if two else 1
        where = {}
        for gi, (name, at, kb, u, n) in enumerate(groups):
            for k in range(n):
                where[u + k] = (gi, k)
        gtok, gread = {}, {}
        wtok = {}
        wfree = {}
        nx = {"group": 0, "split": 0, "unit": 0}

        def load_group():
            gi = nx["group"]
            if gi >= len(groups):
                return
            nx["group"] += 1
            name, at, kb, u, n = groups[gi]
            free = gread.get(gi - NRAW)
            dst = RAW[:, gi % NRAW, 0:n, 0:kb * 128]
            src = D[name][at:at + n, :, :].rearrange("u p c -> p u c")
            gtok[gi] = p.dma("sp", dst, src, free)

        def split_unit(u):
            if u >= len(PLAN):
                return
            gi, k = where[u]
            kb = PLAN[u][2]
            s = u % NW
            src = RAW[:, gi % NRAW, k, 0:kb * 128]
            wtok[u] = split(WH[:, s, 0:kb * 128], WL[:, s, 0:kb * 128], src, gtok[gi], wfree.get(s))
            if k == groups[gi][4] - 1:
                gread[gi] = wtok[u]
                load_group()

        for _ in range(NRAW):
            load_group()

        def next_unit(name):
            u = nx["unit"]
            assert PLAN[u][0] == name, (PLAN[u], name)
            nx["unit"] += 1
            while nx["split"] < min(u + 4, len(PLAN)):
                split_unit(nx["split"])
                nx["split"] += 1
            return u

        bank = {"n": 0}
        bfree = {}

        def next_bank(n=4):
            b = bank["n"] % n
            bank["n"] += 1
            return b

        def unit(name, xh, xl, xtok):
            u = next_unit(name)
            kb, s = PLAN[u][2], u % NW
            b = next_bank()
            out = PS[b][:, :]
            tok = None
            for k in range(kb):
                wh, wl = WH[:, s, 128 * k:128 * k + 128], WL[:, s, 128 * k:128 * k + 128]
                mm(out, wh, xh[k], k == 0, False, wtok[u] if k == 0 else None, bfree.get(b) if k == 0 else None, xtok[k])
                mm(out, wh, xl[k], False, False)
                tok = mm(out, wl, xh[k], False, k == kb - 1, inc=k == kb - 1)
            wfree[s] = tok
            return b, out, tok

        def unit_tok(name, xtok, strided):
            u = next_unit(name)
            s = u % NW
            b = next_bank()
            tok = None
            for t in range(4):
                for k in range(8):
                    tk = slice(t, T, 4) if strided else slice(128 * t, 128 * t + 128)
                    wh, wl = WH[:, s, 128 * k:128 * k + 128], WL[:, s, 128 * k:128 * k + 128]
                    out = PS[b][:, 128 * t:128 * t + 128]
                    mm(out, XH[:, k, tk], wh, k == 0, False, wtok[u] if t == k == 0 else None,
                       bfree.get(b) if t == k == 0 else None, xtok[k])
                    mm(out, XL[:, k, tk], wh, False, False)
                    tok = mm(out, XH[:, k, tk], wl, False, k == 7, inc=t == 3 and k == 7)
            wfree[s] = tok
            return b, PS[b][:, :], tok

        XHL = [XH[:, k, :] for k in range(8)], [XL[:, k, :] for k in range(8)]

        st = {}

        def stat(y, m, tok, mean):
            S1, S2 = TM[:, 0, :], TM[:, 1, :]
            if m == 0:
                st["s2"] = act(S2, y, ACT.Square, tok, st.get("free"))
                st["s1"] = copy(S1, y, tok, st.get("free"), e="pool") if mean else None
                st["sq"] = {}
                return
            sq = TM[:, 6 + m % 2, :]
            a = act(sq, y, ACT.Square, tok, st["sq"].get(m % 2), st.get("sqfree") if m < 3 else None)
            st["s2"] = tt(S2, S2, sq, ALU.add, a, st["s2"])
            st["sq"][m % 2] = st["s2"]
            if mean:
                st["s1"] = tt(S1, S1, y, ALU.add, tok, st["s1"], e="pool")

        def rstd_of(out, var_psum, scale, eps, *after):
            a = act(out, var_psum, ACT.Ln, *after, bias=eps, scale=scale)
            return act(out, out, ACT.Exp, a, scale=-0.5)

        def stats_end(mean, eps_col):
            S1, S2, RS = TM[:, 0, :], TM[:, 1, :], TM[:, 2, :]
            b2 = next_bank()
            t2 = mm(PS[b2][:, :], onesd, S2, True, True, st["s2"], bfree.get(b2), inc=True)
            if not mean:
                r = rstd_of(RS, PS[b2][:, :], 1.0, eps_col, t2)
                bfree[b2] = r
                st["free"] = t2
                return None, [], r, None
            b1 = next_bank()
            t1 = mm(PS[b1][:, :], onesd, S1, True, True, st["s1"], bfree.get(b1), inc=True)
            a = act(S1, PS[b1][:, :], ACT.Square, t1)
            v = tt(S2, PS[b2][:, :], S1, ALU.subtract, a, t2)
            bfree[b2] = v
            v2 = ts(S2, S2, 0.0, ALU.max, v)
            r = rstd_of(RS, S2, 1.0, eps_col, v2)
            st["free"] = [r]
            return PS[b1][:, :], t1, r, b1

        def layer_norm(gname, bname, l):
            M, mt, r, b1 = stats_end(True, EPS5)
            RS = TM[:, 2, :]
            toks = []
            pe = p.now("pe")
            free = {}
            for m in range(8):
                t = TM[:, 3 + m % 3, :]
                a = tt(t, X[:, m, :], M, ALU.subtract, mt, xw[m], free.get(m % 3))
                a2 = tt(t, t, RS, ALU.mult, a, r, e="pool")
                xa = act(X[:, m, :], t, ACT.Identity, a2, scale=vec(gname, 8 * l + m), bias=vec(bname, 8 * l + m))
                free[m % 3] = xa
                xw[m] = xa
                toks.append(split(XH[:, m, :], XL[:, m, :], X[:, m, :], xa, pe))
                if m == 7:
                    bfree[b1] = a
            return toks

        def rms_apply(src, r, gname, gi, srctok):
            RS = TM[:, 2, :]
            toks, free = [], {}
            pe = p.now("pe")
            for m in range(8):
                t = TM[:, 3 + m % 3, :]
                a = stt(t, src[:, m, :], vec(gname, gi + m), RS, ALU.mult, ALU.mult, r, srctok[m], free.get(m % 3))
                toks.append(split(XH[:, m, :], XL[:, m, :], t, a, pe))
                free[m % 3] = toks[-1]
            st["rs_free"] = toks[-1]
            return toks

        def rms_add(r, gi, ytok, with_stats=True):
            RS = TM[:, 2, :]
            free = {}
            for m in range(8):
                t = TM[:, 3 + m % 2, :]
                a = stt(t, Y[:, m, :], vec("ng", gi + m), RS, ALU.mult, ALU.mult, r, ytok[m], free.get(m % 2))
                xw[m] = tt(X[:, m, :], X[:, m, :], t, ALU.add, a, xw[m], e="pool")
                free[m % 2] = xw[m]
                if with_stats:
                    stat(X[:, m, :], m, xw[m], False)

        t_cst = p.dma("pool", CST[:, :], D["small"])
        t_vec = p.dma("pool", VEC[:, :], D["vec"])
        xw = [None] * 8
        for h in range(2):
            t = p.dma("sp", X[:, 4 * h:4 * h + 4, :], D["x"].rearrange("(k p) t -> p k t", p=128)[:, 4 * h:4 * h + 4, :])
            for m in range(4):
                xw[4 * h + m] = t
        EPS5, EPS6 = COL[:, 254:255], COL[:, 255:256]
        e1 = fill(EPS5, 1e-5)
        e2 = fill(EPS6, 1e-6)
        xtok = [split(XH[:, m, :], XL[:, m, :], X[:, m, :], xw[m]) for m in range(8)]
        at0, n0 = places(C0)
        Yf = Y[:, :, :].rearrange("p a b -> p (a b)")
        ARf = AR[:, :, :].rearrange("p a b -> p (a b)")
        t_c0 = p.dma("pool", Yf[:, 0:n0], D["c0"])
        for e in ("act", "dve", "pe", "pool"):
            w = p.waits(e, [t_cst, t_vec, e1, e2])
            p.q[e].append((w, None, None))

        def c_of(base, at, name, lo=0, hi=128):
            a, k = at[name]
            return base[lo:hi, a:a + k]

        def softplus_rows(out, x, tmp, *after):
            u, w, l, d = tmp
            a = act(u, x, ACT.Abs, *after)
            a = act(u, u, ACT.Exp, a, scale=-1.0)
            b = ts(w, u, 1.0, ALU.add, a)
            a = act(l, w, ACT.Ln, b)
            b = ts(d, w, -1.0, ALU.add, b)
            c = ts(w, d, 0.0, ALU.is_equal, b, a)
            e = tt(l, l, w, ALU.add, a, c)
            f = tt(d, d, w, ALU.add, c)
            f = recip(d, d, f)
            e = tt(l, l, d, ALU.mult, e, f)
            e = tt(l, l, u, ALU.mult, e)
            return stt(out, x, 0.0, l, ALU.max, ALU.add, e, *after)

        def conv_psum(dst, ps, w, taps, first, *after):
            a = act(dst, ps, ACT.Identity, *after, scale=w(taps - 1), bias=first)
            for j in range(taps - 2, -1, -1):
                s = taps - 1 - j
                a = stt(dst[:, s:T], ps[:, 0:T - s], w(j), dst[:, s:T], ALU.mult, ALU.add, a, *after)
            return a

        def rope(dst, ps, tok, rot, cos, sin, tmp, tmpfree, b, *after):
            a = act(dst, ps, ACT.Copy, tok, *after)
            b2 = next_bank()
            t = mm(PS[b2][:, :], rot, dst, True, True, a, bfree.get(b2), inc=True)
            d = tt(tmp, PS[b2][:, :], sin, ALU.mult, t, tmpfree)
            bfree[b] = a
            bfree[b2] = d
            e = tt(dst, dst, cos, ALU.mult, a, t, e="pool")
            return tt(dst, dst, tmp, ALU.add, d, e)

        def attention(jobs, scale, lse=None):
            n = len(jobs)
            S = {}

            def A(i):
                j = jobs[i]
                nk = j["nk"]
                ps = PS[4 + i % 2][:, 0:nk]
                more = j.get("more")
                t = mm(ps, j["q"], j["k"], True, more is None, j.get("after"), S.get(("fa", i - 2)), inc=more is None)
                if more is not None:
                    t = mm(ps, more[0], more[1], False, True, inc=True)
                S[("a", i)] = t

            def B(i):
                j = jobs[i]
                nk = j["nk"]
                t = TM[:, i % 3, 0:nk]
                if "cq" in j:
                    a = stt(t, PS[4 + i % 2][:, 0:nk], j["cq"], j["mask"], ALU.add, ALU.add, S[("a", i)], S.get(("e", i - 3)))
                else:
                    a = stt(t, PS[4 + i % 2][:, 0:nk], scale, j["mask"], ALU.mult, ALU.add, S[("a", i)], S.get(("e", i - 3)))
                S[("fa", i)] = a
                nm = COL[:, 8 * (i % 3):8 * (i % 3) + 1]
                if "sink" in j:
                    mx = COL[:, 8 * (i % 3) + 4:8 * (i % 3) + 5]
                    b = rmax(mx, t, a, S.get(("c", i - 3)))
                    S[("b", i)] = ts(nm, mx, j["sink"], ALU.max, b, S.get(("c", i - 3)), s2=-1.0, op1=ALU.mult)
                else:
                    S[("b", i)] = rmax(nm, t, a, S.get(("c", i - 3)), S.get(("dd", i - 3)), negate=True)

            def C(i):
                j = jobs[i]
                t = TM[:, i % 3, 0:j["nk"]]
                nm = COL[:, 8 * (i % 3):8 * (i % 3) + 1]
                l = COL[:, 8 * (i % 3) + 1:8 * (i % 3) + 2]
                S[("c", i)] = act(t, t, ACT.Exp, S[("b", i)], S.get(("d", i - 3)), bias=nm, accum=l)
                if "sink" in j:
                    es = COL[:, 8 * (i % 3) + 2:8 * (i % 3) + 3]
                    S[("c", i)] = act(es, j["sink"], ACT.Exp, S[("b", i)], S.get(("d", i - 3)), bias=nm)

            def Dn(i):
                j = jobs[i]
                nk = j["nk"]
                t = TM[:, i % 3, 0:nk]
                c = 8 * (i % 3)
                l, es, r = COL[:, c + 1:c + 2], COL[:, c + 2:c + 3], COL[:, c + 3:c + 4]
                a = S[("c", i)]
                if "sink" in j:
                    a = tt(l, l, es, ALU.add, a)
                S[("dd", i)] = None
                if lse is not None:
                    copy(j["lout"], l, a)
                    S[("dd", i)] = ts(j["mout"], COL[:, c:c + 1], -1.0, ALU.mult, S[("b", i)])
                a = recip(r, l, a)
                S[("d", i)] = ts(t, t, r, ALU.mult, a)

            def E_(i):
                j = jobs[i]
                nb = j["nk"] // 128
                t = None
                for x in range(nb):
                    t = tr(PS[6 + i % 2][:, 128 * x:128 * x + 128], TM[:, i % 3, 128 * x:128 * x + 128], ident,
                           S[("d", i)], S.get(("f", i - 2)), inc=x == nb - 1)
                S[("e", i)] = t

            def F_(i):
                nk = jobs[i]["nk"]
                S[("f", i)] = act(TM[:, 3 + i % 2, 0:nk], PS[6 + i % 2][:, 0:nk], ACT.Copy, S[("e", i)], S.get(("g", i - 2)))

            def G(i):
                j = jobs[i]
                nb = j["nk"] // 128
                t = None
                for x in range(nb):
                    t = mm(j["out"], j["v"][x], TM[:, 3 + i % 2, 128 * x:128 * x + 128], x == 0, x == nb - 1,
                           S[("f", i)], j.get("outfree"), inc=x == nb - 1)
                S[("g", i)] = t
                if "then" in j:
                    j["then"](t)

            A(0)
            for i in range(n + 2):
                if i + 1 < n:
                    A(i + 1)
                if i < n:
                    B(i)
                    C(i)
                if 0 <= i - 1 < n:
                    Dn(i - 1)
                    E_(i - 1)
                    F_(i - 1)
                if 0 <= i - 2 < n:
                    G(i - 2)

        def mix_out(name, nk, otok):
            for m in range(8):
                b, ps, tok = unit(name, XHL[0][:nk], XHL[1][:nk], otok)
                xw[m] = stt(X[:, m, :], X[:, m, :], ALPHA, ps, ALU.mult, ALU.add, tok, xw[m])
                bfree[b] = xw[m]
                stat(X[:, m, :], m, xw[m], True)

        def mlp(l, xt):
            hfree = {}
            rfree = {}
            for q in range(4):
                ht = []
                o = 16 * (q % 2)
                for m in range(8):
                    b, ps, tok = unit(f"w1_{l}", *XHL, xt)
                    r, h = TM[:, 2 + m % 2, :], TM[:, 4 + m % 2, :]
                    hh, hl = H[:, o + m, :], H[:, o + 8 + m, :]
                    a = act(r, ps, ACT.Relu, tok, rfree.get(m % 2))
                    c = stt(h, ps, 0.0, r, ALU.max, ALU.mult, a, rfree.get(("h", m % 2)))
                    bfree[b] = c
                    d = act(hh, h, ACT.Copy, c, hfree.get(q - 2))
                    e = tt(hl, h, f32(hh), ALU.subtract, d, hfree.get(q - 2))
                    rfree[m % 2] = c
                    rfree[("h", m % 2)] = [e, d]
                    ht.append(e)
                hl_ = [H[:, o + k, :] for k in range(8)], [H[:, o + 8 + k, :] for k in range(8)]
                for m in range(8):
                    b, ps, tok = unit(f"w2_{l}", *hl_, ht)
                    if q == 0:
                        xw[m] = stt(X[:, m, :], X[:, m, :], ALPHA, ps, ALU.mult, ALU.add, tok, xw[m])
                    else:
                        xw[m] = tt(X[:, m, :], X[:, m, :], ps, ALU.add, tok, xw[m])
                    bfree[b] = xw[m]
                    if q == 3:
                        stat(X[:, m, :], m, xw[m], True)
                hfree[q] = tok

        def ffn(l, xt):
            hfree, rfree = {}, {}
            yt = [None] * 8
            i = 0
            for q, n in enumerate((8, 8, 6)):
                ht = []
                o = 16 * (q % 2)
                for m in range(n):
                    g, v = TM[:, 2 + 2 * (i % 2), :], TM[:, 3 + 2 * (i % 2), :]
                    c = []
                    for s, dst in ((0, g), (1, v)):
                        blk = 22 * s + q * 8 + m
                        b, ps, tok = unit(f"up_{l}", *XHL, xt)
                        w = lambda j, blk=blk: vec("fcw", 132 * l + 3 * blk + j)
                        a = conv_psum(dst, ps, w, 3, vec("fcb", 44 * l + blk), tok, rfree.get(i % 2))
                        bfree[b] = a
                        c.append(a)
                    hh, hl = H[:, o + m, :], H[:, o + 8 + m, :]
                    a = act(g, g, ACT.Gelu_apprx_tanh, c[0])
                    a = tt(g, g, v, ALU.mult, a, c[1], e="pool")
                    d = act(hh, g, ACT.Copy, a, hfree.get(q - 2))
                    e = tt(hl, g, f32(hh), ALU.subtract, d, hfree.get(q - 2))
                    rfree[i % 2] = e
                    ht.append(e)
                    i += 1
                hl_ = [H[:, o + k, :] for k in range(n)], [H[:, o + 8 + k, :] for k in range(n)]
                for m in range(8):
                    b, ps, tok = unit(f"dn{n}_{l}", *hl_, ht)
                    if q == 0:
                        yt[m] = act(Y[:, m, :], ps, ACT.Copy, tok)
                    else:
                        yt[m] = tt(Y[:, m, :], Y[:, m, :], ps, ALU.add, tok, yt[m])
                    bfree[b] = yt[m]
                    if q == 2:
                        stat(Y[:, m, :], m, yt[m], False)
                hfree[q] = tok
            return yt

        def hybrid(xt):
            sl = lambda i: AR[:, i, :]
            QKV = [sl(i) for i in range(12)]
            Z = [sl(12 + i) for i in range(4)]
            QA = [sl(16 + i) for i in range(4)]
            KA, VA = sl(20), sl(21)
            GR = sl(22)
            BR = sl(23)
            c0 = lambda name, lo=0, hi=128: c_of(Yf, at0, name, lo, hi)
            cw = p.waits("pe", t_c0), p.waits("dve", t_c0), p.waits("pool", t_c0)
            for e, w in zip(("pe", "dve", "pool"), cw):
                p.q[e].append((w, None, None))
            b, ps, tok = unit("hyb", *XHL, xt)
            tb = act(BR[0:4, :], ps[0:4, :], ACT.Sigmoid, tok)
            r = [sl(24 + i)[32:36, :] for i in range(5)]
            ta = act(r[0], ps[32:36, :], ACT.Identity, tok, bias=vec("dtb", 0, 1, 32, 36))
            bfree[b] = [ta, tb]
            sp = softplus_rows(r[0], r[0], r[1:5], ta)
            ea = act(COL[32:36, 200:201], vec("alog", 0, 1, 32, 36), ACT.Exp)
            g = ts(r[0], r[0], COL[32:36, 200:201], ALU.mult, sp, ea, s2=-1.0, op1=ALU.mult)
            gt = []
            for c in range(4):
                gs = slice(128 * c, 128 * c + 128)
                gt.append(scan(GR[32:36, gs], ones[32:36, :], r[0][:, gs], g))
            qkvt = []
            for i in range(12):
                b, ps, tok = unit("hyb", *XHL, xt)
                w = lambda j, i=i: vec("hcw", 4 * i + j)
                a = conv_psum(QKV[i], ps, w, 4, 0.0, tok)
                bfree[b] = a
                qkvt.append(act(QKV[i], QKV[i], ACT.Silu, a))
            zt = []
            for i in range(4):
                b, ps, tok = unit("hyb", *XHL, xt)
                zt.append(act(Z[i], ps, ACT.Silu, tok))
                bfree[b] = zt[-1]
            free = {}
            for i in range(8):
                sq, rs = TM[:, 2 + i % 2, :], TM[:, 4 + i % 2, :]
                a = act(sq, QKV[i], ACT.Square, qkvt[i], free.get(("s", i % 2)))
                b = next_bank()
                t = mm(PS[b][:, :], ones, sq, True, True, a, bfree.get(b), inc=True)
                free[("s", i % 2)] = t
                rr = rstd_of(rs, PS[b][:, :], 1.0, EPS6, t, free.get(("r", i % 2)))
                bfree[b] = rr
                if i < 4:
                    qkvt[i] = stt(QKV[i], QKV[i], 128 ** -0.5, rs, ALU.mult, ALU.mult, rr)
                else:
                    qkvt[i] = tt(QKV[i], QKV[i], rs, ALU.mult, rr)
                free[("r", i % 2)] = qkvt[i]
            rt = []
            for i in range(5):
                b, ps, tok = unit("hyb", *XHL, xt)
                rt.append(rope(QA[i] if i < 4 else KA, ps, tok, cst["rot1"], c0("cos"), c0("sin"),
                               TM[:, 6 + i % 2, :], rt[i - 2] if i > 1 else None, b))
            b, ps, tok = unit_tok("hyb", xt, False)
            tv = act(VA, ps, ACT.Copy, tok)
            bfree[b] = tv
            p.fence()
            jobs = []
            otok = [None] * 8

            def out_of(j):
                def then(t):
                    otok[j] = split(XH[:, j, :], XL[:, j, :], PS[j][:, :], t)
                return then

            for j in range(4):
                for hp in range(2):
                    h = 4 * hp + j
                    lo = 64 * hp
                    for n in range(4):
                        k0 = max(n - 1, 0)
                        job = dict(q=QA[j][lo:lo + 64, 128 * n:128 * n + 128], k=KA[lo:lo + 64, 128 * k0:128 * n + 128],
                                   nk=128 * (n + 1 - k0), v=[VA[:, 128 * c + lo:128 * c + lo + 64] for c in range(k0, n + 1)],
                                   out=PS[j][lo:lo + 64, 128 * n:128 * n + 128], sink=vec("sink", h),
                                   mask=c0("slide")[:, 256 - 128 * (n + 1 - k0):256])
                        jobs.append(job)
                jobs[-1]["then"] = out_of(j)
            attention(jobs, 64 ** -0.5)
            p.fence()
            gcol = COL[:, 32:48].rearrange("p (c h) -> p c h", c=4)
            bcol = COL[:, 48:64].rearrange("p (c h) -> p c h", c=4)
            bg = COL[:, 64:80].rearrange("p (c h) -> p c h", c=4)
            for c in range(4):
                gs = slice(128 * c, 128 * c + 128)
                mm(PS[0][:, 4 * c:4 * c + 4], GR[32:36, gs], ident[32:36, 32:36], True, True)
                t = mm(PS[1][:, 4 * c:4 * c + 4], BR[0:4, gs], ident[0:4, 0:4], True, True, inc=True)
            a = copy(COL[:, 32:48], PS[0][:, 0:16], t)
            b = copy(COL[:, 48:64], PS[1][:, 0:16], t)
            e = act(COL[:, 64:80], COL[:, 32:48], ACT.Exp, a)
            e = tt(COL[:, 64:80], COL[:, 64:80], COL[:, 48:64], ALU.mult, e, b)
            p.fence()
            I = ident
            for pair in range(2):
                hs = (2 * pair, 2 * pair + 1)
                W = {h: [sl(16 + 8 * x + i) for i in range(6)] for x, h in enumerate(hs)}
                gl = {h: COL[:, 80 + 8 * x:84 + 8 * x] for x, h in enumerate(hs)}
                kt_ = {h: COL[:, 100 + 8 * x:104 + 8 * x] for x, h in enumerate(hs)}
                tk = {}
                for x, h in enumerate(hs):
                    Q, KT = QKV[h], QKV[4 + h]
                    a_, b_, c_, d_, e_, f_ = W[h]
                    pb = 4 * x
                    gb, bb = PS[pb][:, :], PS[pb + 1][:, :]
                    t1 = mm(gb, c0("sel", 32, 36)[:, 128 * h:128 * h + 128], GR[32:36, :], True, True, inc=True)
                    t2 = mm(bb, c0("sel", 0, 4)[:, 128 * h:128 * h + 128], BR[0:4, :], True, True, inc=True)
                    kb = tt(a_, KT, bb, ALU.mult, t2)
                    last = None
                    for c in range(4):
                        gs = slice(128 * c, 128 * c + 128)
                        last = ts(b_[:, gs], gb[:, gs], gcol[:, c, h:h + 1], ALU.subtract, t1, s2=0.0, op1=ALU.min)
                    dc = act(b_, b_, ACT.Exp, last)
                    m1 = tt(b_.rearrange("p (c i) -> p c i", c=4), b_.rearrange("p (c i) -> p c i", c=4),
                            c0("mi")[:, None, :].broadcast_to([128, 4, 128]), ALU.mult, dc)
                    g1 = tt(kt_[h], gb[:, 127:T:128], gcol[:, :, h], ALU.subtract, t1)
                    g1 = act(kt_[h], kt_[h], ACT.Exp, g1)
                    g2 = act(gl[h], gb[:, 127:T:128], ACT.Exp, t1)
                    eg = act(c_, gb, ACT.Exp, t1)
                    for c in range(4):
                        gs = slice(128 * c, 128 * c + 128)
                        mm(PS[pb + 2][:, gs], KT[:, gs], a_[:, gs], True, True, kb)
                        t3 = mm(PS[pb + 3][:, gs], KT[:, gs], Q[:, gs], True, True, inc=True)
                    qk = tt(d_, PS[pb + 3][:, :], b_, ALU.mult, m1, t3)
                    qg = tt(Q, Q, c_, ALU.mult, eg, t3, e="pool")
                    m2 = tt(b_.rearrange("p (c i) -> p c i", c=4), b_.rearrange("p (c i) -> p c i", c=4),
                            c0("ms")[:, None, :].broadcast_to([128, 4, 128]), ALU.mult, qk)
                    at = tt(c_, PS[pb + 2][:, :], b_, ALU.mult, m2, t3, qg)
                    tk[h] = dict(at=at, qk=qk, qg=qg, g1=g1, g2=g2, kb=kb)
                    mo = tt(b_.rearrange("p (c i) -> p c i", c=4), c_.rearrange("p (c i) -> p c i", c=4),
                            c0("lv")[:, 0:128][:, None, :].broadcast_to([128, 4, 128]), ALU.mult, at)
                    tT = tt(f_.rearrange("p (c i) -> p c i", c=4), I[:, None, :].broadcast_to([128, 4, 128]),
                            b_.rearrange("p (c i) -> p c i", c=4), ALU.subtract, mo)
                    for c in range(4):
                        gs = slice(128 * c, 128 * c + 128)
                        t4 = tr(PS[pb][:, gs], f_[:, gs], I, tT, eg, g2, g1, last, inc=c == 3)
                    tk[h]["T"] = act(e_, PS[pb][:, :], ACT.Copy, t4)
                    tk[h]["TT"] = tT
                    tk[h]["free"] = t4
                for lv in range(1, 7):
                    for x, h in enumerate(hs):
                        a_, b_, c_, d_, e_, f_ = W[h]
                        k = tk[h]
                        pb = 4 * x
                        ao = tt(b_.rearrange("p (c i) -> p c i", c=4), c_.rearrange("p (c i) -> p c i", c=4),
                                c0("lv")[:, 128 * lv:128 * lv + 128][:, None, :].broadcast_to([128, 4, 128]),
                                ALU.mult, k["at"], k["free"], e="pool")
                        for c in range(4):
                            gs = slice(128 * c, 128 * c + 128)
                            t1 = mm(PS[pb + 1][:, gs], b_[:, gs], e_[:, gs], True, True, ao, k["T"], inc=c == 3)
                        y = act(a_, PS[pb + 1][:, :], ACT.Copy, t1, k["kb"])
                        for c in range(4):
                            gs = slice(128 * c, 128 * c + 128)
                            t2 = mm(PS[pb + 2][:, gs], a_[:, gs], f_[:, gs], True, True, y, k["TT"], inc=c == 3)
                        if lv < 6:
                            for c in range(4):
                                gs = slice(128 * c, 128 * c + 128)
                                t3 = mm(PS[pb + 3][:, gs], f_[:, gs], a_[:, gs], True, True, k["qk"], inc=c == 3)
                            k["T"] = tt(e_, e_, PS[pb + 3][:, :], ALU.subtract, t3, k["T"])
                        else:
                            t3 = t2
                        k["TT"] = tt(f_, f_, PS[pb + 2][:, :], ALU.subtract, t2, t3, k["TT"])
                        k["free"] = [t2, t3]
                        k["y"] = y
                p.fence()
                for x, h in enumerate(hs):
                    a_, b_, c_, d_, e_, f_ = W[h]
                    k = tk[h]
                    pb = 4 * x
                    for c in range(4):
                        gs = slice(128 * c, 128 * c + 128)
                        t1 = tr(PS[pb][:, gs], QKV[4 + h][:, gs], I, inc=c == 3)
                    for c in range(4):
                        gs = slice(128 * c, 128 * c + 128)
                        t2 = tr(PS[pb + 1][:, gs], QKV[8 + h][:, gs], I, inc=c == 3)
                    s1, s2 = [], []
                    for c in range(4):
                        gs = slice(128 * c, 128 * c + 128)
                        s1.append(ts(a_[:, gs], PS[pb][:, gs], bg[:, c, h:h + 1], ALU.mult, t1))
                        s2.append(act(b_[:, gs], PS[pb + 1][:, gs], ACT.Copy, t2, scale=bcol[:, c, h:h + 1]))
                    for c in range(4):
                        gs = slice(128 * c, 128 * c + 128)
                        t3 = mm(PS[pb + 2][:, gs], a_[:, gs], f_[:, gs], True, True, s1[c], inc=c == 3)
                    nw = ts(c_, PS[pb + 2][:, :], -1.0, ALU.mult, t3)
                    kt = []
                    for c in range(4):
                        gs = slice(128 * c, 128 * c + 128)
                        kt.append(ts(a_[:, gs], PS[pb][:, gs], kt_[h][:, c:c + 1], ALU.mult, t3, k["g1"]))
                    k.update(nw=nw, kt=kt, vb=s2)
                p.fence()
                S = {h: [W[h][4][:, 0:128], W[h][4][:, 128:256]] for h in hs}
                VN = {h: [W[h][4][:, 256:384], W[h][4][:, 384:512]] for h in hs}
                for c in range(4):
                    gs = slice(128 * c, 128 * c + 128)
                    for x, h in enumerate(hs):
                        a_, b_, c_, d_, e_, f_ = W[h]
                        k = tk[h]
                        pb = 4 * x
                        so, sn = S[h][c % 2], S[h][(c + 1) % 2]
                        vn = VN[h][c % 2]
                        t1 = mm(PS[pb][:, 0:128], f_[:, gs], b_[:, gs], True, c == 0, k.get("vfree"), inc=c == 0)
                        if c:
                            t1 = mm(PS[pb][:, 0:128], c_[:, gs], so, False, True, k["S"], inc=True)
                        v = act(vn, PS[pb][:, 0:128], ACT.Copy, t1)
                        k["vfree"] = v
                        if c:
                            mm(PS[pb + 2][:, gs], so, QKV[h][:, gs], True, False)
                        t2 = mm(PS[pb + 2][:, gs], vn, d_[:, gs], c == 0, True, v, inc=True)
                        if c < 3:
                            t3 = mm(PS[pb + 1][:, 0:128], a_[:, gs], vn, True, True, k.get("S"), inc=True)
                            if c == 0:
                                k["S"] = copy(sn, PS[pb + 1][:, 0:128], t3)
                            else:
                                k["S"] = stt(sn, so, gl[h][:, c:c + 1], PS[pb + 1][:, 0:128], ALU.mult, ALU.add, t3, k["S"])
                        k["o"] = t2
                for x, h in enumerate(hs):
                    k = tk[h]
                    a_, b_, c_ = W[h][:3]
                    pb = 4 * x
                    o = PS[pb + 2][:, :]
                    a = act(a_, o, ACT.Square, k["o"])
                    t = mm(PS[pb + 3][:, :], ones, a_, True, True, a, inc=True)
                    r = rstd_of(b_, PS[pb + 3][:, :], 1.0 / 128, EPS6, t)
                    y = stt(c_, o, vec("hnw"), b_, ALU.mult, ALU.mult, r)
                    y = tt(c_, c_, Z[h], ALU.mult, y, e="pool")
                    otok[4 + h] = split(XH[:, 4 + h, :], XL[:, 4 + h, :], c_, y)
                p.fence()
            bfree.clear()
            return otok

        def recurrent(xt):
            sl = lambda i: AR[:, i, :]
            XR, GA = [sl(i) for i in range(8)], [sl(8 + i) for i in range(8)]
            A_, B_ = [sl(16 + i) for i in range(8)], [sl(24 + i) for i in range(8)]
            nl = COL[:, 0:8]
            a = ts(COL[:, 8:16], vec("lam", 0, 8), -1.0, ALU.mult)
            a = softplus_rows(nl, COL[:, 8:16], [COL[:, 16 + 8 * i:24 + 8 * i] for i in range(4)], a)
            nlt = ts(nl, nl, -8.0, ALU.mult, a)
            p8 = COL[:, 48:56]
            nlt = ts(p8, nl, -1.0, ALU.mult, nlt)
            xrt, gat = [], []
            for m in range(8):
                b, ps, tok = unit("rin", *XHL, xt)
                w = lambda j, m=m: vec("rcw", 4 * m + j)
                xrt.append(conv_psum(XR[m], ps, w, 4, vec("rcb", m), tok))
                bfree[b] = xrt[-1]
            for m in range(8):
                b, ps, tok = unit("rin", *XHL, xt)
                gat.append(act(GA[m], ps, ACT.Gelu_apprx_tanh, tok))
                bfree[b] = gat[-1]
            pe = p.now("pe")
            xs = [split(XH[:, m, :], XL[:, m, :], XR[m], xrt[m], pe) for m in range(8)]
            for which in range(2):
                for half in range(2):
                    u = next_unit("rwg")
                    s = u % NW
                    for mo in range(4):
                        m = 4 * half + mo
                        blk = m // 2
                        b = next_bank()
                        for k in range(2):
                            kk = 2 * blk + k
                            c = 128 * (2 * mo + k)
                            wh, wl = WH[:, s, c:c + 128], WL[:, s, c:c + 128]
                            mm(PS[b][:, :], wh, XH[:, kk, :], k == 0, False, wtok[u], bfree.get(b), xs[kk])
                            mm(PS[b][:, :], wh, XL[:, kk, :], False, False)
                            tok = mm(PS[b][:, :], wl, XH[:, kk, :], False, k == 1, inc=k == 1)
                        dst = (A_ if which == 0 else B_)[m]
                        t = act(dst, PS[b][:, :], ACT.Sigmoid, tok, bias=vec("rba" if which == 0 else "rbx", m))
                        bfree[b] = t
                        if which == 0:
                            xs[m] = [xs[m], t]
                        else:
                            xrt[m] = tt(XR[m], XR[m], dst, ALU.mult, t, xs[m], e="pool")
                    wfree[s] = tok
            at, bt = [], []
            for m in range(8):
                t = act(B_[m], A_[m], ACT.Tanh, nlt, xrt[m], xs[m], scale=p8[:, m:m + 1])
                a = act(A_[m], A_[m], ACT.Exp, t, nlt, scale=nl[:, m:m + 1])
                q = TM[:, 2 + m % 2, :]
                c = tt(q, A_[m], A_[m], ALU.mult, a, bt[m - 2] if m > 1 else None)
                bt.append(stt(B_[m], q, 1.0, B_[m], ALU.add, ALU.mult, c, t))
                at.append(a)
            pe = p.now("pe")
            otok = []
            for m in range(8):
                a = act(B_[m], B_[m], ACT.Sqrt, bt[m])
                a = tt(B_[m], B_[m], XR[m], ALU.mult, a, xrt[m], e="pool")
                a = scan(XR[m], A_[m], B_[m], a, at[m])
                a = tt(XR[m], XR[m], GA[m], ALU.mult, a, gat[m])
                otok.append(split(XH[:, m, :], XL[:, m, :], XR[m], a, pe))
            return otok

        at2, n2 = places(C2)
        at3, n3 = places(C3)

        def dilated(xt):
            sl = lambda i: AR[:, i, :]
            QA, KA = [sl(i) for i in range(6)], [sl(6 + i) for i in range(6)]
            VA = [sl(12 + i) for i in range(6)]
            c2 = lambda name, lo=0, hi=128: c_of(ARf[:, 18 * T:], at2, name, lo, hi)
            j = p.fence()
            p.fence(p.dma("pool", ARf[:, 18 * T:18 * T + n2], D["c2"], j))
            rt = []
            for i in range(12):
                b, ps, tok = unit("qkv", *XHL, xt)
                rt.append(rope(QA[i] if i < 6 else KA[i - 6], ps, tok, cst["rot2"], c2("cos"), c2("sin"),
                               TM[:, 6 + i % 2, :], rt[i - 2] if i > 1 else None, b))
            for i in range(6):
                b, ps, tok = unit_tok("qkv", xt, i >= 2)
                bfree[b] = act(VA[i], ps, ACT.Copy, tok)
            p.fence()
            LC = COL[:, 32:80]
            MC = COL[:, 80:128]
            jobs = []
            OB = [sl(25 + i) for i in range(6)]
            ot = [None] * 6

            def out_of(jb):
                def then(t):
                    ot[jb] = act(OB[jb], PS[jb % 2][:, :], ACT.Copy, t)
                    for job in jobs:
                        if job["jb"] == jb + 2:
                            job["outfree"] = ot[jb]
                return then

            for jb in range(6):
                g = jb // 2
                for hp in range(2):
                    h = 2 * jb + hp
                    lo = 64 * hp
                    for n in range(4):
                        if g == 0:
                            k0 = max(n - 1, 0)
                            q = QA[jb][lo:lo + 64, 128 * n:128 * n + 128]
                            k = KA[jb][lo:lo + 64, 128 * k0:128 * n + 128]
                            nk = 128 * (n + 1 - k0)
                            v = [VA[jb][:, 128 * c + lo:128 * c + lo + 64] for c in range(k0, n + 1)]
                            mask = c2("dil1")[:, 256 - nk:256]
                            out = PS[jb % 2][lo:lo + 64, 128 * n:128 * n + 128]
                        else:
                            q = QA[jb][lo:lo + 64, n:T:4]
                            k = KA[jb][lo:lo + 64, n:T:4]
                            nk = 128
                            v = [VA[jb][:, 128 * n + lo:128 * n + lo + 64]]
                            mask = c2("causal")[:, 384:512] if g == 1 else c2("dil3")
                            out = PS[jb % 2][lo:lo + 64, n:T:4]
                        ci = 16 * g + 4 * n + h % 4
                        jobs.append(dict(q=q, k=k, nk=nk, v=v, mask=mask, out=out, jb=jb,
                                         lout=LC[:, ci:ci + 1], mout=MC[:, ci:ci + 1]))
                jobs[-1]["then"] = out_of(jb)
            attention(jobs, 64 ** -0.5, lse=True)
            p.fence()
            a = act(LC, LC, ACT.Ln)
            a = tt(LC, LC, MC, ALU.add, a)
            Lg = [TM[0:4, i, :] for i in range(3)]
            toks = []
            for g in range(3):
                for n in range(4):
                    ci = 16 * g + 4 * n
                    t = tr(PS[2 + g][0:4, 128 * n:128 * n + 128], LC[:, ci:ci + 4], ident, a, inc=n == 3)
                if g == 0:
                    toks.append(copy(Lg[0], PS[2][0:4, :], t))
                else:
                    toks.append(copy(Lg[g].rearrange("p (i r) -> p r i", r=4),
                                     PS[2 + g][0:4, :].rearrange("p (r i) -> p r i", r=4), t))
            mx, sm = TM[0:4, 3, :], TM[0:4, 4, :]
            a = tt(mx, Lg[0], Lg[1], ALU.max, toks)
            a = tt(mx, mx, Lg[2], ALU.max, a)
            et = []
            for g in range(3):
                b = tt(Lg[g], Lg[g], mx, ALU.subtract, a)
                et.append(act(Lg[g], Lg[g], ACT.Exp, b))
            a = tt(sm, Lg[0], Lg[1], ALU.add, et)
            a = tt(sm, sm, Lg[2], ALU.add, a)
            a = recip(sm, sm, a)
            et = [tt(Lg[g], Lg[g], sm, ALU.mult, a) for g in range(3)]
            otok = []
            p.fence()
            for jb in range(6):
                g = jb // 2
                s = c2("sel2", 0, 4)[:, 128 * (jb % 2):128 * (jb % 2) + 128]
                b = PS[jb % 2]
                t = mm(b[:, :], s, Lg[g], True, True, et[g], otok[jb - 2] if jb > 1 else None, inc=True)
                a = tt(OB[jb], OB[jb], b[:, :], ALU.mult, t)
                otok.append(split(XH[:, jb, :], XL[:, jb, :], OB[jb], a))
            p.fence()
            bfree.clear()
            return otok

        def fox(xt, r):
            sl = lambda i: AR[:, i, :]
            QA, KA = [sl(i) for i in range(8)], [sl(8 + i) for i in range(8)]
            VA = [sl(16 + i) for i in range(8)]
            c3 = lambda name, lo=0, hi=128: c_of(ARf[:, 24 * T:], at3, name, lo, hi)
            j = p.fence()
            p.fence(p.dma("pool", ARf[:, 24 * T:24 * T + n3], D["c3"], j))
            RS = TM[:, 2, :]
            for i in range(8):
                b, ps, tok = unit("kvf", *XHL, xt)
                bfree[b] = act(KA[i], ps, ACT.Copy, tok)
            for i in range(8):
                b, ps, tok = unit_tok("kvf", xt, False)
                bfree[b] = act(VA[i], ps, ACT.Copy, tok)
            b, ps, tok = unit("kvf", *XHL, xt)
            CR = Y[0:16, 0, :]
            rr = [Y[0:16, 1 + i, :] for i in range(5)]
            a = act(rr[0], ps[0:16, :], ACT.Identity, tok, bias=vec("bf", 0, 1, 0, 16))
            bfree[b] = a
            a = ts(rr[0], rr[0], -1.0, ALU.mult, a)
            a = softplus_rows(rr[0], rr[0], rr[1:5], a)
            a = ts(rr[0], rr[0], -1.0, ALU.mult, a)
            one = fill(rr[1], 1.0, a)
            ct = scan(CR, rr[1], rr[0], a, one)
            xq = rms_apply(X, r, "ng", 32, xw)
            for i in range(8):
                b, ps, tok = unit("wqb", *XHL, xq)
                bfree[b] = act(QA[i], ps, ACT.Copy, tok, scale=0.125)
            p.fence()
            CC = COL[:, 32:96]
            for n in range(4):
                t = mm(PS[0][:, 16 * n:16 * n + 16], CR[:, 128 * n:128 * n + 128], ident[0:16, 0:16], True, True, ct, inc=n == 3)
            a = copy(CC, PS[0][:, 0:64], t)
            p.fence()
            jobs = []
            otok = [None] * 8

            def out_of(jb):
                def then(t):
                    otok[jb] = split(XH[:, jb, :], XL[:, jb, :], PS[jb % 4][:, :], t)
                    for job in jobs:
                        if job["jb"] == jb + 4:
                            job["outfree"] = otok[jb]
                return then

            for jb in range(8):
                for hp in range(2):
                    h = 2 * jb + hp
                    lo = 64 * hp
                    for n in range(4):
                        nk = 128 * (n + 1)
                        jobs.append(dict(
                            q=QA[jb][lo:lo + 64, 128 * n:128 * n + 128], k=KA[jb][lo:lo + 64, 0:nk], nk=nk,
                            more=(c3("seln", 0, 16)[:, 128 * h:128 * h + 128], CR[:, 0:nk]),
                            cq=CC[:, 16 * n + h:16 * n + h + 1], mask=c3("causal")[:, 512 - nk:512],
                            v=[VA[jb][:, 128 * c + lo:128 * c + lo + 64] for c in range(n + 1)],
                            out=PS[jb % 4][lo:lo + 64, 128 * n:128 * n + 128], jb=jb))
                jobs[-1]["then"] = out_of(jb)
            attention(jobs, 1.0)
            p.fence()
            bfree.clear()
            return otok

        def mix_y(name, nk, otok):
            yt = []
            for m in range(8):
                b, ps, tok = unit(name, XHL[0][:nk], XHL[1][:nk], otok)
                yt.append(act(Y[:, m, :], ps, ACT.Copy, tok))
                bfree[b] = yt[-1]
                stat(Y[:, m, :], m, yt[m], False)
            return yt

        def tail(yt, gi, eps):
            _, _, r, _ = stats_end(False, eps)
            rms_add(r, gi, yt)
            _, _, r, _ = stats_end(False, eps)
            return r

        ot = hybrid(xtok)
        mix_out("hwo", 8, ot)
        xt = layer_norm("ln1g", "ln1b", 0)
        p.fence()
        mlp(0, xt)
        xt = layer_norm("ln2g", "ln2b", 0)
        p.fence()
        ot = recurrent(xt)
        p.fence()
        mix_out("rwo", 8, ot)
        xt = layer_norm("ln1g", "ln1b", 1)
        p.fence()
        mlp(1, xt)
        layer_norm("ln2g", "ln2b", 1)
        p.fence()
        for m in range(8):
            stat(X[:, m, :], m, xw[m], False)
        _, _, r, _ = stats_end(False, EPS6)
        for l in range(2):
            if l == 0:
                xt = rms_apply(X, r, "ng", 0, xw)
                ot = dilated(xt)
                yt = mix_y("woa", 6, ot)
            else:
                xt = rms_apply(X, r, "kvn", 0, xw)
                ot = fox(xt, r)
                yt = mix_y("wob", 8, ot)
            r = tail(yt, 32 * l + 8, EPS6)
            xt = rms_apply(X, r, "ng", 32 * l + 16, xw)
            p.fence()
            yt = ffn(l, xt)
            _, _, r, _ = stats_end(False, EPS6)
            rms_add(r, 32 * l + 24, yt, l == 0)
            if l == 0:
                _, _, r, _ = stats_end(False, EPS6)
            p.fence()
        j = p.fence()
        t = p.dma("sp", D["out"].rearrange("(k p) t -> p k t", p=128), X[:, :, :], xw, j)
        for s in p.dlast.values():
            w = p.waits("sp", s)
            p.q["sp"].append((w, None, None))

        block = ctx.enter_context(nc.Block())

        @block.sync
        def _(eng):
            p.play("sp", eng)

        @block.tensor
        def _(eng):
            p.play("pe", eng)

        @block.scalar
        def _(eng):
            p.play("act", eng)

        @block.vector
        def _(eng):
            p.play("dve", eng)

        @block.gpsimd
        def _(eng):
            p.play("pool", eng)


def shape_constants():
    f = np.float32
    idx = np.arange(128)
    small = np.zeros((5, 128, 128), f)
    small[0] = np.eye(128)
    small[1] = 1.0 / 1024
    small[2] = 1.0
    for i in range(128):
        j = i % 64
        if j < 32:
            small[3, i + 32, i] = -1
        else:
            small[3, i - 32, i] = 1
        if j < 8:
            small[4, i + 8, i] = -1
        elif j < 16:
            small[4, i - 8, i] = 1
    small = small.transpose(1, 0, 2).reshape(128, -1)

    def tables(half, theta):
        inv = (f(theta) ** (-np.arange(half, dtype=f) / f(half))).astype(f)
        ang = (np.arange(T, dtype=f)[:, None] * inv[None, :]).astype(f)
        cos, sin = np.ones((64, T), f), np.zeros((64, T), f)
        for k in range(2 * half):
            cos[k] = np.cos(ang[:, k % half])
            sin[k] = np.sin(ang[:, k % half])
        return np.tile(cos, (2, 1)), np.tile(sin, (2, 1))

    NEG = -1e30
    q, k = idx[:, None], idx[None, :]
    k2 = np.arange(256)[None, :]
    dist = q + 128 - k2
    slide = np.where((dist >= 0) & (dist < 128), 0, NEG).astype(f)
    dil1 = np.where((dist >= 0) & (dist <= 128), 0, NEG).astype(f)
    causal = np.zeros((128, 512), f)
    causal[:, 384:] = np.where(k <= q, 0, NEG)
    dil3 = np.where((k <= q) & ((q - k) % 4 == 0), 0, NEG).astype(f)
    j, i = q, k
    mi = (i >= j).astype(f)
    ms = (i > j).astype(f)
    lv = []
    for l in range(7):
        b = 1 << l
        lv.append(((i // (2 * b) == j // (2 * b)) & (i // b % 2 == 1) & (j // b % 2 == 0)).astype(f))
    lv = np.concatenate(lv, 1)
    sel = np.zeros((128, 4, 128), f)
    sel2 = np.zeros((128, 2, 128), f)
    for h in range(4):
        sel[h, h, :] = 1
        sel[32 + h, h, :] = 1
        sel2[h, h // 2, 64 * (h % 2):64 * (h % 2) + 64] = 1
    seln = np.zeros((128, 16, 128), f)
    for h in range(16):
        seln[h, h, :] = -1
    cos, sin = tables(32, 10000.0)
    c0 = dict(cos=cos, sin=sin, mi=mi, ms=ms, lv=lv, sel=sel.reshape(128, -1), slide=slide)
    cos, sin = tables(8, 500000.0)
    c2 = dict(cos=cos, sin=sin, dil1=dil1, causal=causal, dil3=dil3, sel2=sel2.reshape(128, -1))
    c3 = dict(causal=causal, seln=seln.reshape(128, -1))
    return small, *(np.ascontiguousarray(np.concatenate([c[n] for n, _ in parts], 1), dtype=f)
                    for c, parts in ((c0, C0), (c2, C2), (c3, C3)))


def kernel(**inputs):
    import numpy as _np
    import concourse.bacc as _bacc
    from concourse import mybir as _mybir
    from concourse.bass_utils import run_bass_kernel_spmd as _run

    I = {k: _np.asarray(v) for k, v in inputs.items()}
    f = _np.float32

    def units(w, kb=8):
        K, N = w.shape
        a = w.reshape(K // (128 * kb), kb, 128, N // 128, 128).transpose(0, 3, 2, 1, 4)
        return _np.ascontiguousarray(a).reshape(-1, 128, kb * 128)

    def pad(w, n):
        out = _np.zeros((w.shape[0], n), w.dtype)
        out[:, :w.shape[1]] = w
        return out

    A = {}
    A["x"] = _np.ascontiguousarray(I["x"][0].T)
    w = I["hyb_w_in"][0]
    qa, ka, va, qkv, z, be, al = _np.split(w, [512, 640, 768, 2304, 2816, 2820], axis=1)
    small = _np.zeros((1024, 128), w.dtype)
    small[:, 0:4] = be
    small[:, 32:36] = al
    order = [h for j in range(4) for h in (j, 4 + j)]
    qa = qa.reshape(1024, 8, 64)[:, order].reshape(1024, 512)
    A["hyb"] = units(_np.concatenate([small, qkv, z, qa, ka, va], axis=1))
    w = I["hyb_w_out"][0]
    wa = w[:512].reshape(8, 64, 1024)[order].reshape(512, 1024)
    A["hwo"] = units(_np.concatenate([wa, w[512:]], axis=0))
    for l in range(2):
        A[f"w1_{l}"] = units(I["mlp_w1"][l])
        A[f"w2_{l}"] = units(I["mlp_w2"][l])
        up = I["w_up_2"][l].reshape(1024, 2, 22, 128).transpose(0, 2, 1, 3).reshape(1024, 5632)
        A[f"up_{l}"] = units(up)
        A[f"dn8_{l}"] = units(I["w_down_2"][l][:2048])
        A[f"dn6_{l}"] = units(I["w_down_2"][l][2048:], 6)
    A["rin"] = units(I["rec_w_in"][0])
    g = []
    for w in (I["rec_w_a"][0], I["rec_w_x"][0]):
        a = w.reshape(4, 2, 128, 2, 128).transpose(0, 3, 2, 1, 4).reshape(2, 4, 128, 256)
        g.append(a.transpose(0, 2, 1, 3).reshape(2, 128, 1024))
    A["rwg"] = _np.ascontiguousarray(_np.concatenate(g, 0))
    A["rwo"] = units(I["rec_w_out"][0])
    A["qkv"] = units(I["w_qkv_a_2"][0])
    A["woa"] = units(I["w_o_a_2"][0], 6)
    A["kvf"] = units(pad(I["w_kvf_2"], 2176))
    A["wqb"] = units(I["w_q_b_2"][0])
    A["wob"] = units(I["w_o_b_2"][0])

    def cols(v):
        return _np.ascontiguousarray(v.reshape(-1, 128).T)

    def taps(v):
        return v.reshape(v.shape[0], -1, 128).transpose(2, 1, 0).reshape(128, -1)

    def at(v, lo):
        out = _np.zeros((128, 1), f)
        out[lo:lo + v.shape[0], 0] = v
        return out

    V = dict(
        ln1g=cols(I["ln1_g"]), ln1b=cols(I["ln1_b"]), ln2g=cols(I["ln2_g"]), ln2b=cols(I["ln2_b"]),
        ng=cols(I["norm_gains_2"]), kvn=cols(I["kv_norm_2"]), hcw=taps(I["hyb_conv_w"][0]),
        hnw=cols(I["hyb_norm_w"]), sink=_np.repeat(I["hyb_sinks"][0][None], 128, 0),
        alog=at(I["hyb_a_log"][0], 32), dtb=at(I["hyb_dt_bias"][0], 32),
        rcw=taps(I["rec_conv_w"][0]), rcb=cols(I["rec_conv_b"]), rba=cols(I["rec_b_a"]),
        rbx=cols(I["rec_b_x"]), lam=cols(I["rec_lambda"]), bf=at(I["b_f_2"], 0),
        fcw=_np.concatenate([taps(I["conv_w_2"][l]) for l in range(2)], 1), fcb=cols(I["conv_b_2"]),
    )
    A["vec"] = _np.ascontiguousarray(_np.concatenate([V[n] for n, _ in VEC_SIZES], 1))
    A["small"], A["c0"], A["c2"], A["c3"] = shape_constants()

    nc = _bacc.Bacc("TRN2", target_bir_lowering=False, num_devices=1)
    D, arrays = {}, {}
    for name, a in A.items():
        arrays[f"in_{name}"] = a
        D[name] = nc.dram_tensor(f"in_{name}", a.shape, _mybir.dt.from_np(a.dtype), kind="ExternalInput").ap()
    D["out"] = nc.dram_tensor("out_x", (1024, T), F, kind="ExternalOutput").ap()
    build_program(nc, D)
    r = _run(nc, [arrays], core_ids=[0])
    return _np.ascontiguousarray(r.results[0]["out_x"].T)[None]
```

```python
import numpy as np
import concourse.bass as bass
from concourse import mybir
from contextlib import ExitStack

F = mybir.dt.float32
R = mybir.dt.float32r
ACT = mybir.ActivationFunctionType
ALU = mybir.AluOpType
AXX = mybir.AxisListType.X

T = 512
ALPHA = 4 ** 0.25

VEC_SIZES = [
    ("ln1g", 16), ("ln1b", 16), ("ln2g", 16), ("ln2b", 16), ("ng", 64), ("kvn", 8),
    ("hcw", 48), ("hnw", 1), ("sink", 8), ("alog", 1), ("dtb", 1),
    ("rcw", 32), ("rcb", 8), ("rba", 8), ("rbx", 8), ("lam", 8),
    ("bf", 1), ("fcw", 264), ("fcb", 88),
]
VEC_AT = {}
_n = 0
for _name, _k in VEC_SIZES:
    VEC_AT[_name] = _n
    _n += _k
NVEC = _n

SMALL = ["ident", "onesd", "ones", "rot1", "rot2"]
C0 = [("cos", 512), ("sin", 512), ("mi", 128), ("ms", 128), ("lv", 896), ("sel", 512), ("slide", 256)]
C2 = [("cos", 512), ("sin", 512), ("dil1", 256), ("causal", 512), ("dil3", 128), ("sel2", 256)]
C3 = [("causal", 512)]


def places(parts):
    at, out = 0, {}
    for name, k in parts:
        out[name] = (at, k)
        at += k
    return out, at


def plan_units():
    plan = [("hyb", i, 8) for i in range(23)] + [("hwo", i, 8) for i in range(8)]

    def mlp(l):
        out = []
        for q in range(4):
            out += [(f"w1_{l}", q * 8 + m, 8) for m in range(8)]
            out += [(f"w2_{l}", q * 8 + m, 8) for m in range(8)]
        return out

    def ffn(l):
        out = []
        for q, n in enumerate((8, 8, 6)):
            out += [(f"up_{l}", 2 * (q * 8 + i) + s, 8) for i in range(n) for s in range(2)]
            out += [(f"dn{n}_{l}", (q * 8 if n == 8 else 0) + m, n) for m in range(8)]
        return out

    plan += mlp(0)
    plan += [("rin", i, 8) for i in range(8)] + [("rwg", i, 8) for i in range(4)]
    plan += [("rin", i, 8) for i in range(8, 16)]
    plan += [("rwo", i, 8) for i in range(8)]
    plan += mlp(1)
    plan += [("qkv", i, 8) for i in range(18)] + [("woa", i, 6) for i in range(8)]
    plan += ffn(0)
    plan += [("kvf", i, 8) for i in range(17)] + [("wqb", i, 8) for i in range(8)]
    plan += [("wob", i, 8) for i in range(8)]
    plan += ffn(1)
    return plan


class Program:

    def __init__(self, sems, dsems):
        self.sems = sems
        self.dsems = dsems
        self.q = {e: [] for e in ("pe", "act", "dve", "pool", "sp")}
        self.count = {e: 0 for e in self.q}
        self.seen = {e: {} for e in self.q}
        self.ndma = {"sp": 0, "pool": 0}
        self.dlast = {}

    def waits(self, e, after):
        out = []
        for t in flat(after):
            if self.seen[e].get(t[0], 0) < t[1]:
                self.seen[e][t[0]] = t[1]
                out.append(t)
        return out

    def op(self, e, fn, *after, inc=True):
        w = self.waits(e, after)
        if inc:
            self.count[e] += 1
        self.q[e].append((w, fn, (e, 1) if inc else None))
        return (e, self.count[e]) if inc else None

    def dma(self, e, out, in_, *after):
        ring = self.dsems[e]
        s = ring[self.ndma[e] % len(ring)]
        self.ndma[e] += 1
        before = self.dlast.get(s)
        w = self.waits(e, [after, before or []])
        self.dlast[s] = (s, (before[1] if before else 0) + 16)
        self.q[e].append((w, lambda g: g.dma_start(out, in_), (s, 16)))
        return self.dlast[s]

    def now(self, *engines):
        return [(e, self.count[e]) for e in engines if self.count[e]]

    def fence(self, *also, engines=("pe", "act", "dve", "pool")):
        j = self.now("pe", "act", "dve", "pool") + list(flat(also))
        for e in engines:
            w = self.waits(e, j)
            if w:
                self.q[e].append((w, None, None))
        return j

    def play(self, e, eng):
        for w, fn, inc in self.q[e]:
            for s, v in w:
                eng.wait_ge(self.sems[s], v)
            if fn is None:
                continue
            ins = fn(eng)
            if inc is not None:
                ins.then_inc(self.sems[inc[0]], inc[1])


def flat(x):
    if x is None:
        return
    if isinstance(x, tuple) and len(x) == 2 and isinstance(x[0], str):
        yield x
        return
    for y in x:
        yield from flat(y)


def build_program(nc, D):
    with ExitStack() as ctx:
        def sb(name, shape, dt=F):
            return ctx.enter_context(nc.sbuf_tensor(name, shape, dt))

        names = ["pe", "act", "dve", "pool"] + [f"ds{i}" for i in range(12)] + [f"dp{i}" for i in range(6)]
        sems = {n: ctx.enter_context(nc.semaphore("s_" + n)) for n in names}
        p = Program(sems, {"sp": [f"ds{i}" for i in range(12)], "pool": [f"dp{i}" for i in range(6)]})

        NRAW, NW = 3, 4
        RAW = sb("RAW", [128, NRAW, 2, 1024])
        WH = sb("WH", [128, NW, 1024], R)
        WL = sb("WL", [128, NW, 1024], R)
        X = sb("X", [128, 8, T])
        XH = sb("XH", [128, 8, T], R)
        XL = sb("XL", [128, 8, T], R)
        Y = sb("Y", [128, 8, T])
        TM = sb("TM", [128, 8, T])
        VEC = sb("VEC", [128, NVEC])
        CST = sb("CST", [128, len(SMALL) * 128])
        COL = sb("COL", [128, 256])
        with nc.sbuf_tensor("H", [128, 32, T], R) as H:
            pass
        AR = sb("AR", [128, 32, T])
        PS = [ctx.enter_context(nc.psum_tensor(f"ps{i}", [128, T], F)) for i in range(8)]

        cst = {n: CST[:, 128 * i:128 * i + 128] for i, n in enumerate(SMALL)}
        ident, ones, onesd = cst["ident"], cst["ones"], cst["onesd"]

        def vec(name, i=0, n=1, lo=0, hi=128):
            a = VEC_AT[name] + i
            return VEC[lo:hi, a:a + n]

        def act(out, in_, func, *after, scale=1.0, bias=0.0, accum=None):
            def go(g):
                kw = {} if accum is None else {"accum_out": accum}
                return g.activation(out, in_, func, bias=bias, scale=scale, **kw)
            return p.op("act", go, *after)

        def tt(out, a, b, op, *after, e="dve"):
            return p.op(e, lambda g: g.tensor_tensor(out, a, b, op), *after)

        def ts(out, a, s1, op0, *after, s2=None, op1=ALU.bypass, e="dve"):
            return p.op(e, lambda g: g.tensor_scalar(out, a, s1, s2, op0, op1), *after)

        def stt(out, a, s, b, op0, op1, *after):
            return p.op("dve", lambda g: g.scalar_tensor_tensor(out, a, s, b, op0, op1), *after)

        def copy(out, a, *after, e="dve"):
            return p.op(e, lambda g: g.tensor_copy(out, a), *after)

        def mm(out, lhsT, rhs, start, stop, *after, inc=False):
            return p.op("pe", lambda g: g.matmul(out, lhsT, rhs, start=start, stop=stop), *after, inc=inc)

        def tr(out, in_, idn, *after, inc=False):
            return p.op("pe", lambda g: g.transpose(out, in_, idn), *after, inc=inc)

        def scan(out, a, b, *after):
            return p.op("dve", lambda g: g.tensor_tensor_scan(out, a, b, 0.0, ALU.mult, ALU.add), *after)

        def recip(out, a, *after):
            return p.op("dve", lambda g: g.reciprocal(out, a), *after)

        def rmax(out, a, *after, negate=False):
            return p.op("dve", lambda g: g.reduce_max(out, a, AXX, negate=negate), *after)

        def fill(out, value, *after):
            return p.op("dve", lambda g: g.memset(out, value), *after)

        def f32(ap):
            return ap.bitcast(F)

        def split(h, l, src, *after):
            a = act(h, src, ACT.Copy, *after)
            return [a, tt(l, src, f32(h), ALU.subtract, a, *after)]

        PLAN = plan_units()
        groups, i = [], 0
        while i < len(PLAN):
            name, at, kb = PLAN[i]
            two = i + 1 < len(PLAN) and PLAN[i + 1] == (name, at + 1, kb)
            groups.append((name, at, kb, i, 2 if two else 1))
            i += 2 if two else 1
        where = {}
        for gi, (name, at, kb, u, n) in enumerate(groups):
            for k in range(n):
                where[u + k] = (gi, k)
        gtok, gread = {}, {}
        wtok = {}
        wfree = {}
        nx = {"group": 0, "split": 0, "unit": 0}

        def load_group():
            gi = nx["group"]
            if gi >= len(groups):
                return
            nx["group"] += 1
            name, at, kb, u, n = groups[gi]
            free = gread.get(gi - NRAW)
            dst = RAW[:, gi % NRAW, 0:n, 0:kb * 128]
            src = D[name][at:at + n, :, :].rearrange("u p c -> p u c")
            gtok[gi] = p.dma("sp", dst, src, free)

        def split_unit(u):
            if u >= len(PLAN):
                return
            gi, k = where[u]
            kb = PLAN[u][2]
            s = u % NW
            src = RAW[:, gi % NRAW, k, 0:kb * 128]
            wtok[u] = split(WH[:, s, 0:kb * 128], WL[:, s, 0:kb * 128], src, gtok[gi], wfree.get(s))
            if k == groups[gi][4] - 1:
                gread[gi] = wtok[u]
                load_group()


        def split_to(n):
            while nx["split"] < min(n, len(PLAN)):
                split_unit(nx["split"])
                nx["split"] += 1

        def next_unit(name):
            u = nx["unit"]
            assert PLAN[u][0] == name, (PLAN[u], name)
            nx["unit"] += 1
            split_to(u + NW)
            return u

        bank = {"n": 0}
        bfree = {}

        def next_bank(n=4):
            b = bank["n"] % n
            bank["n"] += 1
            return b

        together = []

        def first_units(name, n, xh, xl, xtok):
            u0 = nx["unit"]
            split_to(u0 + NW)
            nx["unit"] += n
            kb = PLAN[u0][2]
            banks = [next_bank() for _ in range(n)]
            toks = {}
            for k in range(kb):
                for i in range(n):
                    u, b = u0 + i, banks[i]
                    assert PLAN[u][0] == name and PLAN[u][2] == kb
                    s = u % NW
                    out = PS[b][:, :]
                    wh, wl = WH[:, s, 128 * k:128 * k + 128], WL[:, s, 128 * k:128 * k + 128]
                    mm(out, wh, xh[k], k == 0, False, wtok[u] if k == 0 else None, bfree.get(b) if k == 0 else None, xtok[k])
                    mm(out, wh, xl[k], False, False)
                    toks[i] = mm(out, wl, xh[k], False, k == kb - 1, inc=k == kb - 1)
                    wfree[s] = toks[i]
            for i in range(n):
                together.append((name, banks[i], PS[banks[i]][:, :], toks[i]))

        def unit(name, xh, xl, xtok):
            if together:
                got = together.pop(0)
                assert got[0] == name
                return got[1:]
            u = next_unit(name)
            kb, s = PLAN[u][2], u % NW
            b = next_bank()
            out = PS[b][:, :]
            tok = None
            for k in range(kb):
                wh, wl = WH[:, s, 128 * k:128 * k + 128], WL[:, s, 128 * k:128 * k + 128]
                mm(out, wh, xh[k], k == 0, False, wtok[u] if k == 0 else None, bfree.get(b) if k == 0 else None, xtok[k])
                mm(out, wh, xl[k], False, False)
                tok = mm(out, wl, xh[k], False, k == kb - 1, inc=k == kb - 1)
            wfree[s] = tok
            return b, out, tok

        def unit_tok(name, n, xtok, strided):
            us = [next_unit(name)]
            if n == 2:
                us.append(us[0] + 1)
                assert PLAN[us[1]][0] == name and us[0] % 2 == 0
                nx["unit"] += 1
            s = us[0] % NW
            bs = [next_bank() for _ in range(n)]
            tok = None
            w = 128 * n
            for t in range(4):
                b = bs[t * n // 4]
                c = w * (t % (4 // n))
                out = PS[b][:, c:c + w]
                for k in range(8):
                    tk = slice(t, T, 4) if strided else slice(128 * t, 128 * t + 128)
                    wh = WH[:, s:s + n, 128 * k:128 * k + 128]
                    wl = WL[:, s:s + n, 128 * k:128 * k + 128]
                    mm(out, XH[:, k, tk], wh, k == 0, False, [wtok[u] for u in us] if t == k == 0 else None,
                       bfree.get(b) if k == 0 else None, xtok[k])
                    mm(out, XL[:, k, tk], wh, False, False)
                    tok = mm(out, XH[:, k, tk], wl, False, k == 7, inc=t == 3 and k == 7)
            for u in us:
                wfree[u % NW] = tok
            split_to(us[-1] + NW)
            return bs, tok

        def v_pair(dst, name, xtok, strided):
            bs, tok = unit_tok(name, 2, xtok, strided)
            for i, b in enumerate(bs):
                src = PS[b][:, :].rearrange("p (t n c) -> p t n c", t=2, n=2)
                bfree[b] = [act(dst[n][:, 256 * i:256 * i + 256].rearrange("p (t c) -> p t c", t=2),
                                src[:, :, n, :], ACT.Copy, tok) for n in range(2)]

        XHL = [XH[:, k, :] for k in range(8)], [XL[:, k, :] for k in range(8)]

        def tables():
            p.op("act", lambda g: g.preload_act_table_set("natural_log_exp_and_others"), inc=False)

        st = {}

        def stat(y, m, tok, mean):
            S1, S2 = TM[:, 0, :], TM[:, 1, :]
            if m == 0:
                st["s2"] = act(S2, y, ACT.Square, tok, st.get("free"))
                st["s1"] = copy(S1, y, tok, st.get("free"), e="pool") if mean else None
                st["sq"] = {}
                return
            sq = TM[:, 6 + m % 2, :]
            a = act(sq, y, ACT.Square, tok, st["sq"].get(m % 2), st.get("sqfree") if m < 3 else None)
            st["s2"] = tt(S2, S2, sq, ALU.add, a, st["s2"])
            st["sq"][m % 2] = st["s2"]
            if mean:
                st["s1"] = tt(S1, S1, y, ALU.add, tok, st["s1"], e="pool")

        def rstd_of(out, var_psum, scale, eps, *after):
            a = act(out, var_psum, ACT.Ln, *after, bias=eps, scale=scale)
            return act(out, out, ACT.Exp, a, scale=-0.5)

        def stats_end(mean, eps_col):
            S1, S2, RS = TM[:, 0, :], TM[:, 1, :], TM[:, 2, :]
            b2 = next_bank()
            t2 = mm(PS[b2][:, :], onesd, S2, True, True, st["s2"], bfree.get(b2), inc=True)
            if not mean:
                r = rstd_of(RS, PS[b2][:, :], 1.0, eps_col, t2)
                bfree[b2] = r
                st["free"] = t2
                return None, [], r, None
            b1 = next_bank()
            t1 = mm(PS[b1][:, :], onesd, S1, True, True, st["s1"], bfree.get(b1), inc=True)
            a = act(S1, PS[b1][:, :], ACT.Square, t1)
            v = tt(S2, PS[b2][:, :], S1, ALU.subtract, a, t2)
            bfree[b2] = v
            v2 = ts(S2, S2, 0.0, ALU.max, v)
            r = rstd_of(RS, S2, 1.0, eps_col, v2)
            st["free"] = [r]
            return PS[b1][:, :], t1, r, b1

        def layer_norm(gname, bname, l, last=False):
            M, mt, r, b1 = stats_end(True, EPS5)
            RS = TM[:, 2, :]
            pe = p.now("pe")
            toks, A1, A2, A3, A4, A5 = [None] * 8, {}, {}, {}, {}, {}
            b = next_bank() if last else None
            for i in range(10):
                if i < 8:
                    t = TM[:, 3 + i % 3, :]
                    A1[i] = tt(t, X[:, i, :], M, ALU.subtract, mt, xw[i], A3.get(i - 3))
                    A2[i] = tt(t, t, RS, ALU.mult, A1[i], r, e="pool")
                    if i == 7:
                        bfree[b1] = A1[i]
                m = i - 1
                if 0 <= m < 8:
                    t = TM[:, 3 + m % 3, :]
                    kw = dict(scale=vec(gname, 8 * l + m), bias=vec(bname, 8 * l + m))
                    if not last:
                        toks[m] = [act(XH[:, m, :], t, ACT.Identity, A2[m], pe, **kw)]
                    A3[m] = xw[m] = act(X[:, m, :], t, ACT.Identity, A2[m], **kw)
                    if last:
                        sq = TM[:, 6 + m % 2, :]
                        A4[m] = act(sq, X[:, m, :], ACT.Square, xw[m], A5.get(m - 2))
                        A5[m] = mm(PS[b][:, :], onesd, sq, m == 0, m == 7, A4[m], bfree.get(b), inc=True)
                m = i - 2
                if 0 <= m < 8 and not last:
                    toks[m].append(tt(XL[:, m, :], X[:, m, :], f32(XH[:, m, :]), ALU.subtract, toks[m][0], xw[m], pe))
            if last:
                r = rstd_of(RS, PS[b][:, :], 1.0, EPS6, A5[7], A2[7])
                bfree[b] = r
                return r
            return toks

        def rms_apply(src, r, gname, gi, srctok):
            RS = TM[:, 2, :]
            pe = p.now("pe")
            toks, A1 = [None] * 8, {}
            for i in range(10):
                if i < 8:
                    t = TM[:, 3 + i % 3, :]
                    A1[i] = stt(t, src[:, i, :], vec(gname, gi + i), RS, ALU.mult, ALU.mult, r, srctok[i],
                                toks[i - 3] if i > 2 else None)
                    toks[i] = [act(XH[:, i, :], t, ACT.Copy, A1[i], pe)]
                m = i - 2
                if 0 <= m < 8:
                    t = TM[:, 3 + m % 3, :]
                    toks[m].append(tt(XL[:, m, :], t, f32(XH[:, m, :]), ALU.subtract, toks[m][0], pe))
            return toks

        def rms_add(r, gi, ytok, with_stats=True):
            RS = TM[:, 2, :]
            b = next_bank()
            A1, A2, A3, A4 = {}, {}, {}, {}
            for i in range(11):
                if i < 8:
                    t = TM[:, 3 + i % 3, :]
                    A1[i] = stt(t, Y[:, i, :], vec("ng", gi + i), RS, ALU.mult, ALU.mult, r, ytok[i], A2.get(i - 3))
                    A2[i] = xw[i] = tt(X[:, i, :], X[:, i, :], t, ALU.add, A1[i], xw[i], e="pool")
                m = i - 2
                if with_stats and 0 <= m < 8:
                    sq = TM[:, 6 + m % 2, :]
                    A3[m] = act(sq, X[:, m, :], ACT.Square, xw[m], A4.get(m - 2))
                    A4[m] = mm(PS[b][:, :], onesd, sq, m == 0, m == 7, A3[m], bfree.get(b), inc=True)
            if not with_stats:
                return None
            r2 = rstd_of(RS, PS[b][:, :], 1.0, EPS6, A4[7], A1[7])
            bfree[b] = r2
            return r2

        xw = [None] * 8
        xin = D["x"].rearrange("(k p) t -> p k t", p=128)
        xw[0] = p.dma("sp", X[:, 0:1, :], xin[:, 0:1, :])
        load_group()
        for m in range(1, 8):
            xw[m] = p.dma("sp", X[:, m:m + 1, :], xin[:, m:m + 1, :])
        for _ in range(NRAW - 1):
            load_group()
        t_vec = p.dma("pool", VEC[:, :], D["vec"])
        t_cst = p.dma("pool", CST[:, :], D["small"])
        EPS5, EPS6 = COL[:, 254:255], COL[:, 255:256]
        e1 = fill(EPS5, 1e-5)
        e2 = fill(EPS6, 1e-6)
        split_to(2)
        xtok = [split(XH[:, m, :], XL[:, m, :], X[:, m, :], xw[m]) for m in range(8)]
        at0, n0 = places(C0)
        Yf = Y[:, :, :].rearrange("p a b -> p (a b)")
        ARf = AR[:, :, :].rearrange("p a b -> p (a b)")
        t_c0 = p.dma("pool", Yf[:, 0:n0], D["c0"], xw[7])

        def hold(e, *toks):
            w = p.waits(e, toks)
            p.q[e].append((w, None, None))

        def c_of(base, at, name, lo=0, hi=128):
            a, k = at[name]
            return base[lo:hi, a:a + k]

        def softplus_steps(out, x, tmp, *after):
            u, w, l, d = tmp
            a = act(u, x, ACT.Abs, *after)
            yield
            a = act(u, u, ACT.Exp, a, scale=-1.0)
            yield
            b = ts(w, u, 1.0, ALU.add, a)
            yield
            a = act(l, w, ACT.Ln, b)
            yield
            b = ts(d, w, -1.0, ALU.add, b)
            c = ts(w, d, 0.0, ALU.is_equal, b, a)
            yield
            e = tt(l, l, w, ALU.add, a, c)
            f = tt(d, d, w, ALU.add, c)
            yield
            f = recip(d, d, f)
            yield
            e = tt(l, l, d, ALU.mult, e, f)
            yield
            e = tt(l, l, u, ALU.mult, e)
            yield
            yield stt(out, x, 0.0, l, ALU.max, ALU.add, e, *after)

        def run(steps, n=None):
            last = None
            while n is None or n > 0:
                try:
                    last = next(steps)
                except StopIteration:
                    break
                n = None if n is None else n - 1
            return last

        def conv_psum(dst, ps, w, taps, first, *after):
            a = act(dst, ps, ACT.Identity, *after, scale=w(taps - 1), bias=first)
            for j in range(taps - 2, -1, -1):
                s = taps - 1 - j
                a = stt(dst[:, s:T], ps[:, 0:T - s], w(j), dst[:, s:T], ALU.mult, ALU.add, a, *after)
            return a

        def rope(dst, ps, tok, rot, cos, sin, tmp, tmpfree, b, *after):
            a = act(dst, ps, ACT.Copy, tok, *after)
            b2 = next_bank()
            t = mm(PS[b2][:, :], rot, dst, True, True, a, bfree.get(b2), inc=True)
            d = tt(tmp, PS[b2][:, :], sin, ALU.mult, t, tmpfree)
            bfree[b] = a
            bfree[b2] = d
            e = tt(dst, dst, cos, ALU.mult, a, t, e="pool")
            return tt(dst, dst, tmp, ALU.add, d, e)

        def attention(jobs, scale, lse=None):
            n = len(jobs)
            S = {}

            def A(i):
                j = jobs[i]
                nk = j["nk"]
                ps = PS[4 + i % 2][:, 0:nk]
                more = j.get("more")
                t = mm(ps, j["q"], j["k"], True, more is None, j.get("after"), S.get(("fa", i - 2)), inc=more is None)
                if more is not None:
                    t = mm(ps, more[0], more[1], False, True, inc=True)
                S[("a", i)] = t

            def B(i):
                j = jobs[i]
                nk = j["nk"]
                t = TM[:, i % 3, 0:nk]
                if "cq" in j:
                    a = stt(t, PS[4 + i % 2][:, 0:nk], j["cq"], j["mask"], ALU.add, ALU.add, S[("a", i)], S.get(("e", i - 3)))
                else:
                    a = stt(t, PS[4 + i % 2][:, 0:nk], scale, j["mask"], ALU.mult, ALU.add, S[("a", i)], S.get(("e", i - 3)))
                S[("fa", i)] = a
                nm = COL[:, 8 * (i % 3):8 * (i % 3) + 1]
                if "sink" in j:
                    mx = COL[:, 8 * (i % 3) + 4:8 * (i % 3) + 5]
                    b = rmax(mx, t, a, S.get(("c", i - 3)))
                    S[("b", i)] = ts(nm, mx, j["sink"], ALU.max, b, S.get(("c", i - 3)), s2=-1.0, op1=ALU.mult)
                else:
                    S[("b", i)] = rmax(nm, t, a, S.get(("c", i - 3)), S.get(("dd", i - 3)), negate=True)

            def C(i):
                j = jobs[i]
                t = TM[:, i % 3, 0:j["nk"]]
                nm = COL[:, 8 * (i % 3):8 * (i % 3) + 1]
                l = COL[:, 8 * (i % 3) + 1:8 * (i % 3) + 2]
                S[("c", i)] = act(t, t, ACT.Exp, S[("b", i)], S.get(("d", i - 3)), bias=nm, accum=l)
                if "sink" in j:
                    es = COL[:, 8 * (i % 3) + 2:8 * (i % 3) + 3]
                    S[("c", i)] = act(es, j["sink"], ACT.Exp, S[("b", i)], S.get(("d", i - 3)), bias=nm)

            def Dn(i):
                j = jobs[i]
                nk = j["nk"]
                t = TM[:, i % 3, 0:nk]
                c = 8 * (i % 3)
                l, es, r = COL[:, c + 1:c + 2], COL[:, c + 2:c + 3], COL[:, c + 3:c + 4]
                a = S[("c", i)]
                if "sink" in j:
                    a = tt(l, l, es, ALU.add, a)
                S[("dd", i)] = None
                if lse is not None:
                    copy(j["lout"], l, a)
                    S[("dd", i)] = ts(j["mout"], COL[:, c:c + 1], -1.0, ALU.mult, S[("b", i)])
                a = recip(r, l, a)
                S[("d", i)] = ts(t, t, r, ALU.mult, a)

            def E_(i):
                j = jobs[i]
                nb = j["nk"] // 128
                t = None
                for x in range(nb):
                    t = tr(PS[6 + i % 2][:, 128 * x:128 * x + 128], TM[:, i % 3, 128 * x:128 * x + 128], ident,
                           S[("d", i)], S.get(("f", i - 2)), inc=x == nb - 1)
                S[("e", i)] = t

            def F_(i):
                nk = jobs[i]["nk"]
                S[("f", i)] = act(TM[:, 3 + i % 2, 0:nk], PS[6 + i % 2][:, 0:nk], ACT.Copy, S[("e", i)], S.get(("g", i - 2)))

            def G(i):
                j = jobs[i]
                nb = j["nk"] // 128
                t = None
                for x in range(nb):
                    t = mm(j["out"], j["v"][x], TM[:, 3 + i % 2, 128 * x:128 * x + 128], x == 0, x == nb - 1,
                           S[("f", i)], j.get("outfree"), inc=x == nb - 1)
                S[("g", i)] = t
                if "then" in j:
                    j["then"](t)

            A(0)
            for i in range(n + 2):
                if i + 1 < n:
                    A(i + 1)
                if i < n:
                    B(i)
                    C(i)
                if 0 <= i - 1 < n:
                    Dn(i - 1)
                    E_(i - 1)
                    F_(i - 1)
                if 0 <= i - 2 < n:
                    G(i - 2)

        def mix_out(name, nk, otok):
            tables()
            first_units(name, 3, XHL[0][:nk], XHL[1][:nk], otok)
            for m in range(8):
                b, ps, tok = unit(name, XHL[0][:nk], XHL[1][:nk], otok)
                xw[m] = stt(X[:, m, :], X[:, m, :], ALPHA, ps, ALU.mult, ALU.add, tok, xw[m])
                bfree[b] = xw[m]
                stat(X[:, m, :], m, xw[m], True)

        def mlp(l, xt):
            hfree = {}
            rfree = {}
            first_units(f"w1_{l}", 3, *XHL, xt)
            for q in range(4):
                ht = []
                o = 16 * (q % 2)
                for m in range(8):
                    b, ps, tok = unit(f"w1_{l}", *XHL, xt)
                    r, h = TM[:, 2 + m % 2, :], TM[:, 4 + m % 2, :]
                    hh, hl = H[:, o + m, :], H[:, o + 8 + m, :]
                    a = act(r, ps, ACT.Relu, tok, rfree.get(m % 2))
                    c = stt(h, ps, 0.0, r, ALU.max, ALU.mult, a, rfree.get(("h", m % 2)))
                    bfree[b] = c
                    d = act(hh, h, ACT.Copy, c, hfree.get(q - 2))
                    e = tt(hl, h, f32(hh), ALU.subtract, d, hfree.get(q - 2))
                    rfree[m % 2] = c
                    rfree[("h", m % 2)] = [e, d]
                    ht.append(e)
                hl_ = [H[:, o + k, :] for k in range(8)], [H[:, o + 8 + k, :] for k in range(8)]
                for m in range(8):
                    b, ps, tok = unit(f"w2_{l}", *hl_, ht)
                    if q == 0:
                        xw[m] = stt(X[:, m, :], X[:, m, :], ALPHA, ps, ALU.mult, ALU.add, tok, xw[m])
                    else:
                        xw[m] = tt(X[:, m, :], X[:, m, :], ps, ALU.add, tok, xw[m])
                    bfree[b] = xw[m]
                    if q == 3:
                        stat(X[:, m, :], m, xw[m], True)
                hfree[q] = tok

        def ffn(l, xt):
            hfree, rfree = {}, {}
            yt = [None] * 8
            i = 0
            first_units(f"up_{l}", 3, *XHL, xt)
            for q, n in enumerate((8, 8, 6)):
                ht = []
                o = 16 * (q % 2)
                for m in range(n):
                    g, v = TM[:, 2 + 2 * (i % 2), :], TM[:, 3 + 2 * (i % 2), :]
                    c = []
                    for s, dst in ((0, g), (1, v)):
                        blk = 22 * s + q * 8 + m
                        b, ps, tok = unit(f"up_{l}", *XHL, xt)
                        w = lambda j, blk=blk: vec("fcw", 132 * l + 3 * blk + j)
                        a = conv_psum(dst, ps, w, 3, vec("fcb", 44 * l + blk), tok, rfree.get(i % 2))
                        bfree[b] = a
                        c.append(a)
                    hh, hl = H[:, o + m, :], H[:, o + 8 + m, :]
                    a = act(g, g, ACT.Gelu_apprx_tanh, c[0])
                    a = tt(g, g, v, ALU.mult, a, c[1], e="pool")
                    d = act(hh, g, ACT.Copy, a, hfree.get(q - 2))
                    e = tt(hl, g, f32(hh), ALU.subtract, d, hfree.get(q - 2))
                    rfree[i % 2] = e
                    ht.append(e)
                    i += 1
                hl_ = [H[:, o + k, :] for k in range(n)], [H[:, o + 8 + k, :] for k in range(n)]
                if q == 2:
                    tables()
                for m in range(8):
                    b, ps, tok = unit(f"dn{n}_{l}", *hl_, ht)
                    if q == 0:
                        yt[m] = act(Y[:, m, :], ps, ACT.Copy, tok)
                    else:
                        yt[m] = tt(Y[:, m, :], Y[:, m, :], ps, ALU.add, tok, yt[m])
                    bfree[b] = yt[m]
                    if q == 2:
                        stat(Y[:, m, :], m, yt[m], False)
                hfree[q] = tok
            return yt

        def hybrid(xt):
            first_units("hyb", 3, *XHL, xt)
            sl = lambda i: AR[:, i, :]
            QKV = [sl(i) for i in range(12)]
            Z = [sl(12 + i) for i in range(4)]
            QA = [sl(16 + i) for i in range(4)]
            KA, VA = sl(20), sl(21)
            GR = sl(22)
            BR = sl(23)
            c0 = lambda name, lo=0, hi=128: c_of(Yf, at0, name, lo, hi)
            for e in ("act", "dve", "pe", "pool"):
                hold(e, t_cst, t_vec, e1, e2)
            b, ps, tok = unit("hyb", *XHL, xt)
            tb = act(BR[0:4, :], ps[0:4, :], ACT.Sigmoid, tok)
            r = [sl(24 + i)[32:36, :] for i in range(5)]
            ta = act(r[0], ps[32:36, :], ACT.Identity, tok, bias=vec("dtb", 0, 1, 32, 36))
            bfree[b] = [ta, tb]

            def decay_rows():
                tables()
                ea = act(COL[32:36, 200:201], vec("alog", 0, 1, 32, 36), ACT.Exp)
                sp = None
                for sp in softplus_steps(r[0], r[0], r[1:5], ta):
                    yield
                g = ts(r[0], r[0], COL[32:36, 200:201], ALU.mult, sp, ea, s2=-1.0, op1=ALU.mult)
                yield
                for c in range(4):
                    gs = slice(128 * c, 128 * c + 128)
                    scan(GR[32:36, gs], ones[32:36, :], r[0][:, gs], g)
                    yield

            rows = decay_rows()
            qkvt = []
            for i in range(12):
                b, ps, tok = unit("hyb", *XHL, xt)
                w = lambda j, i=i: vec("hcw", 4 * i + j)
                a = conv_psum(QKV[i], ps, w, 4, 0.0, tok)
                bfree[b] = a
                qkvt.append(a)
                run(rows, 2)
            run(rows)
            for i in range(12):
                qkvt[i] = act(QKV[i], QKV[i], ACT.Silu, qkvt[i])
            zt = []
            for i in range(4):
                b, ps, tok = unit("hyb", *XHL, xt)
                zt.append(act(Z[i], ps, ACT.Silu, tok))
                bfree[b] = zt[-1]
            free = {}
            for i in range(8):
                sq, rs = TM[:, 2 + i % 2, :], TM[:, 4 + i % 2, :]
                a = act(sq, QKV[i], ACT.Square, qkvt[i], free.get(("s", i % 2)))
                b = next_bank()
                t = mm(PS[b][:, :], ones, sq, True, True, a, bfree.get(b), inc=True)
                free[("s", i % 2)] = t
                rr = rstd_of(rs, PS[b][:, :], 1.0, EPS6, t, free.get(("r", i % 2)))
                bfree[b] = rr
                if i < 4:
                    qkvt[i] = stt(QKV[i], QKV[i], 128 ** -0.5, rs, ALU.mult, ALU.mult, rr)
                else:
                    qkvt[i] = tt(QKV[i], QKV[i], rs, ALU.mult, rr)
                free[("r", i % 2)] = qkvt[i]
            rt = []
            for e in ("pe", "dve", "pool"):
                hold(e, t_c0)
            for i in range(5):
                b, ps, tok = unit("hyb", *XHL, xt)
                rt.append(rope(QA[i] if i < 4 else KA, ps, tok, cst["rot1"], c0("cos"), c0("sin"),
                               TM[:, 6 + i % 2, :], rt[i - 2] if i > 1 else None, b))
            bs, tok = unit_tok("hyb", 1, xt, False)
            bfree[bs[0]] = act(VA, PS[bs[0]][:, :], ACT.Copy, tok)
            p.fence()
            jobs = []
            otok = [None] * 8

            def out_of(j):
                def then(t):
                    otok[j] = split(XH[:, j, :], XL[:, j, :], PS[j][:, :], t)
                return then

            for j in range(4):
                for hp in range(2):
                    h = 4 * hp + j
                    lo = 64 * hp
                    for n in range(4):
                        k0 = max(n - 1, 0)
                        job = dict(q=QA[j][lo:lo + 64, 128 * n:128 * n + 128], k=KA[lo:lo + 64, 128 * k0:128 * n + 128],
                                   nk=128 * (n + 1 - k0), v=[VA[:, 128 * c + lo:128 * c + lo + 64] for c in range(k0, n + 1)],
                                   out=PS[j][lo:lo + 64, 128 * n:128 * n + 128], sink=vec("sink", h),
                                   mask=c0("slide")[:, 256 - 128 * (n + 1 - k0):256])
                        jobs.append(job)
                jobs[-1]["then"] = out_of(j)
            attention(jobs, 64 ** -0.5)
            p.fence()
            gcol = COL[:, 32:48].rearrange("p (c h) -> p c h", c=4)
            bcol = COL[:, 48:64].rearrange("p (c h) -> p c h", c=4)
            bg = COL[:, 64:80].rearrange("p (c h) -> p c h", c=4)
            for c in range(4):
                gs = slice(128 * c, 128 * c + 128)
                mm(PS[0][:, 4 * c:4 * c + 4], GR[32:36, gs], ident[32:36, 32:36], True, True)
                t = mm(PS[1][:, 4 * c:4 * c + 4], BR[0:4, gs], ident[0:4, 0:4], True, True, inc=True)
            a = copy(COL[:, 32:48], PS[0][:, 0:16], t)
            b = copy(COL[:, 48:64], PS[1][:, 0:16], t)
            e = act(COL[:, 64:80], COL[:, 32:48], ACT.Exp, a)
            e = tt(COL[:, 64:80], COL[:, 64:80], COL[:, 48:64], ALU.mult, e, b)
            p.fence()
            I = ident
            for pair in range(2):
                hs = (2 * pair, 2 * pair + 1)
                W = {h: [sl(16 + 8 * x + i) for i in range(6)] for x, h in enumerate(hs)}
                gl = {h: COL[:, 80 + 8 * x:84 + 8 * x] for x, h in enumerate(hs)}
                kt_ = {h: COL[:, 100 + 8 * x:104 + 8 * x] for x, h in enumerate(hs)}
                tk = {}
                for x, h in enumerate(hs):
                    Q, KT = QKV[h], QKV[4 + h]
                    a_, b_, c_, d_, e_, f_ = W[h]
                    pb = 4 * x
                    gb, bb = PS[pb][:, :], PS[pb + 1][:, :]
                    t1 = mm(gb, c0("sel", 32, 36)[:, 128 * h:128 * h + 128], GR[32:36, :], True, True, inc=True)
                    t2 = mm(bb, c0("sel", 0, 4)[:, 128 * h:128 * h + 128], BR[0:4, :], True, True, inc=True)
                    kb = tt(a_, KT, bb, ALU.mult, t2)
                    last = None
                    for c in range(4):
                        gs = slice(128 * c, 128 * c + 128)
                        last = ts(b_[:, gs], gb[:, gs], gcol[:, c, h:h + 1], ALU.subtract, t1, s2=0.0, op1=ALU.min)
                    dc = act(b_, b_, ACT.Exp, last)
                    m1 = tt(b_.rearrange("p (c i) -> p c i", c=4), b_.rearrange("p (c i) -> p c i", c=4),
                            c0("mi")[:, None, :].broadcast_to([128, 4, 128]), ALU.mult, dc)
                    g1 = tt(kt_[h], gb[:, 127:T:128], gcol[:, :, h], ALU.subtract, t1)
                    g1 = act(kt_[h], kt_[h], ACT.Exp, g1)
                    g2 = act(gl[h], gb[:, 127:T:128], ACT.Exp, t1)
                    eg = act(c_, gb, ACT.Exp, t1)
                    for c in range(4):
                        gs = slice(128 * c, 128 * c + 128)
                        mm(PS[pb + 2][:, gs], KT[:, gs], a_[:, gs], True, True, kb)
                        t3 = mm(PS[pb + 3][:, gs], KT[:, gs], Q[:, gs], True, True, inc=True)
                    qk = tt(d_, PS[pb + 3][:, :], b_, ALU.mult, m1, t3)
                    qg = tt(Q, Q, c_, ALU.mult, eg, t3, e="pool")
                    m2 = tt(b_.rearrange("p (c i) -> p c i", c=4), b_.rearrange("p (c i) -> p c i", c=4),
                            c0("ms")[:, None, :].broadcast_to([128, 4, 128]), ALU.mult, qk)
                    at = tt(c_, PS[pb + 2][:, :], b_, ALU.mult, m2, t3, qg)
                    tk[h] = dict(at=at, qk=qk, qg=qg, g1=g1, g2=g2, kb=kb)
                    mo = tt(b_.rearrange("p (c i) -> p c i", c=4), c_.rearrange("p (c i) -> p c i", c=4),
                            c0("lv")[:, 0:128][:, None, :].broadcast_to([128, 4, 128]), ALU.mult, at)
                    tT = tt(f_.rearrange("p (c i) -> p c i", c=4), I[:, None, :].broadcast_to([128, 4, 128]),
                            b_.rearrange("p (c i) -> p c i", c=4), ALU.subtract, mo)
                    for c in range(4):
                        gs = slice(128 * c, 128 * c + 128)
                        t4 = tr(PS[pb][:, gs], f_[:, gs], I, tT, eg, g2, g1, last, inc=c == 3)
                    tk[h]["T"] = act(e_, PS[pb][:, :], ACT.Copy, t4)
                    tk[h]["TT"] = tT
                    tk[h]["free"] = t4
                for lv in range(1, 7):
                    for x, h in enumerate(hs):
                        a_, b_, c_, d_, e_, f_ = W[h]
                        k = tk[h]
                        pb = 4 * x
                        ao = tt(b_.rearrange("p (c i) -> p c i", c=4), c_.rearrange("p (c i) -> p c i", c=4),
                                c0("lv")[:, 128 * lv:128 * lv + 128][:, None, :].broadcast_to([128, 4, 128]),
                                ALU.mult, k["at"], k["free"], e="pool")
                        for c in range(4):
                            gs = slice(128 * c, 128 * c + 128)
                            t1 = mm(PS[pb + 1][:, gs], b_[:, gs], e_[:, gs], True, True, ao, k["T"], inc=c == 3)
                        y = act(a_, PS[pb + 1][:, :], ACT.Copy, t1, k["kb"])
                        for c in range(4):
                            gs = slice(128 * c, 128 * c + 128)
                            t2 = mm(PS[pb + 2][:, gs], a_[:, gs], f_[:, gs], True, True, y, k["TT"], inc=c == 3)
                        if lv < 6:
                            for c in range(4):
                                gs = slice(128 * c, 128 * c + 128)
                                t3 = mm(PS[pb + 3][:, gs], f_[:, gs], a_[:, gs], True, True, k["qk"], inc=c == 3)
                            k["T"] = tt(e_, e_, PS[pb + 3][:, :], ALU.subtract, t3, k["T"])
                        else:
                            t3 = t2
                        k["TT"] = tt(f_, f_, PS[pb + 2][:, :], ALU.subtract, t2, t3, k["TT"])
                        k["free"] = [t2, t3]
                        k["y"] = y
                p.fence()
                for x, h in enumerate(hs):
                    a_, b_, c_, d_, e_, f_ = W[h]
                    k = tk[h]
                    pb = 4 * x
                    for c in range(4):
                        gs = slice(128 * c, 128 * c + 128)
                        t1 = tr(PS[pb][:, gs], QKV[4 + h][:, gs], I, inc=c == 3)
                    for c in range(4):
                        gs = slice(128 * c, 128 * c + 128)
                        t2 = tr(PS[pb + 1][:, gs], QKV[8 + h][:, gs], I, inc=c == 3)
                    s1, s2 = [], []
                    for c in range(4):
                        gs = slice(128 * c, 128 * c + 128)
                        s1.append(ts(a_[:, gs], PS[pb][:, gs], bg[:, c, h:h + 1], ALU.mult, t1))
                        s2.append(act(b_[:, gs], PS[pb + 1][:, gs], ACT.Copy, t2, scale=bcol[:, c, h:h + 1]))
                    for c in range(4):
                        gs = slice(128 * c, 128 * c + 128)
                        t3 = mm(PS[pb + 2][:, gs], a_[:, gs], f_[:, gs], True, True, s1[c], inc=c == 3)
                    nw = ts(c_, PS[pb + 2][:, :], -1.0, ALU.mult, t3)
                    kt = []
                    for c in range(4):
                        gs = slice(128 * c, 128 * c + 128)
                        kt.append(ts(a_[:, gs], PS[pb][:, gs], kt_[h][:, c:c + 1], ALU.mult, t3, k["g1"]))
                    k.update(nw=nw, kt=kt, vb=s2)
                p.fence()
                S = {h: [W[h][4][:, 0:128], W[h][4][:, 128:256]] for h in hs}
                VN = {h: [W[h][4][:, 256:384], W[h][4][:, 384:512]] for h in hs}
                for c in range(4):
                    gs = slice(128 * c, 128 * c + 128)
                    for x, h in enumerate(hs):
                        a_, b_, c_, d_, e_, f_ = W[h]
                        k = tk[h]
                        pb = 4 * x
                        so, sn = S[h][c % 2], S[h][(c + 1) % 2]
                        vn = VN[h][c % 2]
                        t1 = mm(PS[pb][:, 0:128], f_[:, gs], b_[:, gs], True, c == 0, k.get("vfree"), inc=c == 0)
                        if c:
                            t1 = mm(PS[pb][:, 0:128], c_[:, gs], so, False, True, k["S"], inc=True)
                        v = act(vn, PS[pb][:, 0:128], ACT.Copy, t1)
                        k["vfree"] = v
                        if c:
                            mm(PS[pb + 2][:, gs], so, QKV[h][:, gs], True, False)
                        t2 = mm(PS[pb + 2][:, gs], vn, d_[:, gs], c == 0, True, v, inc=True)
                        if c < 3:
                            t3 = mm(PS[pb + 1][:, 0:128], a_[:, gs], vn, True, True, k.get("S"), inc=True)
                            if c == 0:
                                k["S"] = copy(sn, PS[pb + 1][:, 0:128], t3)
                            else:
                                k["S"] = stt(sn, so, gl[h][:, c:c + 1], PS[pb + 1][:, 0:128], ALU.mult, ALU.add, t3, k["S"])
                        k["o"] = t2
                for x, h in enumerate(hs):
                    k = tk[h]
                    a_, b_, c_ = W[h][:3]
                    pb = 4 * x
                    o = PS[pb + 2][:, :]
                    a = act(a_, o, ACT.Square, k["o"])
                    t = mm(PS[pb + 3][:, :], ones, a_, True, True, a, inc=True)
                    r = rstd_of(b_, PS[pb + 3][:, :], 1.0 / 128, EPS6, t)
                    y = stt(c_, o, vec("hnw"), b_, ALU.mult, ALU.mult, r)
                    y = tt(c_, c_, Z[h], ALU.mult, y, e="pool")
                    otok[4 + h] = split(XH[:, 4 + h, :], XL[:, 4 + h, :], c_, y)
                p.fence()
            bfree.clear()
            return otok

        def recurrent(xt):
            sl = lambda i: AR[:, i, :]
            XR, A_ = [sl(i) for i in range(8)], [sl(8 + i) for i in range(8)]
            B_, GA = [Y[:, i, :] for i in range(8)], [sl(16 + i) for i in range(8)]
            nl = COL[:, 0:8]
            a = ts(COL[:, 8:16], vec("lam", 0, 8), -1.0, ALU.mult)
            a = run(softplus_steps(nl, COL[:, 8:16], [COL[:, 16 + 8 * i:24 + 8 * i] for i in range(4)], a))
            nlt = ts(nl, nl, -8.0, ALU.mult, a)
            p8 = COL[:, 48:56]
            nlt = ts(p8, nl, -1.0, ALU.mult, nlt)
            xrt, xs = [], []
            first_units("rin", 3, *XHL, xt)
            for m in range(8):
                b, ps, tok = unit("rin", *XHL, xt)
                w = lambda j, m=m: vec("rcw", 4 * m + j)
                xrt.append(conv_psum(XR[m], ps, w, 4, vec("rcb", m), tok))
                bfree[b] = xrt[-1]
                HH, HL = H[:, 16 + m, :], H[:, 24 + m, :]
                xs.append(split(HH, HL, XR[m], xrt[m]))
            rt, it = {}, {}
            last = None
            for half in range(2):
                for which in range(2):
                    u = next_unit("rwg")
                    s = u % NW
                    for mo in range(4):
                        m = 4 * half + mo
                        b = next_bank()
                        for k in range(2):
                            kk = 2 * (m // 2) + k
                            c = 128 * (2 * mo + k)
                            wh, wl = WH[:, s, c:c + 128], WL[:, s, c:c + 128]
                            mm(PS[b][:, :], wh, H[:, 16 + kk, :], k == 0, False, wtok[u], bfree.get(b), xs[kk])
                            mm(PS[b][:, :], wh, H[:, 24 + kk, :], False, False)
                            last = mm(PS[b][:, :], wl, H[:, 16 + kk, :], False, k == 1, inc=k == 1)
                        dst = (A_ if which == 0 else B_)[m]
                        t = act(dst, PS[b][:, :], ACT.Sigmoid, last, bias=vec("rba" if which == 0 else "rbx", m))
                        bfree[b] = t
                        if which == 0:
                            rt[m] = t
                        else:
                            it[m] = tt(XR[m], XR[m], dst, ALU.mult, t, xs[m], e="pool")
                    wfree[s] = last
            gat, ht, at, bt = {}, {}, {}, {}

            def gate(m):
                b, ps, tok = unit("rin", *XHL, xt)
                gat[m] = act(GA[m], ps, ACT.Copy, tok, last)
                bfree[b] = gat[m]

            def decay(m):
                t = act(B_[m], A_[m], ACT.Tanh, nlt, it[m], rt[m], scale=p8[:, m:m + 1])
                at[m] = act(A_[m], A_[m], ACT.Exp, t, nlt, scale=nl[:, m:m + 1])
                q = TM[:, 2 + m % 2, :]
                c = tt(q, A_[m], A_[m], ALU.mult, at[m], bt.get(m - 2))
                bt[m] = stt(B_[m], q, 1.0, B_[m], ALU.add, ALU.mult, c, t)

            def root(m):
                a = act(B_[m], B_[m], ACT.Sqrt, bt[m])
                a = tt(B_[m], B_[m], XR[m], ALU.mult, a, it[m], e="pool")
                ht[m] = scan(XR[m], A_[m], B_[m], a, at[m])

            for m in range(4):
                gate(m)
                decay(2 * m)
                decay(2 * m + 1)
            for m in range(4, 8):
                gate(m)
                root(2 * m - 8)
                root(2 * m - 7)
            pe = p.now("pe")
            otok, ga, y = [None] * 8, {}, {}
            for i in range(10):
                if i < 8:
                    ga[i] = act(GA[i], GA[i], ACT.Gelu_apprx_tanh, gat[i])
                    y[i] = tt(XR[i], XR[i], GA[i], ALU.mult, ga[i], ht[i], e="pool")
                m = i - 1
                if 0 <= m < 8:
                    otok[m] = [act(XH[:, m, :], XR[m], ACT.Copy, y[m], pe)]
                m = i - 2
                if 0 <= m < 8:
                    otok[m].append(tt(XL[:, m, :], XR[m], f32(XH[:, m, :]), ALU.subtract, otok[m][0], y[m], pe))
            return otok

        at2, n2 = places(C2)
        at3, n3 = places(C3)

        def dilated(xt):
            sl = lambda i: AR[:, i, :]
            QA, KA = [sl(i) for i in range(6)], [sl(6 + i) for i in range(6)]
            VA = [sl(12 + i) for i in range(6)]
            c2 = lambda name, lo=0, hi=128: c_of(ARf[:, 18 * T:], at2, name, lo, hi)
            j = p.now("pe", "act", "dve", "pool")
            t_c2 = p.dma("pool", ARf[:, 18 * T:18 * T + n2], D["c2"], j)
            hold("act", j)
            hold("dve", j)
            rt = []
            first_units("qkv", 3, *XHL, xt)
            hold("dve", t_c2)
            hold("pool", t_c2)
            for i in range(12):
                if i == 3:
                    for v in range(0, 6, 2):
                        v_pair(VA[v:v + 2], "qkv", xt, v >= 2)
                b, ps, tok = unit("qkv", *XHL, xt)
                rt.append(rope(QA[i] if i < 6 else KA[i - 6], ps, tok, cst["rot2"], c2("cos"), c2("sin"),
                               TM[:, 6 + i % 2, :], rt[i - 2] if i > 1 else None, b))
            p.fence()
            LC = COL[:, 32:80]
            MC = COL[:, 80:128]
            jobs = []
            OB = [sl(25 + i) for i in range(6)]
            ot = [None] * 6

            def out_of(jb):
                def then(t):
                    ot[jb] = act(OB[jb], PS[jb % 2][:, :], ACT.Copy, t)
                    for job in jobs:
                        if job["jb"] == jb + 2:
                            job["outfree"] = ot[jb]
                return then

            for jb in range(6):
                g = jb // 2
                for hp in range(2):
                    h = 2 * jb + hp
                    lo = 64 * hp
                    for n in range(4):
                        if g == 0:
                            k0 = max(n - 1, 0)
                            q = QA[jb][lo:lo + 64, 128 * n:128 * n + 128]
                            k = KA[jb][lo:lo + 64, 128 * k0:128 * n + 128]
                            nk = 128 * (n + 1 - k0)
                            v = [VA[jb][:, 128 * c + lo:128 * c + lo + 64] for c in range(k0, n + 1)]
                            mask = c2("dil1")[:, 256 - nk:256]
                            out = PS[jb % 2][lo:lo + 64, 128 * n:128 * n + 128]
                        else:
                            q = QA[jb][lo:lo + 64, n:T:4]
                            k = KA[jb][lo:lo + 64, n:T:4]
                            nk = 128
                            v = [VA[jb][:, 128 * n + lo:128 * n + lo + 64]]
                            mask = c2("causal")[:, 384:512] if g == 1 else c2("dil3")
                            out = PS[jb % 2][lo:lo + 64, n:T:4]
                        ci = 16 * g + 4 * n + h % 4
                        jobs.append(dict(q=q, k=k, nk=nk, v=v, mask=mask, out=out, jb=jb,
                                         lout=LC[:, ci:ci + 1], mout=MC[:, ci:ci + 1]))
                jobs[-1]["then"] = out_of(jb)
            attention(jobs, 64 ** -0.5, lse=True)
            p.fence()
            a = act(LC, LC, ACT.Ln)
            a = tt(LC, LC, MC, ALU.add, a)
            Lg = [TM[0:4, i, :] for i in range(3)]
            toks = []
            for g in range(3):
                for n in range(4):
                    ci = 16 * g + 4 * n
                    t = tr(PS[2 + g][0:4, 128 * n:128 * n + 128], LC[:, ci:ci + 4], ident, a, inc=n == 3)
                if g == 0:
                    toks.append(copy(Lg[0], PS[2][0:4, :], t))
                else:
                    toks.append(copy(Lg[g].rearrange("p (i r) -> p r i", r=4),
                                     PS[2 + g][0:4, :].rearrange("p (r i) -> p r i", r=4), t))
            mx, sm = TM[0:4, 3, :], TM[0:4, 4, :]
            a = tt(mx, Lg[0], Lg[1], ALU.max, toks)
            a = tt(mx, mx, Lg[2], ALU.max, a)
            et = []
            for g in range(3):
                b = tt(Lg[g], Lg[g], mx, ALU.subtract, a)
                et.append(act(Lg[g], Lg[g], ACT.Exp, b))
            a = tt(sm, Lg[0], Lg[1], ALU.add, et)
            a = tt(sm, sm, Lg[2], ALU.add, a)
            a = recip(sm, sm, a)
            et = [tt(Lg[g], Lg[g], sm, ALU.mult, a) for g in range(3)]
            otok = []
            p.fence()
            for jb in range(6):
                g = jb // 2
                s = c2("sel2", 0, 4)[:, 128 * (jb % 2):128 * (jb % 2) + 128]
                b = PS[jb % 2]
                t = mm(b[:, :], s, Lg[g], True, True, et[g], otok[jb - 2] if jb > 1 else None, inc=True)
                a = tt(OB[jb], OB[jb], b[:, :], ALU.mult, t)
                otok.append(split(XH[:, jb, :], XL[:, jb, :], OB[jb], a))
            p.fence()
            bfree.clear()
            return otok

        def fox(xt, r):
            sl = lambda i: AR[:, i, :]
            QZ, KC = [sl(i) for i in range(16)], [sl(16 + i) for i in range(16)]
            VA = [Y[:, i, :] for i in range(8)]
            j = p.now("pe", "act", "dve", "pool")
            zt = p.op("pool", lambda g: g.memset(AR[:, 0:16, :], 0.0), j)
            z1 = fill(AR[64:65, 0:16:2, :], 1.0, zt)
            z2 = fill(AR[0:1, 1:16:2, :], 1.0, zt)
            mask = TM[:, 7, :]
            tmk = p.dma("pool", mask, D["c3"], j)
            first_units("kvf", 3, *XHL, xt)
            b, ps, tok = unit("kvf", *XHL, xt)
            CR = TM[0:16, 6, :]
            rr = [TM[0:16, 3, :], TM[0:16, 4, :], TM[0:16, 5, :], TM[0:16, 0, :], TM[0:16, 1, :]]
            a = act(rr[0], ps[0:16, :], ACT.Identity, tok, j, bias=vec("bf", 0, 1, 0, 16))
            bfree[b] = a
            a = ts(rr[0], rr[0], -1.0, ALU.mult, a)
            c_steps = softplus_steps(rr[0], rr[0], rr[1:5], a)
            kt = {}
            for i in range(8):
                if i == 2:
                    run(c_steps, 2)
                    for v in range(0, 8, 2):
                        v_pair(VA[v:v + 2], "kvf", xt, False)
                        if v < 4:
                            run(c_steps, 4)
                        if v == 4:
                            a = run(c_steps)
                            one = fill(rr[1], 1.0, a)
                            ct = scan(CR, rr[1], rr[0], a, one)
                b, ps, tok = unit("kvf", *XHL, xt)
                bfree[b] = act(KC[2 * i], ps, ACT.Copy, tok, j)
                kt[i] = copy(KC[2 * i + 1], KC[2 * i], bfree[b], e="pool")
            t1 = p.dma("pool", AR[64:65, 16:32:2, :], CR[0:16:2, :], ct, kt.values())
            t2 = p.dma("pool", AR[0:1, 17:32:2, :], CR[1:16:2, :], ct, kt.values())
            xq = rms_apply(X, r, "ng", 32, xw)
            CC = COL[:, 32:96]
            b = next_bank()
            for n in range(4):
                t = mm(PS[b][:, 16 * n:16 * n + 16], CR[:, 128 * n:128 * n + 128], ident[0:16, 0:16], True, True,
                       ct, bfree.get(b), inc=n == 3)
            bfree[b] = ts(CC, PS[b][:, 0:64], -1.0, ALU.mult, t, j)
            first_units("wqb", 3, *XHL, xq)
            for i in range(8):
                b, ps, tok = unit("wqb", *XHL, xq)
                bfree[b] = [act(QZ[2 * i][0:64, :], ps[0:64, :], ACT.Copy, tok, z1, z2, scale=0.125),
                            ts(QZ[2 * i + 1][64:128, :], ps[64:128, :], 0.125, ALU.mult, tok, z1, z2)]
            p.fence(t1, t2, tmk)
            jobs = []
            otok = [None] * 8

            def out_of(jb):
                def then(t):
                    otok[jb] = split(XH[:, jb, :], XL[:, jb, :], PS[jb % 4][:, :], t)
                    for job in jobs:
                        if job["jb"] == jb + 4:
                            job["outfree"] = otok[jb]
                return then

            for jb in range(8):
                for hp in range(2):
                    h = 2 * jb + hp
                    lo = 64 * hp
                    for n in range(4):
                        nk = 128 * (n + 1)
                        jobs.append(dict(
                            q=QZ[h][:, 128 * n:128 * n + 128], k=KC[h][:, 0:nk], nk=nk,
                            cq=CC[:, 16 * n + h:16 * n + h + 1], mask=mask[:, 512 - nk:512],
                            v=[VA[jb][:, 128 * c + lo:128 * c + lo + 64] for c in range(n + 1)],
                            out=PS[jb % 4][lo:lo + 64, 128 * n:128 * n + 128], jb=jb))
                jobs[-1]["then"] = out_of(jb)
            attention(jobs, 1.0)
            p.fence()
            bfree.clear()
            return otok

        def mix_y(name, nk, otok):
            tables()
            yt = []
            first_units(name, 3, XHL[0][:nk], XHL[1][:nk], otok)
            for m in range(8):
                b, ps, tok = unit(name, XHL[0][:nk], XHL[1][:nk], otok)
                yt.append(act(Y[:, m, :], ps, ACT.Copy, tok))
                bfree[b] = yt[-1]
                stat(Y[:, m, :], m, yt[m], False)
            return yt

        def tail(yt, gi, eps):
            _, _, r, _ = stats_end(False, eps)
            return rms_add(r, gi, yt)

        ot = hybrid(xtok)
        mix_out("hwo", 8, ot)
        xt = layer_norm("ln1g", "ln1b", 0)
        p.fence(engines=("act", "dve", "pool"))
        mlp(0, xt)
        xt = layer_norm("ln2g", "ln2b", 0)
        p.fence(engines=("act", "dve", "pool"))
        ot = recurrent(xt)
        mix_out("rwo", 8, ot)
        xt = layer_norm("ln1g", "ln1b", 1)
        p.fence(engines=("act", "dve", "pool"))
        mlp(1, xt)
        r = layer_norm("ln2g", "ln2b", 1, last=True)
        p.fence(engines=("act", "dve", "pool"))
        for l in range(2):
            if l == 0:
                xt = rms_apply(X, r, "ng", 0, xw)
                ot = dilated(xt)
                yt = mix_y("woa", 6, ot)
            else:
                xt = rms_apply(X, r, "kvn", 0, xw)
                ot = fox(xt, r)
                yt = mix_y("wob", 8, ot)
            r = tail(yt, 32 * l + 8, EPS6)
            xt = rms_apply(X, r, "ng", 32 * l + 16, xw)
            p.fence(engines=("act", "dve", "pool"))
            yt = ffn(l, xt)
            _, _, r, _ = stats_end(False, EPS6)
            r = rms_add(r, 32 * l + 24, yt, l == 0)
            p.fence(engines=("act", "dve", "pool"))
        j = p.fence()
        t = p.dma("sp", D["out"].rearrange("(k p) t -> p k t", p=128), X[:, :, :], xw, j)
        for s in p.dlast.values():
            w = p.waits("sp", s)
            p.q["sp"].append((w, None, None))

        block = ctx.enter_context(nc.Block())

        @block.sync
        def _(eng):
            p.play("sp", eng)

        @block.tensor
        def _(eng):
            p.play("pe", eng)

        @block.scalar
        def _(eng):
            p.play("act", eng)

        @block.vector
        def _(eng):
            p.play("dve", eng)

        @block.gpsimd
        def _(eng):
            p.play("pool", eng)


def shape_constants():
    f = np.float32
    idx = np.arange(128)
    small = np.zeros((5, 128, 128), f)
    small[0] = np.eye(128)
    small[1] = 1.0 / 1024
    small[2] = 1.0
    for i in range(128):
        j = i % 64
        if j < 32:
            small[3, i + 32, i] = -1
        else:
            small[3, i - 32, i] = 1
        if j < 8:
            small[4, i + 8, i] = -1
        elif j < 16:
            small[4, i - 8, i] = 1
    small = small.transpose(1, 0, 2).reshape(128, -1)

    def tables(half, theta):
        inv = (f(theta) ** (-np.arange(half, dtype=f) / f(half))).astype(f)
        ang = (np.arange(T, dtype=f)[:, None] * inv[None, :]).astype(f)
        cos, sin = np.ones((64, T), f), np.zeros((64, T), f)
        for k in range(2 * half):
            cos[k] = np.cos(ang[:, k % half])
            sin[k] = np.sin(ang[:, k % half])
        return np.tile(cos, (2, 1)), np.tile(sin, (2, 1))

    NEG = -1e30
    q, k = idx[:, None], idx[None, :]
    k2 = np.arange(256)[None, :]
    dist = q + 128 - k2
    slide = np.where((dist >= 0) & (dist < 128), 0, NEG).astype(f)
    dil1 = np.where((dist >= 0) & (dist <= 128), 0, NEG).astype(f)
    causal = np.zeros((128, 512), f)
    causal[:, 384:] = np.where(k <= q, 0, NEG)
    dil3 = np.where((k <= q) & ((q - k) % 4 == 0), 0, NEG).astype(f)
    j, i = q, k
    mi = (i >= j).astype(f)
    ms = (i > j).astype(f)
    lv = []
    for l in range(7):
        b = 1 << l
        lv.append(((i // (2 * b) == j // (2 * b)) & (i // b % 2 == 1) & (j // b % 2 == 0)).astype(f))
    lv = np.concatenate(lv, 1)
    sel = np.zeros((128, 4, 128), f)
    sel2 = np.zeros((128, 2, 128), f)
    for h in range(4):
        sel[h, h, :] = 1
        sel[32 + h, h, :] = 1
        sel2[h, h // 2, 64 * (h % 2):64 * (h % 2) + 64] = 1
    cos, sin = tables(32, 10000.0)
    c0 = dict(cos=cos, sin=sin, mi=mi, ms=ms, lv=lv, sel=sel.reshape(128, -1), slide=slide)
    cos, sin = tables(8, 500000.0)
    c2 = dict(cos=cos, sin=sin, dil1=dil1, causal=causal, dil3=dil3, sel2=sel2.reshape(128, -1))
    c3 = dict(causal=causal)
    return small, *(np.ascontiguousarray(np.concatenate([c[n] for n, _ in parts], 1), dtype=f)
                    for c, parts in ((c0, C0), (c2, C2), (c3, C3)))


def kernel(**inputs):
    import numpy as _np
    import concourse.bacc as _bacc
    from concourse import mybir as _mybir
    from concourse.bass_utils import run_bass_kernel_spmd as _run

    I = {k: _np.asarray(v) for k, v in inputs.items()}
    f = _np.float32

    def units(w, kb=8):
        K, N = w.shape
        a = w.reshape(K // (128 * kb), kb, 128, N // 128, 128).transpose(0, 3, 2, 1, 4)
        return _np.ascontiguousarray(a).reshape(-1, 128, kb * 128)

    def pad(w, n):
        out = _np.zeros((w.shape[0], n), w.dtype)
        out[:, :w.shape[1]] = w
        return out

    A = {}
    A["x"] = _np.ascontiguousarray(I["x"][0].T)
    w = I["hyb_w_in"][0]
    qa, ka, va, qkv, z, be, al = _np.split(w, [512, 640, 768, 2304, 2816, 2820], axis=1)
    small = _np.zeros((1024, 128), w.dtype)
    small[:, 0:4] = be
    small[:, 32:36] = al
    order = [h for j in range(4) for h in (j, 4 + j)]
    qa = qa.reshape(1024, 8, 64)[:, order].reshape(1024, 512)
    A["hyb"] = units(_np.concatenate([small, qkv, z, qa, ka, va], axis=1))
    w = I["hyb_w_out"][0]
    wa = w[:512].reshape(8, 64, 1024)[order].reshape(512, 1024)
    A["hwo"] = units(_np.concatenate([wa, w[512:]], axis=0))
    for l in range(2):
        A[f"w1_{l}"] = units(I["mlp_w1"][l])
        A[f"w2_{l}"] = units(I["mlp_w2"][l])
        up = I["w_up_2"][l].reshape(1024, 2, 22, 128).transpose(0, 2, 1, 3).reshape(1024, 5632)
        A[f"up_{l}"] = units(up)
        A[f"dn8_{l}"] = units(I["w_down_2"][l][:2048])
        A[f"dn6_{l}"] = units(I["w_down_2"][l][2048:], 6)
    A["rin"] = units(I["rec_w_in"][0])
    g = []
    for w in (I["rec_w_a"][0], I["rec_w_x"][0]):
        a = w.reshape(4, 2, 128, 2, 128).transpose(0, 3, 2, 1, 4).reshape(2, 4, 128, 256)
        g.append(a.transpose(0, 2, 1, 3).reshape(2, 128, 1024))
    A["rwg"] = _np.ascontiguousarray(_np.stack(g, 1).reshape(4, 128, 1024))
    A["rwo"] = units(I["rec_w_out"][0])
    w = I["w_qkv_a_2"][0]
    A["qkv"] = units(_np.concatenate([w[:, :384], w[:, 1536:], w[:, 384:1536]], axis=1))
    A["woa"] = units(I["w_o_a_2"][0], 6)
    w = I["w_kvf_2"]
    A["kvf"] = units(_np.concatenate([pad(w[:, 2048:], 128), w[:, :256], w[:, 1024:2048], w[:, 256:1024]], axis=1))
    A["wqb"] = units(I["w_q_b_2"][0])
    A["wob"] = units(I["w_o_b_2"][0])

    def cols(v):
        return _np.ascontiguousarray(v.reshape(-1, 128).T)

    def taps(v):
        return v.reshape(v.shape[0], -1, 128).transpose(2, 1, 0).reshape(128, -1)

    def at(v, lo):
        out = _np.zeros((128, 1), f)
        out[lo:lo + v.shape[0], 0] = v
        return out

    V = dict(
        ln1g=cols(I["ln1_g"]), ln1b=cols(I["ln1_b"]), ln2g=cols(I["ln2_g"]), ln2b=cols(I["ln2_b"]),
        ng=cols(I["norm_gains_2"]), kvn=cols(I["kv_norm_2"]), hcw=taps(I["hyb_conv_w"][0]),
        hnw=cols(I["hyb_norm_w"]), sink=_np.repeat(I["hyb_sinks"][0][None], 128, 0),
        alog=at(I["hyb_a_log"][0], 32), dtb=at(I["hyb_dt_bias"][0], 32),
        rcw=taps(I["rec_conv_w"][0]), rcb=cols(I["rec_conv_b"]), rba=cols(I["rec_b_a"]),
        rbx=cols(I["rec_b_x"]), lam=cols(I["rec_lambda"]), bf=at(I["b_f_2"], 0),
        fcw=_np.concatenate([taps(I["conv_w_2"][l]) for l in range(2)], 1), fcb=cols(I["conv_b_2"]),
    )
    A["vec"] = _np.ascontiguousarray(_np.concatenate([V[n] for n, _ in VEC_SIZES], 1))
    A["small"], A["c0"], A["c2"], A["c3"] = shape_constants()

    nc = _bacc.Bacc("TRN2", target_bir_lowering=False, num_devices=1)
    D, arrays = {}, {}
    for name, a in A.items():
        arrays[f"in_{name}"] = a
        D[name] = nc.dram_tensor(f"in_{name}", a.shape, _mybir.dt.from_np(a.dtype), kind="ExternalInput").ap()
    D["out"] = nc.dram_tensor("out_x", (1024, T), F, kind="ExternalOutput").ap()
    build_program(nc, D)
    r = _run(nc, [arrays], core_ids=[0])
    return _np.ascontiguousarray(r.results[0]["out_x"].T)[None]
```

```python
import numpy as np
import concourse.bass as bass
from concourse import mybir
from contextlib import ExitStack
from functools import partial

F = mybir.dt.float32
R = mybir.dt.float32r
B16 = mybir.dt.bfloat16
ACT = mybir.ActivationFunctionType
ALU = mybir.AluOpType
AXX = mybir.AxisListType.X

T = 512
ALPHA = 4 ** 0.25

VEC_SIZES = [
    ("ln1g", 16), ("ln1b", 16), ("ln2g", 16), ("ln2b", 16), ("ng", 64), ("kvn", 8),
    ("hcw", 48), ("hnw", 1), ("sink", 8), ("alog", 1), ("dtb", 1),
    ("rcw", 32), ("rcb", 8), ("rba", 8), ("rbx", 8), ("lam", 8),
    ("bf", 1), ("fcw", 264), ("fcb", 88),
]
VEC_AT = {}
_n = 0
for _name, _k in VEC_SIZES:
    VEC_AT[_name] = _n
    _n += _k
NVEC = _n

SMALL = ["ident", "onesd", "ones", "rot1", "rot2", "causal"]
C0 = [("cos", 512), ("sin", 512), ("mi", 128), ("ms", 128), ("lv", 896), ("sel", 512), ("slide", 256)]
C2 = [("cos", 512), ("sin", 512), ("dil1", 256), ("dil3", 128), ("sel2", 256)]


def places(parts):
    at, out = 0, {}
    for name, k in parts:
        out[name] = (at, k)
        at += k
    return out, at


def plan_units():
    plan = [("hyb", i, 8) for i in range(23)] + [("hwo", i, 8) for i in range(8)]

    def mlp(l):
        out = []
        for q in range(4):
            out += [(f"w1_{l}", q * 8 + m, 8) for m in range(8)]
            out += [(f"w2_{l}", q * 8 + m, 8) for m in range(8)]
        return out

    def ffn(l):
        out = []
        for q, n in enumerate((8, 8, 6)):
            out += [(f"up_{l}", 2 * (q * 8 + i) + s, 8) for i in range(n) for s in range(2)]
            out += [(f"dn{n}_{l}", (q * 8 if n == 8 else 0) + m, n) for m in range(8)]
        return out

    plan += mlp(0)
    plan += [("rin", i, 8) for i in range(8)] + [("rwg", i, 8) for i in range(4)]
    plan += [("rin", i, 8) for i in range(8, 16)]
    plan += [("rwo", i, 8) for i in range(8)]
    plan += mlp(1)
    plan += [("qkv", i, 8) for i in range(18)] + [("woa", i, 6) for i in range(8)]
    plan += ffn(0)
    plan += [("kvf", i, 8) for i in range(17)] + [("wqb", i, 8) for i in range(8)]
    plan += [("wob", i, 8) for i in range(8)]
    plan += ffn(1)
    return plan


class Program:

    def __init__(self, sems, dsems):
        self.sems = sems
        self.dsems = dsems
        self.q = {e: [] for e in ("pe", "act", "dve", "pool", "sp")}
        self.count = {e: 0 for e in self.q}
        self.seen = {e: {} for e in self.q}
        self.ndma = {"sp": 0, "pool": 0}
        self.dlast = {}

    def waits(self, e, after):
        out = []
        for t in flat(after):
            if self.seen[e].get(t[0], 0) < t[1]:
                self.seen[e][t[0]] = t[1]
                out.append(t)
        return out

    def op(self, e, fn, *after, inc=True):
        w = self.waits(e, after)
        if inc:
            self.count[e] += 1
        self.q[e].append((w, fn, (e, 1) if inc else None))
        return (e, self.count[e]) if inc else None

    def dma(self, e, out, in_, *after):
        ring = self.dsems[e]
        s = ring[self.ndma[e] % len(ring)]
        self.ndma[e] += 1
        before = self.dlast.get(s)
        w = self.waits(e, [after, before or []])
        self.dlast[s] = (s, (before[1] if before else 0) + 16)
        self.q[e].append((w, lambda g: g.dma_start(out, in_), (s, 16)))
        return self.dlast[s]

    def now(self, *engines):
        return [(e, self.count[e]) for e in engines if self.count[e]]

    def fence(self, *also, engines=("pe", "act", "dve", "pool")):
        j = self.now("pe", "act", "dve", "pool") + list(flat(also))
        for e in engines:
            w = self.waits(e, j)
            if w:
                self.q[e].append((w, None, None))
        return j

    def play(self, e, eng):
        for w, fn, inc in self.q[e]:
            for s, v in w:
                eng.wait_ge(self.sems[s], v)
            if fn is None:
                continue
            ins = fn(eng)
            if inc is not None:
                ins.then_inc(self.sems[inc[0]], inc[1])


def flat(x):
    if x is None:
        return
    if isinstance(x, tuple) and len(x) == 2 and isinstance(x[0], str):
        yield x
        return
    for y in x:
        yield from flat(y)


def build_program(nc, D):
    with ExitStack() as ctx:
        def sb(name, shape, dt=F):
            return ctx.enter_context(nc.sbuf_tensor(name, shape, dt))

        names = ["pe", "act", "dve", "pool"] + [f"ds{i}" for i in range(12)] + [f"dp{i}" for i in range(6)]
        sems = {n: ctx.enter_context(nc.semaphore("s_" + n)) for n in names}
        p = Program(sems, {"sp": [f"ds{i}" for i in range(12)], "pool": [f"dp{i}" for i in range(6)]})

        NRAW, NW = 3, 4
        RAW = sb("RAW", [128, NRAW, 2, 1024])
        WH = sb("WH", [128, NW, 1024], R)
        WL = sb("WL", [128, NW, 1024], R)
        X = sb("X", [128, 8, T])
        with nc.sbuf_tensor("XH", [128, 8, T], R) as XH, nc.sbuf_tensor("XL", [128, 8, T], R) as XL:
            pass
        XF = sb("XF", [128, 16, T])
        Y = sb("Y", [128, 8, T])
        TM = sb("TM", [128, 8, T])
        VEC = sb("VEC", [128, NVEC])
        CST = sb("CST", [128, len(SMALL) * 128])
        COL = sb("COL", [128, 256])
        identb = sb("IDB", [128, 128], B16)[:, :]
        causal = sb("CSL", [128, 128], B16)[:, :]
        with nc.sbuf_tensor("H", [128, 32, T], R) as H:
            pass
        AR = sb("AR", [128, 32, T])
        PS = [ctx.enter_context(nc.psum_tensor(f"ps{i}", [128, T], F)) for i in range(8)]

        cst = {n: CST[:, 128 * i:128 * i + 128] for i, n in enumerate(SMALL)}
        ident, ones, onesd = cst["ident"], cst["ones"], cst["onesd"]

        def vec(name, i=0, n=1, lo=0, hi=128):
            a = VEC_AT[name] + i
            return VEC[lo:hi, a:a + n]

        def act(out, in_, func, *after, scale=1.0, bias=0.0, accum=None):
            def go(g):
                kw = {} if accum is None else {"accum_out": accum}
                return g.activation(out, in_, func, bias=bias, scale=scale, **kw)
            return p.op("act", go, *after)

        def tt(out, a, b, op, *after, e="dve"):
            return p.op(e, lambda g: g.tensor_tensor(out, a, b, op), *after)

        def ts(out, a, s1, op0, *after, s2=None, op1=ALU.bypass, e="dve"):
            return p.op(e, lambda g: g.tensor_scalar(out, a, s1, s2, op0, op1), *after)

        def stt(out, a, s, b, op0, op1, *after):
            return p.op("dve", lambda g: g.scalar_tensor_tensor(out, a, s, b, op0, op1), *after)

        def copy(out, a, *after, e="dve"):
            return p.op(e, lambda g: g.tensor_copy(out, a), *after)

        def mm(out, lhsT, rhs, start, stop, *after, inc=False):
            return p.op("pe", lambda g: g.matmul(out, lhsT, rhs, start=start, stop=stop), *after, inc=inc)

        def tr(out, in_, idn, *after, inc=False):
            return p.op("pe", lambda g: g.transpose(out, in_, idn), *after, inc=inc)

        def scan(out, a, b, *after):
            return p.op("dve", lambda g: g.tensor_tensor_scan(out, a, b, 0.0, ALU.mult, ALU.add), *after)

        def recip(out, a, *after):
            return p.op("dve", lambda g: g.reciprocal(out, a), *after)

        def rmax(out, a, *after, negate=False):
            return p.op("dve", lambda g: g.reduce_max(out, a, AXX, negate=negate), *after)

        def fill(out, value, *after):
            return p.op("dve", lambda g: g.memset(out, value), *after)

        def f32(ap):
            return ap.bitcast(F)

        def split(h, l, src, *after):
            a = act(h, src, ACT.Copy, *after)
            return [a, tt(l, src, f32(h), ALU.subtract, a, *after)]

        PLAN = plan_units()
        groups, i = [], 0
        while i < len(PLAN):
            name, at, kb = PLAN[i]
            two = i + 1 < len(PLAN) and PLAN[i + 1] == (name, at + 1, kb)
            groups.append((name, at, kb, i, 2 if two else 1))
            i += 2 if two else 1
        where = {}
        for gi, (name, at, kb, u, n) in enumerate(groups):
            for k in range(n):
                where[u + k] = (gi, k)
        gtok, gread = {}, {}
        wtok = {}
        wfree = {}
        nx = {"group": 0, "split": 0, "unit": 0}

        def load_group():
            gi = nx["group"]
            if gi >= len(groups):
                return
            nx["group"] += 1
            name, at, kb, u, n = groups[gi]
            free = gread.get(gi - NRAW)
            dst = RAW[:, gi % NRAW, 0:n, 0:kb * 128]
            src = D[name][at:at + n, :, :].rearrange("u p c -> p u c")
            if gi == 0:
                gtok[gi] = [p.dma("sp", dst[:, i:i + 1, :], src[:, i:i + 1, :]) for i in range(n)]
            else:
                gtok[gi] = [p.dma("sp", dst, src, free)] * n

        def split_unit(u):
            if u >= len(PLAN):
                return
            gi, k = where[u]
            kb = PLAN[u][2]
            s = u % NW
            src = RAW[:, gi % NRAW, k, 0:kb * 128]
            wtok[u] = split(WH[:, s, 0:kb * 128], WL[:, s, 0:kb * 128], src, gtok[gi][k], wfree.get(s))
            if k == groups[gi][4] - 1:
                gread[gi] = wtok[u]
                load_group()


        def split_to(n):
            while nx["split"] < min(n, len(PLAN)):
                split_unit(nx["split"])
                nx["split"] += 1

        def next_unit(name):
            u = nx["unit"]
            assert PLAN[u][0] == name, (PLAN[u], name)
            nx["unit"] += 1
            split_to(u + NW)
            return u

        bank = {"n": 0}
        bfree = {}

        def next_bank(n=4):
            b = bank["n"] % n
            bank["n"] += 1
            return b

        together = []

        def side_by_side(name, n, xh, xl, xtok, banks=None):
            u0 = nx["unit"]
            split_to(u0 + NW)
            nx["unit"] += n
            kb = PLAN[u0][2]
            banks = banks or [next_bank() for _ in range(n)]
            toks = {}
            for k in range(kb):
                for i in range(n):
                    u, b = u0 + i, banks[i]
                    assert PLAN[u][0] == name and PLAN[u][2] == kb
                    s = u % NW
                    out = PS[b][:, :]
                    wh, wl = WH[:, s, 128 * k:128 * k + 128], WL[:, s, 128 * k:128 * k + 128]
                    mm(out, wh, xh[k], k == 0, False, wtok[u] if k == 0 else None, bfree.get(b) if k == 0 else None, xtok[k])
                    mm(out, wh, xl[k], False, False)
                    toks[i] = mm(out, wl, xh[k], False, k == kb - 1, inc=k == kb - 1)
                    wfree[s] = toks[i]
                    if (k, i) != (kb - 1, n - 1):
                        yield
            for i in range(n):
                together.append((u0 + i, name, banks[i], PS[banks[i]][:, :], toks[i]))

        def first_units(*args):
            run(side_by_side(*args))

        def unit(name, xh, xl, xtok):
            if together:
                got = together.pop(0)
                assert got[1] == name
                split_to(got[0] + 1 + NW)
                return got[2:]
            u = next_unit(name)
            kb, s = PLAN[u][2], u % NW
            b = next_bank()
            out = PS[b][:, :]
            tok = None
            for k in range(kb):
                wh, wl = WH[:, s, 128 * k:128 * k + 128], WL[:, s, 128 * k:128 * k + 128]
                mm(out, wh, xh[k], k == 0, False, wtok[u] if k == 0 else None, bfree.get(b) if k == 0 else None, xtok[k])
                mm(out, wh, xl[k], False, False)
                tok = mm(out, wl, xh[k], False, k == kb - 1, inc=k == kb - 1)
            wfree[s] = tok
            return b, out, tok

        def unit_tok(name, n, xtok, strided):
            us = [next_unit(name)]
            if n == 2:
                us.append(us[0] + 1)
                assert PLAN[us[1]][0] == name and us[0] % 2 == 0
                nx["unit"] += 1
            s = us[0] % NW
            bs = [next_bank() for _ in range(n)]
            tok = None
            w = 128 * n
            for t in range(4):
                b = bs[t * n // 4]
                c = w * (t % (4 // n))
                out = PS[b][:, c:c + w]
                for k in range(8):
                    tk = slice(t, T, 4) if strided else slice(128 * t, 128 * t + 128)
                    wh = WH[:, s:s + n, 128 * k:128 * k + 128]
                    wl = WL[:, s:s + n, 128 * k:128 * k + 128]
                    mm(out, XH[:, k, tk], wh, k == 0, False, [wtok[u] for u in us] if t == k == 0 else None,
                       bfree.get(b) if k == 0 else None, xtok[k])
                    mm(out, XL[:, k, tk], wh, False, False)
                    tok = mm(out, XH[:, k, tk], wl, False, k == 7, inc=t == 3 and k == 7)
            for u in us:
                wfree[u % NW] = tok
            split_to(us[-1] + NW)
            return bs, tok

        def v_pair(dst, name, xtok, strided):
            bs, tok = unit_tok(name, 2, xtok, strided)
            for i, b in enumerate(bs):
                src = PS[b][:, :].rearrange("p (t n c) -> p t n c", t=2, n=2)
                bfree[b] = [act(dst[n][:, 256 * i:256 * i + 256].rearrange("p (t c) -> p t c", t=2),
                                src[:, :, n, :], ACT.Copy, tok) for n in range(2)]

        XHL = [XH[:, k, :] for k in range(8)], [XL[:, k, :] for k in range(8)]

        def tables():
            p.op("act", lambda g: g.preload_act_table_set("natural_log_exp_and_others"), inc=False)

        st = {}

        def stat(y, m, tok, mean):
            S1, S2 = TM[:, 0, :], TM[:, 1, :]
            if m == 0:
                st["s2"] = act(S2, y, ACT.Square, tok, st.get("free"))
                st["s1"] = copy(S1, y, tok, st.get("free"), e="pool") if mean else None
                st["sq"] = {}
                return
            sq = TM[:, 6 + m % 2, :]
            a = act(sq, y, ACT.Square, tok, st["sq"].get(m % 2), st.get("sqfree") if m < 3 else None)
            st["s2"] = tt(S2, S2, sq, ALU.add, a, st["s2"])
            st["sq"][m % 2] = st["s2"]
            if mean:
                st["s1"] = tt(S1, S1, y, ALU.add, tok, st["s1"], e="pool" if m < 7 else "dve")

        def rstd_of(out, var_psum, scale, eps, *after):
            a = act(out, var_psum, ACT.Ln, *after, bias=eps, scale=scale)
            return act(out, out, ACT.Exp, a, scale=-0.5)

        def busy(n):
            for _ in range(n):
                mm(PS[7][:, 0:128], ident, ident, True, True)

        def stats_end(mean, eps_col):
            busy(8)
            S1, S2, RS = TM[:, 0, :], TM[:, 1, :], TM[:, 2, :]
            b2 = next_bank()
            if mean:
                b1 = next_bank()
                t1 = mm(PS[b1][:, :], onesd, S1, True, True, st["s1"], bfree.get(b1), inc=True)
            t2 = mm(PS[b2][:, :], onesd, S2, True, True, st["s2"], bfree.get(b2), inc=True)
            busy(24 if mean else 18)
            if not mean:
                r = rstd_of(RS, PS[b2][:, :], 1.0, eps_col, t2)
                bfree[b2] = r
                st["free"] = t2
                return None, [], r, None
            a = act(S1, PS[b1][:, :], ACT.Square, t1)
            v = tt(S2, PS[b2][:, :], S1, ALU.subtract, a, t2)
            bfree[b2] = v
            v2 = ts(S2, S2, 0.0, ALU.max, v)
            r = rstd_of(RS, S2, 1.0, eps_col, v2)
            st["free"] = [r]
            return PS[b1][:, :], t1, r, b1

        def layer_norm(gname, bname, l, last=False):
            M, mt, r, b1 = stats_end(True, EPS5)
            RS = TM[:, 2, :]
            pe = p.now("pe")
            toks, A1, A2, A3, A4, A5 = [None] * 8, {}, {}, {}, {}, {}
            b = next_bank() if last else None
            for i in range(10):
                if i < 8:
                    t = TM[:, 3 + i % 3, :]
                    A1[i] = tt(t, X[:, i, :], M, ALU.subtract, mt, xw[i], A3.get(i - 3))
                    A2[i] = tt(t, t, RS, ALU.mult, A1[i], r, e="pool")
                    if i == 7:
                        bfree[b1] = A1[i]
                m = i - 1
                if 0 <= m < 8:
                    t = TM[:, 3 + m % 3, :]
                    kw = dict(scale=vec(gname, 8 * l + m), bias=vec(bname, 8 * l + m))
                    if not last:
                        toks[m] = [act(XH[:, m, :], t, ACT.Identity, A2[m], pe, **kw)]
                    A3[m] = xw[m] = act(X[:, m, :], t, ACT.Identity, A2[m], **kw)
                    if last:
                        sq = TM[:, 6 + m % 2, :]
                        A4[m] = act(sq, X[:, m, :], ACT.Square, xw[m], A5.get(m - 2))
                        A5[m] = mm(PS[b][:, :], onesd, sq, m == 0, m == 7, A4[m], bfree.get(b), inc=True)
                m = i - 2
                if 0 <= m < 8 and not last:
                    toks[m].append(tt(XL[:, m, :], X[:, m, :], f32(XH[:, m, :]), ALU.subtract, toks[m][0], xw[m], pe))
            if last:
                busy(12)
                r = rstd_of(RS, PS[b][:, :], 1.0, EPS6, A5[7], A2[7])
                bfree[b] = r
                return r
            return toks

        def rms_apply(src, r, gname, gi, srctok):
            RS = TM[:, 2, :]
            pe = p.now("pe")
            toks, A1 = [None] * 8, {}
            for i in range(10):
                if i < 8:
                    t = TM[:, 3 + i % 3, :]
                    A1[i] = stt(t, src[:, i, :], vec(gname, gi + i), RS, ALU.mult, ALU.mult, r, srctok[i],
                                toks[i - 3] if i > 2 else None)
                    toks[i] = [act(XH[:, i, :], t, ACT.Copy, A1[i], pe)]
                m = i - 2
                if 0 <= m < 8:
                    t = TM[:, 3 + m % 3, :]
                    toks[m].append(tt(XL[:, m, :], t, f32(XH[:, m, :]), ALU.subtract, toks[m][0], pe))
            return toks

        def rms_add(r, gi, ytok, with_stats=True):
            RS = TM[:, 2, :]
            b = next_bank()
            A1, A2, A3, A4 = {}, {}, {}, {}
            for i in range(11):
                if i < 8:
                    t = TM[:, 3 + i % 3, :]
                    A1[i] = stt(t, Y[:, i, :], vec("ng", gi + i), RS, ALU.mult, ALU.mult, r, ytok[i], A2.get(i - 3))
                    A2[i] = xw[i] = tt(X[:, i, :], X[:, i, :], t, ALU.add, A1[i], xw[i], e="pool" if i in (1, 3, 5) else "dve")
                m = i - 2
                if with_stats and 0 <= m < 8:
                    sq = TM[:, 6 + m % 2, :]
                    A3[m] = act(sq, X[:, m, :], ACT.Square, xw[m], A4.get(m - 2))
                    A4[m] = mm(PS[b][:, :], onesd, sq, m == 0, m == 7, A3[m], bfree.get(b), inc=True)
                    if m == 7:
                        busy(12)
            if not with_stats:
                return None
            r2 = rstd_of(RS, PS[b][:, :], 1.0, EPS6, A4[7], A1[7])
            bfree[b] = r2
            return r2

        def rms_add_on(r, gi, ytok, gj, name):
            p.fence(engines=("act", "dve", "pool"))
            RS = TM[:, 2, :]
            pe = p.now("pe")
            b = next_bank()
            xt = [None] * 8
            beside = side_by_side(name, 3, *XHL, xt)
            A1, A2, A3, A4 = {}, {}, {}, {}
            for i in range(10):
                if i < 8:
                    t = TM[:, 3 + i % 3, :]
                    A1[i] = stt(t, Y[:, i, :], vec("ng", gi + i), RS, ALU.mult, ALU.mult, r, ytok[i], A2.get(i - 3))
                    A2[i] = xw[i] = tt(X[:, i, :], X[:, i, :], t, ALU.add, A1[i], xw[i], e="pool" if i in (2, 4, 6) else "dve")
                m = i - 1
                if 0 <= m < 8:
                    xt[m] = [act(XH[:, m, :], X[:, m, :], ACT.Copy, xw[m], pe, scale=vec("ng", gj + m))]
                    sq = TM[:, 6 + m % 2, :]
                    A3[m] = act(sq, X[:, m, :], ACT.Square, xw[m], A4.get(m - 2))
                m = i - 2
                if 0 <= m < 8:
                    xt[m].append(stt(XL[:, m, :], X[:, m, :], vec("ng", gj + m), f32(XH[:, m, :]), ALU.mult,
                                     ALU.subtract, xt[m][0], xw[m], pe))
                    run(beside, 3 if m < 7 else None)
                    A4[m] = mm(PS[b][:, :], onesd, TM[:, 6 + m % 2, :], m == 0, m == 7, A3[m], bfree.get(b), inc=True)
            r2 = rstd_of(RS, PS[b][:, :], 1.0, EPS6, A4[7], A1[7])
            bfree[b] = r2
            return r2, xt

        xw = [None] * 8
        xin = D["x"].rearrange("(k p) t -> p k t", p=128)
        xw[0] = p.dma("sp", X[:, 0:1, :], xin[:, 0:1, :])
        load_group()
        for m in range(1, 8):
            xw[m] = p.dma("sp", X[:, m:m + 1, :], xin[:, m:m + 1, :])
        for _ in range(NRAW - 1):
            load_group()
        t_vec = p.dma("pool", VEC[:, :], D["vec"])
        t_cst = p.dma("pool", CST[:, :], D["small"])
        EPS5, EPS6 = COL[:, 254:255], COL[:, 255:256]
        e1 = fill(EPS5, 1e-5)
        e2 = fill(EPS6, 1e-6)
        split_to(2)
        xtok = [split(XH[:, m, :], XL[:, m, :], X[:, m, :], xw[m]) for m in range(8)]
        tcb = [act(identb, ident, ACT.Copy, t_cst), act(causal, cst["causal"], ACT.Copy, t_cst)]
        at0, n0 = places(C0)
        Yf = Y[:, :, :].rearrange("p a b -> p (a b)")
        ARf = AR[:, :, :].rearrange("p a b -> p (a b)")
        t_c0 = p.dma("pool", Yf[:, 0:n0], D["c0"], xw[7])

        def hold(e, *toks):
            w = p.waits(e, toks)
            p.q[e].append((w, None, None))

        def c_of(base, at, name, lo=0, hi=128):
            a, k = at[name]
            return base[lo:hi, a:a + k]

        def softplus_steps(out, x, tmp, *after):
            u, w, l, d = tmp
            a = act(u, x, ACT.Abs, *after)
            yield
            a = act(u, u, ACT.Exp, a, scale=-1.0)
            yield
            b = ts(w, u, 1.0, ALU.add, a)
            yield
            a = act(l, w, ACT.Ln, b)
            yield
            b = ts(d, w, -1.0, ALU.add, b)
            c = ts(w, d, 0.0, ALU.is_equal, b, a)
            yield
            e = tt(l, l, w, ALU.add, a, c)
            f = tt(d, d, w, ALU.add, c)
            yield
            f = recip(d, d, f)
            yield
            e = tt(l, l, d, ALU.mult, e, f)
            yield
            e = tt(l, l, u, ALU.mult, e)
            yield
            yield stt(out, x, 0.0, l, ALU.max, ALU.add, e, *after)

        def run(steps, n=None):
            last = None
            while n is None or n > 0:
                try:
                    last = next(steps)
                except StopIteration:
                    break
                n = None if n is None else n - 1
            return last

        def conv_psum(dst, ps, w, taps, first, *after):
            a = act(dst, ps, ACT.Identity, *after, scale=w(taps - 1), bias=first)
            for j in range(taps - 2, -1, -1):
                s = taps - 1 - j
                a = stt(dst[:, s:T], ps[:, 0:T - s], w(j), dst[:, s:T], ALU.mult, ALU.add, a, *after)
            return a

        def rope(dst, ps, tok, rot, cos, sin, tmp, tmpfree, b, scale):
            a = act(dst, ps, ACT.Copy, tok, scale=scale)
            b2 = next_bank()
            t = mm(PS[b2][:, :], rot, dst, True, True, a, bfree.get(b2), inc=True)
            d = tt(tmp, PS[b2][:, :], sin, ALU.mult, t, tmpfree)
            bfree[b] = a
            bfree[b2] = d
            e = tt(dst, dst, cos, ALU.mult, a, t, e="pool")
            return tt(dst, dst, tmp, ALU.add, d, e)

        def attention(jobs, sbanks, tbanks, lse=False):
            n, ns, nt = len(jobs), len(sbanks), len(tbanks)
            S = {}

            def col(i, k):
                return COL[:, 8 * (i % 3) + k:8 * (i % 3) + k + 1]

            def scores(i):
                return PS[sbanks[i % ns]][:, 0:jobs[i]["nk"]]

            def A(i):
                j = jobs[i]
                nk, w = j["nk"], j["mask"].shape[1]
                mm(scores(i), j["q"], j["k"], True, False, j.get("after"), S.get(("c", i - ns)), S.get(("b", i - ns)))
                S[("a", i)] = mm(scores(i)[:, nk - w:nk], identb, j["mask"], False, True, inc=True)

            def B(i):
                j = jobs[i]
                free = S.get(("c", i - 3)), S.get(("dd", i - 3))
                if "sink" in j:
                    b = rmax(col(i, 4), scores(i), S[("a", i)], *free)
                    S[("b", i)] = ts(col(i, 0), col(i, 4), j["sink"], ALU.max, b, *free, s2=-1.0, op1=ALU.mult)
                else:
                    S[("b", i)] = rmax(col(i, 0), scores(i), S[("a", i)], *free, negate=True)

            def C(i):
                j = jobs[i]
                free = S.get(("d", i - 3)), S.get(("e", i - 3))
                S[("c", i)] = act(TM[:, i % 3, 0:j["nk"]], scores(i), ACT.Exp, S[("b", i)], *free, bias=col(i, 0), accum=col(i, 1))
                if "sink" in j:
                    S[("c", i)] = act(col(i, 2), j["sink"], ACT.Exp, S[("b", i)], *free, bias=col(i, 0))

            def Dn(i):
                j = jobs[i]
                t = TM[:, i % 3, 0:j["nk"]]
                a = S[("c", i)]
                if "sink" in j:
                    a = tt(col(i, 1), col(i, 1), col(i, 2), ALU.add, a)
                if lse:
                    copy(j["lout"], col(i, 1), a)
                    S[("dd", i)] = ts(j["mout"], col(i, 0), -1.0, ALU.mult, S[("b", i)])
                a = recip(col(i, 3), col(i, 1), a)
                S[("d", i)] = ts(t, t, col(i, 3), ALU.mult, a)

            def E_(i):
                nb = jobs[i]["nk"] // 128
                t = None
                for x in range(nb):
                    t = tr(PS[tbanks[i % nt]][:, 128 * x:128 * x + 128], TM[:, i % 3, 128 * x:128 * x + 128], ident,
                           S[("d", i)], S.get(("f", i - nt)), inc=x == nb - 1)
                S[("e", i)] = t

            def F_(i):
                nk = jobs[i]["nk"]
                S[("f", i)] = act(TM[:, 3 + i % 2, 0:nk], PS[tbanks[i % nt]][:, 0:nk], ACT.Copy, S[("e", i)], S.get(("g", i - 2)))

            def G(i):
                j = jobs[i]
                nb = j["nk"] // 128
                t = None
                for x in range(nb):
                    t = mm(j["out"], j["v"][x], TM[:, 3 + i % 2, 128 * x:128 * x + 128], x == 0, x == nb - 1,
                           S[("f", i)], j.get("outfree"), inc=x == nb - 1)
                S[("g", i)] = t

            for i in range(ns - 1):
                A(i)
            for i in range(n + 3):
                if 0 <= i - 2 < n:
                    E_(i - 2)
                    F_(i - 2)
                if 0 <= i - 3 < n:
                    G(i - 3)
                if i + ns - 1 < n:
                    A(i + ns - 1)
                if i < n:
                    B(i)
                    C(i)
                if 0 <= i - 1 < n:
                    Dn(i - 1)
                if 0 <= i - 3 < n and "then" in jobs[i - 3]:
                    jobs[i - 3]["then"](S[("g", i - 3)])
                yield

        def mix_out(name, nk, otok, ahead=None):
            if ahead is None:
                tables()
            run(ahead or side_by_side(name, 3, XHL[0][:nk], XHL[1][:nk], otok))
            for m in range(8):
                b, ps, tok = unit(name, XHL[0][:nk], XHL[1][:nk], otok)
                xw[m] = stt(X[:, m, :], X[:, m, :], ALPHA, ps, ALU.mult, ALU.add, tok, xw[m])
                bfree[b] = xw[m]
                stat(X[:, m, :], m, xw[m], True)

        def mlp(l, xt):
            hfree = {}
            rfree = {}
            first_units(f"w1_{l}", 3, *XHL, xt)
            for q in range(4):
                ht = []
                o = 16 * (q % 2)
                for m in range(8):
                    b, ps, tok = unit(f"w1_{l}", *XHL, xt)
                    r, h = TM[:, 2 + m % 2, :], TM[:, 4 + m % 2, :]
                    hh, hl = H[:, o + m, :], H[:, o + 8 + m, :]
                    a = act(r, ps, ACT.Relu, tok, rfree.get(m % 2))
                    c = stt(h, ps, 0.0, r, ALU.max, ALU.mult, a, rfree.get(("h", m % 2)))
                    bfree[b] = c
                    d = act(hh, h, ACT.Copy, c, hfree.get(q - 2))
                    e = tt(hl, h, f32(hh), ALU.subtract, d, hfree.get(q - 2))
                    rfree[m % 2] = c
                    rfree[("h", m % 2)] = [e, d]
                    ht.append(e)
                hl_ = [H[:, o + k, :] for k in range(8)], [H[:, o + 8 + k, :] for k in range(8)]
                for m in range(8):
                    b, ps, tok = unit(f"w2_{l}", *hl_, ht)
                    if q == 0:
                        xw[m] = stt(X[:, m, :], X[:, m, :], ALPHA, ps, ALU.mult, ALU.add, tok, xw[m])
                    else:
                        xw[m] = tt(X[:, m, :], X[:, m, :], ps, ALU.add, tok, xw[m])
                    bfree[b] = xw[m]
                    if q == 3:
                        stat(X[:, m, :], m, xw[m], True)
                hfree[q] = tok

        def ffn(l, xt, r2):
            hfree, rfree, ufree = {}, {}, {}
            RS = TM[:, 2, :]
            older, later = [], []

            def taps(dst, u, w, a, c, s):
                for j in (1, 0):
                    a = stt(dst[:, 2 - j:T], u[:, 0:T + j - 2], w(j), dst[:, 2 - j:T], ALU.mult, ALU.add, a)
                ufree[s] = a
                c.append(a)

            def finish(g, v, c, at, par, q, ht):
                hh, hl = H[:, at, :], H[:, at + 8, :]
                a = act(g, g, ACT.Gelu_apprx_tanh, c[0])
                a = tt(g, g, v, ALU.mult, a, c[1], e="pool" if len(ht) < shared[q] else "dve")
                d = act(hh, g, ACT.Copy, a, hfree.get(q - 2))
                e = tt(hl, g, f32(hh), ALU.subtract, d, hfree.get(q - 2))
                rfree[par] = e
                ht.append(e)

            shared = (7, 7, 5)
            yt = [None] * 8
            i = 0
            for q, n in enumerate((8, 8, 6)):
                ht = []
                o = 16 * (q % 2)
                for m in range(n):
                    par = i % 2
                    pair = (TM[:, 3, :], TM[:, 4, :]) if par else (TM[:, 5, :], TM[:, 0, :])
                    c = []
                    for s in range(2):
                        blk = 22 * s + q * 8 + m
                        b, ps, tok = unit(f"up_{l}", *XHL, xt)
                        w = lambda j, blk=blk: vec("fcw", 132 * l + 3 * blk + j)
                        u = TM[:, 6 + s, :]
                        bfree[b] = tt(u, ps, RS, ALU.mult, tok, r2, ufree.get(s))
                        a = act(pair[s], u, ACT.Identity, bfree[b], rfree.get(par), scale=w(2), bias=vec("fcb", 44 * l + blk))
                        if older:
                            older.pop()()
                        older.append(partial(taps, pair[s], u, w, a, c, s))
                        if s == 1:
                            if m == n - 1:
                                older.pop()()
                            if later:
                                later.pop()()
                    later.append(partial(finish, *pair, c, o + m, par, q, ht))
                    i += 1
                later.pop()()
                hl_ = [H[:, o + k, :] for k in range(n)], [H[:, o + 8 + k, :] for k in range(n)]
                if q == 2:
                    tables()
                    st["sqfree"] = [ufree[0], ufree[1]]
                for m in range(8):
                    b, ps, tok = unit(f"dn{n}_{l}", *hl_, ht)
                    if q == 0:
                        yt[m] = act(Y[:, m, :], ps, ACT.Copy, tok)
                    else:
                        yt[m] = tt(Y[:, m, :], Y[:, m, :], ps, ALU.add, tok, yt[m])
                    bfree[b] = yt[m]
                    if q == 2:
                        stat(Y[:, m, :], m, yt[m], False)
                hfree[q] = tok
            return yt

        def hybrid(xt):
            first_units("hyb", 2, *XHL, xt)
            sl = lambda i: AR[:, i, :]
            QKV = [sl(i) for i in range(12)]
            Z = [sl(12 + i) for i in range(4)]
            QA = [sl(16 + i) for i in range(4)]
            KA, VA = sl(20), sl(21)
            GR = sl(22)
            BR = sl(23)
            c0 = lambda name, lo=0, hi=128: c_of(Yf, at0, name, lo, hi)
            for e in ("act", "dve", "pe", "pool"):
                hold(e, t_cst, t_vec, e1, e2, tcb)
            b, ps, tok = unit("hyb", *XHL, xt)
            tb = act(BR[0:4, :], ps[0:4, :], ACT.Sigmoid, tok)
            r = [sl(24 + i)[32:36, :] for i in range(5)]
            ta = act(r[0], ps[32:36, :], ACT.Identity, tok, bias=vec("dtb", 0, 1, 32, 36))
            bfree[b] = [ta, tb]

            def decay_rows():
                tables()
                ea = act(COL[32:36, 200:201], vec("alog", 0, 1, 32, 36), ACT.Exp)
                sp = None
                for sp in softplus_steps(r[0], r[0], r[1:5], ta):
                    yield
                g = ts(r[0], r[0], COL[32:36, 200:201], ALU.mult, sp, ea, s2=-1.0, op1=ALU.mult)
                yield
                for c in range(4):
                    gs = slice(128 * c, 128 * c + 128)
                    scan(GR[32:36, gs], ones[32:36, :], r[0][:, gs], g)
                    yield

            rows = decay_rows()
            qkvt = []
            for i in range(12):
                b, ps, tok = unit("hyb", *XHL, xt)
                w = lambda j, i=i: vec("hcw", 4 * i + j)
                a = conv_psum(QKV[i], ps, w, 4, 0.0, tok)
                bfree[b] = a
                qkvt.append(a)
                if i < 3:
                    qkvt[i] = act(QKV[i], QKV[i], ACT.Silu, a)
                else:
                    run(rows, 2)
            run(rows)
            for i in range(3, 12):
                qkvt[i] = act(QKV[i], QKV[i], ACT.Silu, qkvt[i])
            tables()
            for e in ("pe", "dve", "pool", "act"):
                hold(e, t_c0)
            free, nrm = {}, {}

            def norm_square(i):
                nrm[i] = act(TM[:, 2 + i % 2, :], QKV[i], ACT.Square, qkvt[i], free.get(("s", i % 2)))

            def norm_rest(i):
                sq, rs = TM[:, 2 + i % 2, :], TM[:, 4 + i % 2, :]
                b = next_bank()
                t = mm(PS[b][:, :], ones, sq, True, True, nrm[i], bfree.get(b), inc=True)
                free[("s", i % 2)] = t
                rr = rstd_of(rs, PS[b][:, :], 1.0, EPS6, t, free.get(("r", i % 2)))
                bfree[b] = rr
                if i < 4:
                    qkvt[i] = stt(QKV[i], QKV[i], 128 ** -0.5, rs, ALU.mult, ALU.mult, rr, qkvt[i])
                else:
                    qkvt[i] = tt(QKV[i], QKV[i], rs, ALU.mult, rr, qkvt[i])
                free[("r", i % 2)] = qkvt[i]

            def norms(i):
                for m in (2 * i - 2, 2 * i - 1):
                    if 0 <= m < 8:
                        norm_rest(m)
                for m in (2 * i, 2 * i + 1):
                    if m < 8:
                        norm_square(m)

            zt = []
            for i in range(4):
                b, ps, tok = unit("hyb", *XHL, xt)
                zt.append(act(Z[i], ps, ACT.Copy, tok))
                bfree[b] = zt[-1]
                norms(i)
            rt = []
            for i in range(5):
                b, ps, tok = unit("hyb", *XHL, xt)
                rt.append(rope(QA[i] if i < 4 else KA, ps, tok, cst["rot1"], c0("cos"), c0("sin"),
                               TM[:, 6 + i % 2, :], rt[i - 2] if i > 1 else None, b, 0.125 if i < 4 else 1.0))
                if i == 0:
                    norms(4)
            for i in range(4):
                zt[i] = act(Z[i], Z[i], ACT.Silu, zt[i])
            bs, tok = unit_tok("hyb", 1, xt, False)
            bfree[bs[0]] = act(VA, PS[bs[0]][:, :], ACT.Copy, tok)
            tables()
            p.fence()
            slide = c0("cos").bitcast(B16)[:, 0:256]
            mb = act(slide, c0("slide"), ACT.Copy)
            gcol = COL[:, 32:48].rearrange("p (c h) -> p c h", c=4)
            bcol = COL[:, 48:64].rearrange("p (c h) -> p c h", c=4)
            bg = COL[:, 64:80].rearrange("p (c h) -> p c h", c=4)
            for c in range(4):
                gs = slice(128 * c, 128 * c + 128)
                mm(PS[0][:, 4 * c:4 * c + 4], GR[32:36, gs], ident[32:36, 32:36], True, True)
                t = mm(PS[1][:, 4 * c:4 * c + 4], BR[0:4, gs], ident[0:4, 0:4], True, True, inc=True)
            a = copy(COL[:, 32:48], PS[0][:, 0:16], t)
            b = copy(COL[:, 48:64], PS[1][:, 0:16], t)
            e = act(COL[:, 64:80], COL[:, 32:48], ACT.Exp, a)
            tcol = tt(COL[:, 64:80], COL[:, 64:80], COL[:, 48:64], ALU.mult, e, b)
            for e in ("pe", "act", "dve", "pool"):
                hold(e, tcol, mb)
            jobs = []
            otok = [None] * 8

            def out_of(j):
                def then(t):
                    otok[j] = split(XH[:, j, :], XL[:, j, :], PS[7][:, :], t)
                    for job in jobs:
                        if job["j"] == j + 1:
                            job["outfree"] = otok[j]
                return then

            for j in range(4):
                for hp in range(2):
                    h = 4 * hp + j
                    lo = 64 * hp
                    for n in range(4):
                        k0 = max(n - 1, 0)
                        nk = 128 * (n + 1 - k0)
                        jobs.append(dict(
                            q=QA[j][lo:lo + 64, 128 * n:128 * n + 128], k=KA[lo:lo + 64, 128 * k0:128 * n + 128],
                            nk=nk, v=[VA[:, 128 * c + lo:128 * c + lo + 64] for c in range(k0, n + 1)],
                            out=PS[7][lo:lo + 64, 128 * n:128 * n + 128], sink=vec("sink", h),
                            mask=slide[:, 256 - nk:256], j=j))
                jobs[-1]["then"] = out_of(j)
            spare = [sl(24 + i) for i in range(8)] + [TM[:, 5, :], TM[:, 6, :], TM[:, 7, :], Y[:, 7, :]]
            CH = [slice(128 * c, 128 * c + 128) for c in range(4)]

            def by4(t):
                return t.rearrange("p (c i) -> p c i", c=4)

            def each(m):
                return m[:, None, :].broadcast_to([128, 4, 128])

            def along(v, h):
                return v[:, :, h:h + 1].broadcast_to([128, 4, 128])

            def four(out, a, b, *after):
                for gs in CH:
                    t = mm(out[:, gs], a[:, gs], b[:, gs], True, True, *after, inc=gs is CH[3])
                return t

            def turn(out, a, *after):
                for gs in CH:
                    t = tr(out[:, gs], a[:, gs], ident, *after, inc=gs is CH[3])
                return t

            def delta(h):
                P = PS[h][:, :]
                Q, K, V = QKV[h], QKV[4 + h], QKV[8 + h]
                a_, c_ = XF[:, 4 + h, :], XF[:, 12 + h, :]
                d_, e_, f_ = spare[3 * h:3 * h + 3]
                gl = COL[:, 80 + 4 * h:84 + 4 * h]
                kt = COL[:, 100 + 4 * h:104 + 4 * h]
                t = mm(P, c0("sel", 32, 36)[:, 128 * h:128 * h + 128], GR[32:36, :], True, True, inc=True)
                g = tt(kt, P[:, 127:T:128], gcol[:, :, h], ALU.subtract, t)
                d = tt(by4(d_), by4(P), along(gcol, h), ALU.subtract, t)
                dm = ts(d_, d_, 0.0, ALU.min, d)
                eg = act(c_, P, ACT.Exp, d)
                g2 = act(gl, P[:, 127:T:128], ACT.Exp, d)
                g1 = act(kt, kt, ACT.Exp, g)
                dc = act(d_, d_, ACT.Exp, dm)
                yield
                t = mm(P, c0("sel", 0, 4)[:, 128 * h:128 * h + 128], BR[0:4, :], True, True, eg, g2, inc=True)
                kb = tt(a_, K, P, ALU.mult, t)
                m1 = tt(by4(d_), by4(d_), each(c0("mi")), ALU.mult, dc, e="pool")
                m2 = tt(by4(e_), by4(d_), each(c0("ms")), ALU.mult, m1, e="pool")
                yield
                t = four(P, K, Q, kb)
                qk = tt(d_, P, d_, ALU.mult, t, m1, m2)
                qg = tt(Q, Q, c_, ALU.mult, eg, t, e="pool")
                yield
                t = four(P, K, a_, qk)
                at = tt(c_, P, e_, ALU.mult, t, m2, qg)
                yield
                t = turn(P, K, at)
                kc = act(K, P, ACT.Copy, t)
                mo = tt(by4(e_), by4(c_), each(c0("lv")[:, 0:128]), ALU.mult, at, e="pool")
                yield
                t = turn(P, V, kc)
                vb = tt(by4(V), by4(P), along(bcol, h), ALU.mult, t)
                TT = tt(by4(f_), each(ident), by4(e_), ALU.subtract, mo)
                yield
                t = turn(P, f_, TT, vb)
                Tt = act(e_, P, ACT.Copy, t, TT)
                yield
                for lv in range(1, 7):
                    t = four(P, c_, e_, Tt, TT)
                    y = tt(by4(a_), by4(P), each(c0("lv")[:, 128 * lv:128 * lv + 128]), ALU.mult, t)
                    yield
                    if lv < 6:
                        t = four(P, f_, a_, y)
                        Tt = tt(e_, e_, P, ALU.subtract, t, Tt)
                        yield
                    t = four(P, a_, f_, y, Tt)
                    TT = tt(f_, f_, P, ALU.subtract, t, TT)
                    if lv < 6:
                        yield
                ka = tt(by4(a_), by4(K), along(bg, h), ALU.mult, t, kc, e="pool")
                kl = tt(by4(e_), by4(K), kt[:, :, None].broadcast_to([128, 4, 128]), ALU.mult, t, kc, g1, e="pool")
                yield
                t = four(P, a_, f_, ka, TT)
                nw = ts(c_, P, -1.0, ALU.mult, t)
                yield
                St, o = None, nw
                for c, gs in enumerate(CH):
                    so, sn = a_[:, 128 * (c % 2):128 * (c % 2) + 128], a_[:, 128 * ((c + 1) % 2):128 * ((c + 1) % 2) + 128]
                    vn = a_[:, 256 + 128 * (c % 2):384 + 128 * (c % 2)]
                    t = mm(P[:, 0:128], f_[:, gs], V[:, gs], True, c == 0, nw, o, vb, inc=c == 0)
                    if c:
                        t = mm(P[:, 0:128], c_[:, gs], so, False, True, St, inc=True)
                    v = copy(vn, P[:, 0:128], t)
                    yield
                    if c:
                        mm(P[:, 256:384], so, Q[:, gs], True, False, v)
                    t = mm(P[:, 256:384], vn, d_[:, gs], c == 0, True, v, qk, qg, inc=c == 3)
                    if c < 3:
                        t = mm(P[:, 128:256], e_[:, gs], vn, True, True, kl, inc=True)
                        if c == 0:
                            St = copy(sn, P[:, 128:256], t)
                        else:
                            St = stt(sn, so, gl[:, c:c + 1], P[:, 128:256], ALU.mult, ALU.add, t, St, g2)
                    o = copy(Q[:, gs], P[:, 256:384], t)
                    yield
                a = act(a_, Q, ACT.Square, o)
                yield
                t = mm(P, ones, a_, True, True, a, inc=True)
                r = rstd_of(c_, P, 1.0 / 128, EPS6, t)
                yield
                y = stt(e_, Q, vec("hnw"), c_, ALU.mult, ALU.mult, r)
                y = tt(e_, e_, Z[h], ALU.mult, y, e="pool")
                otok[4 + h] = split(XH[:, 4 + h, :], XL[:, 4 + h, :], e_, y)

            att = attention(jobs, (4, 5), (6,))
            heads = [delta(h) for h in range(4)]
            rounds, ahead = 0, None
            over = set()
            while len(over) < 5:
                for g in heads[0:2] + ([att] if rounds % 2 else []) + heads[2:4] + [att]:
                    if g not in over and next(g, "end") == "end":
                        over.add(g)
                rounds += 1
                if att in over:
                    if ahead is None:
                        for b in (4, 5, 6):
                            bfree[b] = p.now("act", "dve")
                        ahead = side_by_side("hwo", 3, *XHL, otok, (4, 5, 6))
                        left = 12
                    if left and rounds >= 30:
                        run(ahead, 2)
                        left -= 2
            run(ahead, left)
            p.fence(engines=("act", "dve", "pool"))
            bfree.clear()
            for b in range(4):
                bfree[b] = p.now("pe", "act", "dve")
            return otok, ahead

        def recurrent(xt):
            sl = lambda i: AR[:, i, :]
            XR, A_ = [sl(i) for i in range(8)], [sl(8 + i) for i in range(8)]
            B_, GA = [Y[:, i, :] for i in range(8)], [sl(16 + i) for i in range(8)]
            nl = COL[:, 0:8]
            a = ts(COL[:, 8:16], vec("lam", 0, 8), -1.0, ALU.mult)
            a = run(softplus_steps(nl, COL[:, 8:16], [COL[:, 16 + 8 * i:24 + 8 * i] for i in range(4)], a))
            nlt = ts(nl, nl, -8.0, ALU.mult, a)
            p8 = COL[:, 48:56]
            nlt = ts(p8, nl, -1.0, ALU.mult, nlt)
            xrt, xs = [], []
            first_units("rin", 3, *XHL, xt)
            for m in range(8):
                b, ps, tok = unit("rin", *XHL, xt)
                w = lambda j, m=m: vec("rcw", 4 * m + j)
                if m:
                    xs.append(split(H[:, 15 + m, :], H[:, 23 + m, :], XR[m - 1], xrt[m - 1]))
                xrt.append(conv_psum(XR[m], ps, w, 4, vec("rcb", m), tok))
                bfree[b] = xrt[-1]
            xs.append(split(H[:, 23, :], H[:, 31, :], XR[7], xrt[7]))
            rt, it = {}, {}
            last = None
            for half in range(2):
                for which in range(2):
                    u = next_unit("rwg")
                    s = u % NW
                    for mo in range(4):
                        m = 4 * half + mo
                        b = next_bank()
                        for k in range(2):
                            kk = 2 * (m // 2) + k
                            c = 128 * (2 * mo + k)
                            wh, wl = WH[:, s, c:c + 128], WL[:, s, c:c + 128]
                            mm(PS[b][:, :], wh, H[:, 16 + kk, :], k == 0, False, wtok[u], bfree.get(b), xs[kk])
                            mm(PS[b][:, :], wh, H[:, 24 + kk, :], False, False)
                            last = mm(PS[b][:, :], wl, H[:, 16 + kk, :], False, k == 1, inc=k == 1)
                        dst = (A_ if which == 0 else B_)[m]
                        t = act(dst, PS[b][:, :], ACT.Sigmoid, last, bias=vec("rba" if which == 0 else "rbx", m))
                        bfree[b] = t
                        if which == 0:
                            rt[m] = t
                        else:
                            it[m] = tt(XR[m], XR[m], dst, ALU.mult, t, xs[m], e="pool")
                    wfree[s] = last
            gat, ht, at, bt = {}, {}, {}, {}

            def gate(m):
                b, ps, tok = unit("rin", *XHL, xt)
                gat[m] = act(GA[m], ps, ACT.Copy, tok, last)
                bfree[b] = gat[m]

            def decay(m):
                t = act(B_[m], A_[m], ACT.Tanh, nlt, it[m], rt[m], scale=p8[:, m:m + 1])
                at[m] = act(A_[m], A_[m], ACT.Exp, t, nlt, scale=nl[:, m:m + 1])
                q = TM[:, 2 + m % 2, :]
                c = tt(q, A_[m], A_[m], ALU.mult, at[m], bt.get(m - 2))
                bt[m] = stt(B_[m], q, 1.0, B_[m], ALU.add, ALU.mult, c, t)

            def root(m):
                a = act(B_[m], B_[m], ACT.Sqrt, bt[m])
                a = tt(B_[m], B_[m], XR[m], ALU.mult, a, it[m], e="pool")
                ht[m] = scan(XR[m], A_[m], B_[m], a, at[m])

            for m in range(4):
                gate(m)
                decay(2 * m)
                decay(2 * m + 1)
            y = {}

            def gated(m):
                ga = act(GA[m], GA[m], ACT.Gelu_apprx_tanh, gat[m])
                y[m] = tt(XR[m], XR[m], GA[m], ALU.mult, ga, ht[m], e="pool" if m < 6 else "dve")

            for m in range(4, 8):
                gate(m)
                if m < 6:
                    for n in range(4 * m - 16, 4 * m - 12):
                        root(n)
                if m == 6:
                    for n in range(6):
                        gated(n)
            pe = p.now("pe")
            busy(10)
            otok = [None] * 8
            for i in range(9):
                if i < 8:
                    otok[i] = [act(XH[:, i, :], XR[i], ACT.Copy, y[i], pe)]
                m = i - 1
                if 0 <= m < 8:
                    otok[m].append(tt(XL[:, m, :], XR[m], f32(XH[:, m, :]), ALU.subtract, otok[m][0], y[m], pe))
                if i == 3:
                    gated(6)
                    gated(7)
            return otok

        at2, n2 = places(C2)

        def dilated(xt):
            sl = lambda i: AR[:, i, :]
            QA, KA = [sl(i) for i in range(6)], [sl(6 + i) for i in range(6)]
            VA = [sl(12 + i) for i in range(6)]
            c2 = lambda name, lo=0, hi=128: c_of(ARf[:, 18 * T:], at2, name, lo, hi)
            j = p.now("pe", "act", "dve", "pool")
            t_c2 = p.dma("pool", ARf[:, 18 * T:18 * T + n2], D["c2"], j)
            hold("act", j)
            hold("dve", j)
            rt = []
            first_units("qkv", 3, *XHL, xt)
            hold("dve", t_c2)
            hold("pool", t_c2)
            for i in range(12):
                if i == 3:
                    for v in range(0, 6, 2):
                        v_pair(VA[v:v + 2], "qkv", xt, v >= 2)
                b, ps, tok = unit("qkv", *XHL, xt)
                rt.append(rope(QA[i] if i < 6 else KA[i - 6], ps, tok, cst["rot2"], c2("cos"), c2("sin"),
                               TM[:, 6 + i % 2, :], rt[i - 2] if i > 1 else None, b, 0.125 if i < 6 else 1.0))
            p.fence()
            band, diag = c2("cos").bitcast(B16)[:, 0:256], c2("cos").bitcast(B16)[:, 256:384]
            hold("pe", act(band, c2("dil1"), ACT.Copy), act(diag, c2("dil3"), ACT.Copy))
            LC = COL[:, 32:80]
            MC = COL[:, 80:128]
            jobs = []
            OB = [sl(25 + i) for i in range(6)]
            ot = [None] * 6

            def out_of(jb):
                def then(t):
                    ot[jb] = act(OB[jb], PS[jb % 2][:, :], ACT.Copy, t)
                    for job in jobs:
                        if job["jb"] == jb + 2:
                            job["outfree"] = ot[jb]
                return then

            for jb in range(6):
                g = jb // 2
                for hp in range(2):
                    h = 2 * jb + hp
                    lo = 64 * hp
                    for n in range(4):
                        if g == 0:
                            k0 = max(n - 1, 0)
                            q = QA[jb][lo:lo + 64, 128 * n:128 * n + 128]
                            k = KA[jb][lo:lo + 64, 128 * k0:128 * n + 128]
                            nk = 128 * (n + 1 - k0)
                            v = [VA[jb][:, 128 * c + lo:128 * c + lo + 64] for c in range(k0, n + 1)]
                            mask = band[:, 256 - nk:256]
                            out = PS[jb % 2][lo:lo + 64, 128 * n:128 * n + 128]
                        else:
                            q = QA[jb][lo:lo + 64, n:T:4]
                            k = KA[jb][lo:lo + 64, n:T:4]
                            nk = 128
                            v = [VA[jb][:, 128 * n + lo:128 * n + lo + 64]]
                            mask = causal if g == 1 else diag
                            out = PS[jb % 2][lo:lo + 64, n:T:4]
                        ci = 16 * g + 4 * n + h % 4
                        jobs.append(dict(q=q, k=k, nk=nk, v=v, mask=mask, out=out, jb=jb,
                                         lout=LC[:, ci:ci + 1], mout=MC[:, ci:ci + 1]))
                jobs[-1]["then"] = out_of(jb)
            run(attention(jobs, (3, 4, 5), (6, 7), lse=True))
            p.fence()
            a = act(LC, LC, ACT.Ln)
            a = tt(LC, LC, MC, ALU.add, a)
            Lg = [TM[0:4, i, :] for i in range(3)]
            toks = []
            for g in range(3):
                for n in range(4):
                    ci = 16 * g + 4 * n
                    t = tr(PS[2 + g][0:4, 128 * n:128 * n + 128], LC[:, ci:ci + 4], ident, a, inc=n == 3)
                if g == 0:
                    toks.append(copy(Lg[0], PS[2][0:4, :], t))
                else:
                    toks.append(copy(Lg[g].rearrange("p (i r) -> p r i", r=4),
                                     PS[2 + g][0:4, :].rearrange("p (r i) -> p r i", r=4), t))
            mx, sm = TM[0:4, 3, :], TM[0:4, 4, :]
            a = tt(mx, Lg[0], Lg[1], ALU.max, toks)
            a = tt(mx, mx, Lg[2], ALU.max, a)
            et = []
            for g in range(3):
                b = tt(Lg[g], Lg[g], mx, ALU.subtract, a)
                et.append(act(Lg[g], Lg[g], ACT.Exp, b))
            a = tt(sm, Lg[0], Lg[1], ALU.add, et)
            a = tt(sm, sm, Lg[2], ALU.add, a)
            a = recip(sm, sm, a)
            et = [tt(Lg[g], Lg[g], sm, ALU.mult, a) for g in range(3)]
            otok = [None] * 6
            busy(24)
            bfree.clear()
            ahead = side_by_side("woa", 3, XHL[0][:6], XHL[1][:6], otok, (4, 5, 6))
            for jb in range(6):
                g = jb // 2
                s = c2("sel2", 0, 4)[:, 128 * (jb % 2):128 * (jb % 2) + 128]
                b = PS[jb % 4]
                t = mm(b[:, :], s, Lg[g], True, True, et, otok[jb - 4] if jb > 3 else None, inc=True)
                a = tt(OB[jb], OB[jb], b[:, :], ALU.mult, t)
                otok[jb] = split(XH[:, jb, :], XL[:, jb, :], OB[jb], a)
                bfree[jb % 4] = otok[jb]
                if jb > 1:
                    run(ahead, 3)
            return otok, ahead

        def fox(xt, r):
            sl = lambda i: AR[:, i, :]
            QZ, KC = [sl(i) for i in range(16)], [sl(16 + i) for i in range(16)]
            VA = [Y[:, i, :] for i in range(8)]
            j = p.now("pe", "act", "dve", "pool")
            zt = p.op("pool", lambda g: g.memset(AR[:, 0:16, :], 0.0), j)
            first_units("kvf", 3, *XHL, xt)
            b, ps, tok = unit("kvf", *XHL, xt)
            CR, ONE, NC = TM[0:16, 6, :], TM[0:16, 7, :], TM[0:16, 0, :]
            rr = [TM[0:16, 3, :], TM[0:16, 4, :], TM[0:16, 5, :], TM[0:16, 0, :], TM[0:16, 1, :]]
            a = act(rr[0], ps[0:16, :], ACT.Identity, tok, j, bias=vec("bf", 0, 1, 0, 16))
            bfree[b] = a
            a = ts(rr[0], rr[0], -1.0, ALU.mult, a)
            c_steps = softplus_steps(rr[0], rr[0], rr[1:5], a)
            kt = {}
            for i in range(8):
                if i == 2:
                    run(c_steps, 2)
                    for v in range(0, 8, 2):
                        v_pair(VA[v:v + 2], "kvf", xt, False)
                        if v < 4:
                            run(c_steps, 4)
                        if v == 4:
                            a = run(c_steps)
                            one = fill(ONE, 1.0, a)
                            ct = scan(CR, ONE, rr[0], a, one)
                            nt = ts(NC, CR, -1.0, ALU.mult, ct)
                b, ps, tok = unit("kvf", *XHL, xt)
                bfree[b] = act(KC[2 * i], ps, ACT.Copy, tok, j)
                kt[i] = copy(KC[2 * i + 1], KC[2 * i], bfree[b], e="pool")
            dmas = []
            for par, lo in ((0, 64), (1, 0)):
                hs = slice(par, 16, 2)
                dmas += [p.dma("pool", AR[lo:lo + 1, 16 + par:32:2, :], CR[hs, :], ct, kt.values()),
                         p.dma("pool", AR[lo + 1:lo + 2, 16 + par:32:2, :], ONE[hs, :], one, kt.values()),
                         p.dma("pool", AR[lo:lo + 1, par:16:2, :], ONE[hs, :], one, zt),
                         p.dma("pool", AR[lo + 1:lo + 2, par:16:2, :], NC[hs, :], nt, zt)]
            xq = rms_apply(X, r, "ng", 32, xw)
            first_units("wqb", 3, *XHL, xq)
            for i in range(8):
                b, ps, tok = unit("wqb", *XHL, xq)
                bfree[b] = [act(QZ[2 * i][0:64, :], ps[0:64, :], ACT.Copy, tok, zt, scale=0.125),
                            ts(QZ[2 * i + 1][64:128, :], ps[64:128, :], 0.125, ALU.mult, tok, zt)]
            p.fence(dmas)
            jobs = []
            otok = [None] * 8

            def out_of(jb):
                def then(t):
                    otok[jb] = split(XH[:, jb, :], XL[:, jb, :], PS[jb % 3][:, :], t)
                    for job in jobs:
                        if job["jb"] == jb + 3:
                            job["outfree"] = otok[jb]
                return then

            for jb in range(8):
                for hp in range(2):
                    h = 2 * jb + hp
                    lo = 64 * hp
                    for n in range(4):
                        nk = 128 * (n + 1)
                        jobs.append(dict(
                            q=QZ[h][:, 128 * n:128 * n + 128], k=KC[h][:, 0:nk], nk=nk,
                            mask=causal,
                            v=[VA[jb][:, 128 * c + lo:128 * c + lo + 64] for c in range(n + 1)],
                            out=PS[jb % 3][lo:lo + 64, 128 * n:128 * n + 128], jb=jb))
                jobs[-1]["then"] = out_of(jb)
            run(attention(jobs, (3, 4, 5), (6, 7)))
            bfree.clear()
            ahead = side_by_side("wob", 3, *XHL, otok, (3, 4, 5))
            run(ahead, 21)
            for b in range(4):
                bfree[b] = p.now("act", "dve")
            return otok, ahead

        def mix_y(name, nk, otok, ahead=None):
            yt = []
            run(ahead or side_by_side(name, 3, XHL[0][:nk], XHL[1][:nk], otok))
            hold("act", otok)
            tables()
            for m in range(8):
                b, ps, tok = unit(name, XHL[0][:nk], XHL[1][:nk], otok)
                yt.append(act(Y[:, m, :], ps, ACT.Copy, tok))
                bfree[b] = yt[-1]
                stat(Y[:, m, :], m, yt[m], False)
            return yt

        ot, ahead = hybrid(xtok)
        mix_out("hwo", 8, ot, ahead)
        xt = layer_norm("ln1g", "ln1b", 0)
        p.fence(engines=("act", "dve", "pool"))
        mlp(0, xt)
        xt = layer_norm("ln2g", "ln2b", 0)
        p.fence(engines=("act", "dve", "pool"))
        ot = recurrent(xt)
        mix_out("rwo", 8, ot)
        xt = layer_norm("ln1g", "ln1b", 1)
        p.fence(engines=("act", "dve", "pool"))
        mlp(1, xt)
        r = layer_norm("ln2g", "ln2b", 1, last=True)
        p.fence(engines=("act", "dve", "pool"))
        for l in range(2):
            if l == 0:
                xt = rms_apply(X, r, "ng", 0, xw)
                ot, ahead = dilated(xt)
                yt = mix_y("woa", 6, ot, ahead)
            else:
                xt = rms_apply(X, r, "kvn", 0, xw)
                ot, ahead = fox(xt, r)
                yt = mix_y("wob", 8, ot, ahead)
            _, _, r, _ = stats_end(False, EPS6)
            r, xt = rms_add_on(r, 32 * l + 8, yt, 32 * l + 16, f"up_{l}")
            yt = ffn(l, xt, r)
            _, _, r, _ = stats_end(False, EPS6)
            r = rms_add(r, 32 * l + 24, yt, l == 0)
            if l == 1:
                for m in range(8):
                    p.dma("sp", D["out"][128 * m:128 * m + 128, :], X[:, m, :], xw[m])
            p.fence(engines=("act", "dve", "pool"))
        p.fence()
        for s in p.dlast.values():
            w = p.waits("sp", s)
            p.q["sp"].append((w, None, None))

        block = ctx.enter_context(nc.Block())

        @block.sync
        def _(eng):
            p.play("sp", eng)

        @block.tensor
        def _(eng):
            p.play("pe", eng)

        @block.scalar
        def _(eng):
            p.play("act", eng)

        @block.vector
        def _(eng):
            p.play("dve", eng)

        @block.gpsimd
        def _(eng):
            p.play("pool", eng)


def shape_constants():
    f = np.float32
    idx = np.arange(128)
    small = np.zeros((6, 128, 128), f)
    small[0] = np.eye(128)
    small[1] = 1.0 / 1024
    small[2] = 1.0
    for i in range(128):
        j = i % 64
        if j < 32:
            small[3, i + 32, i] = -1
        else:
            small[3, i - 32, i] = 1
        if j < 8:
            small[4, i + 8, i] = -1
        elif j < 16:
            small[4, i - 8, i] = 1
    NEG = -1e30
    small[5] = np.where(idx[None, :] <= idx[:, None], 0, NEG)
    small = small.transpose(1, 0, 2).reshape(128, -1)

    def tables(half, theta):
        inv = (f(theta) ** (-np.arange(half, dtype=f) / f(half))).astype(f)
        ang = (np.arange(T, dtype=f)[:, None] * inv[None, :]).astype(f)
        cos, sin = np.ones((64, T), f), np.zeros((64, T), f)
        for k in range(2 * half):
            cos[k] = np.cos(ang[:, k % half])
            sin[k] = np.sin(ang[:, k % half])
        return np.tile(cos, (2, 1)), np.tile(sin, (2, 1))

    q, k = idx[:, None], idx[None, :]
    k2 = np.arange(256)[None, :]
    dist = q + 128 - k2
    slide = np.where((dist >= 0) & (dist < 128), 0, NEG).astype(f)
    dil1 = np.where((dist >= 0) & (dist <= 128), 0, NEG).astype(f)
    dil3 = np.where((k <= q) & ((q - k) % 4 == 0), 0, NEG).astype(f)
    j, i = q, k
    mi = (i >= j).astype(f)
    ms = (i > j).astype(f)
    lv = []
    for l in range(7):
        b = 1 << l
        lv.append(((i // (2 * b) == j // (2 * b)) & (i // b % 2 == 1) & (j // b % 2 == 0)).astype(f))
    lv = np.concatenate([lv[0]] + [m.T for m in lv[1:]], 1)
    sel = np.zeros((128, 4, 128), f)
    sel2 = np.zeros((128, 2, 128), f)
    for h in range(4):
        sel[h, h, :] = 1
        sel[32 + h, h, :] = 1
        sel2[h, h // 2, 64 * (h % 2):64 * (h % 2) + 64] = 1
    cos, sin = tables(32, 10000.0)
    c0 = dict(cos=cos, sin=sin, mi=mi, ms=ms, lv=lv, sel=sel.reshape(128, -1), slide=slide)
    cos, sin = tables(8, 500000.0)
    c2 = dict(cos=cos, sin=sin, dil1=dil1, dil3=dil3, sel2=sel2.reshape(128, -1))
    return small, *(np.ascontiguousarray(np.concatenate([c[n] for n, _ in parts], 1), dtype=f)
                    for c, parts in ((c0, C0), (c2, C2)))


def kernel(**inputs):
    import numpy as _np
    import concourse.bacc as _bacc
    from concourse import mybir as _mybir
    from concourse.bass_utils import run_bass_kernel_spmd as _run

    I = {k: _np.asarray(v) for k, v in inputs.items()}
    f = _np.float32

    def units(w, kb=8):
        K, N = w.shape
        a = w.reshape(K // (128 * kb), kb, 128, N // 128, 128).transpose(0, 3, 2, 1, 4)
        return _np.ascontiguousarray(a).reshape(-1, 128, kb * 128)

    def pad(w, n):
        out = _np.zeros((w.shape[0], n), w.dtype)
        out[:, :w.shape[1]] = w
        return out

    A = {}
    A["x"] = _np.ascontiguousarray(I["x"][0].T)
    w = I["hyb_w_in"][0]
    qa, ka, va, qkv, z, be, al = _np.split(w, [512, 640, 768, 2304, 2816, 2820], axis=1)
    small = _np.zeros((1024, 128), w.dtype)
    small[:, 0:4] = be
    small[:, 32:36] = al
    order = [h for j in range(4) for h in (j, 4 + j)]
    qa = qa.reshape(1024, 8, 64)[:, order].reshape(1024, 512)
    A["hyb"] = units(_np.concatenate([small, qkv, z, qa, ka, va], axis=1))
    w = I["hyb_w_out"][0]
    wa = w[:512].reshape(8, 64, 1024)[order].reshape(512, 1024)
    A["hwo"] = units(_np.concatenate([wa, w[512:]], axis=0))
    for l in range(2):
        A[f"w1_{l}"] = units(I["mlp_w1"][l])
        A[f"w2_{l}"] = units(I["mlp_w2"][l])
        up = I["w_up_2"][l].reshape(1024, 2, 22, 128).transpose(0, 2, 1, 3).reshape(1024, 5632)
        A[f"up_{l}"] = units(up)
        A[f"dn8_{l}"] = units(I["w_down_2"][l][:2048])
        A[f"dn6_{l}"] = units(I["w_down_2"][l][2048:], 6)
    A["rin"] = units(I["rec_w_in"][0])
    g = []
    for w in (I["rec_w_a"][0], I["rec_w_x"][0]):
        a = w.reshape(4, 2, 128, 2, 128).transpose(0, 3, 2, 1, 4).reshape(2, 4, 128, 256)
        g.append(a.transpose(0, 2, 1, 3).reshape(2, 128, 1024))
    A["rwg"] = _np.ascontiguousarray(_np.stack(g, 1).reshape(4, 128, 1024))
    A["rwo"] = units(I["rec_w_out"][0])
    w = I["w_qkv_a_2"][0]
    A["qkv"] = units(_np.concatenate([w[:, :384], w[:, 1536:], w[:, 384:1536]], axis=1))
    A["woa"] = units(I["w_o_a_2"][0], 6)
    w = I["w_kvf_2"]
    A["kvf"] = units(_np.concatenate([pad(w[:, 2048:], 128), w[:, :256], w[:, 1024:2048], w[:, 256:1024]], axis=1))
    A["wqb"] = units(I["w_q_b_2"][0])
    A["wob"] = units(I["w_o_b_2"][0])

    def cols(v):
        return _np.ascontiguousarray(v.reshape(-1, 128).T)

    def taps(v):
        return v.reshape(v.shape[0], -1, 128).transpose(2, 1, 0).reshape(128, -1)

    def at(v, lo):
        out = _np.zeros((128, 1), f)
        out[lo:lo + v.shape[0], 0] = v
        return out

    V = dict(
        ln1g=cols(I["ln1_g"]), ln1b=cols(I["ln1_b"]), ln2g=cols(I["ln2_g"]), ln2b=cols(I["ln2_b"]),
        ng=cols(I["norm_gains_2"]), kvn=cols(I["kv_norm_2"]), hcw=taps(I["hyb_conv_w"][0]),
        hnw=cols(I["hyb_norm_w"]), sink=_np.repeat(I["hyb_sinks"][0][None], 128, 0),
        alog=at(I["hyb_a_log"][0], 32), dtb=at(I["hyb_dt_bias"][0], 32),
        rcw=taps(I["rec_conv_w"][0]), rcb=cols(I["rec_conv_b"]), rba=cols(I["rec_b_a"]),
        rbx=cols(I["rec_b_x"]), lam=cols(I["rec_lambda"]), bf=at(I["b_f_2"], 0),
        fcw=_np.concatenate([taps(I["conv_w_2"][l]) for l in range(2)], 1), fcb=cols(I["conv_b_2"]),
    )
    A["vec"] = _np.ascontiguousarray(_np.concatenate([V[n] for n, _ in VEC_SIZES], 1))
    A["small"], A["c0"], A["c2"] = shape_constants()

    nc = _bacc.Bacc("TRN2", target_bir_lowering=False, num_devices=1)
    D, arrays = {}, {}
    for name, a in A.items():
        arrays[f"in_{name}"] = a
        D[name] = nc.dram_tensor(f"in_{name}", a.shape, _mybir.dt.from_np(a.dtype), kind="ExternalInput").ap()
    D["out"] = nc.dram_tensor("out_x", (1024, T), F, kind="ExternalOutput").ap()
    build_program(nc, D)
    r = _run(nc, [arrays], core_ids=[0])
    return _np.ascontiguousarray(r.results[0]["out_x"].T)[None]
```
